# Optimizing a Trainium2 kernel written in Bass

```python
import jax, jax.numpy as jnp
from jax import lax
import numpy as np

D_MODEL = 1024
BATCH = 1
SEQ = 1024
DEPTH = 1

GRID_W = 64
CTX_LEN = 256
HEAD_DIM = 64
N_Q_HEADS = 12
N_KV_HEADS = 4
Q_PER_KV = N_Q_HEADS // N_KV_HEADS
ATTN_WIDTH = N_Q_HEADS * HEAD_DIM
KV_WIDTH = N_KV_HEADS * HEAD_DIM
N_FOURIER_GROUPS = 4
FOURIER_GROUP_DIM = 64
FOURIER_WIDTH = N_FOURIER_GROUPS * FOURIER_GROUP_DIM
MIX_WIDTH = FOURIER_WIDTH + ATTN_WIDTH
IN_WIDTH = FOURIER_WIDTH + ATTN_WIDTH + 2 * KV_WIDTH
Q_BLOCK = 128
ROPE_BASE = 10000.0
N_EXPERTS = 16
EC_CAPACITY_FACTOR = 2
D_EXPERT = 2048
N_MOD = 6
NORM_EPS = 1e-6

kernel_name = "hymba_fnet_gqa_ec_moe_dit"

def rms_norm(x, g):
    xf = x.astype(jnp.float32)
    y = xf * lax.rsqrt(jnp.mean(xf * xf, axis=-1, keepdims=True) + NORM_EPS)
    return (y * g.astype(jnp.float32)).astype(x.dtype)

def modulate(x, g, shift, scale):
    return rms_norm(x, g) * (1 + scale) + shift

def split_projection(p):
    f = p[..., :FOURIER_WIDTH]
    q = p[..., FOURIER_WIDTH:FOURIER_WIDTH + ATTN_WIDTH]
    k = p[..., FOURIER_WIDTH + ATTN_WIDTH:FOURIER_WIDTH + ATTN_WIDTH + KV_WIDTH]
    v = p[..., FOURIER_WIDTH + ATTN_WIDTH + KV_WIDTH:]
    return f, q, k, v

def fourier_mix(f, w_four):
    B, N = f.shape[:2]
    fg = f.reshape(B, N, N_FOURIER_GROUPS, FOURIER_GROUP_DIM).astype(jnp.float32)
    y = jnp.fft.fftn(fg, axes=(1, 3), norm="ortho").real.astype(f.dtype)
    y = jnp.einsum('bngc,gcd->bngd', y, w_four)
    return y.reshape(B, N, FOURIER_WIDTH)

def rope_1d(x, pos):
    half = x.shape[-1] // 2
    freqs = ROPE_BASE ** (-jnp.arange(half, dtype=jnp.float32) / half)
    ang = pos.astype(jnp.float32)[:, None] * freqs[None, :]
    cos = jnp.cos(ang)[None, :, None, :]
    sin = jnp.sin(ang)[None, :, None, :]
    x1 = x[..., :half].astype(jnp.float32)
    x2 = x[..., half:].astype(jnp.float32)
    return jnp.concatenate([x1 * cos - x2 * sin, x1 * sin + x2 * cos], axis=-1).astype(x.dtype)

def axial_rope(x, row, col):
    h = HEAD_DIM // 2
    return jnp.concatenate([rope_1d(x[..., :h], row), rope_1d(x[..., h:], col)], axis=-1)

def heads(t, n_heads, g):
    B, N = t.shape[:2]
    return rms_norm(t.reshape(B, N, n_heads, HEAD_DIM), g)

def gqa_block(qi, k_all, v_all):
    s = jnp.einsum('bqkgd,bskd->bkgqs', qi, k_all).astype(jnp.float32) * (HEAD_DIM ** -0.5)
    p = jax.nn.softmax(s, axis=-1).astype(v_all.dtype)
    return jnp.einsum('bkgqs,bskd->bqkgd', p, v_all)

def latent_attention(q, k_lat, v_lat, k_ctx, v_ctx):
    B, N = q.shape[:2]
    k_all = jnp.concatenate([k_lat, k_ctx], axis=1)
    v_all = jnp.concatenate([v_lat, v_ctx], axis=1)
    nb = N // Q_BLOCK
    qb = q.reshape(B, nb, Q_BLOCK, N_KV_HEADS, Q_PER_KV, HEAD_DIM).swapaxes(0, 1)
    o = lax.map(lambda qi: gqa_block(qi, k_all, v_all), qb)
    return o.swapaxes(0, 1).reshape(B, N, ATTN_WIDTH)

def context_attention(q, k, v):
    B, L = q.shape[:2]
    qg = q.reshape(B, L, N_KV_HEADS, Q_PER_KV, HEAD_DIM)
    return gqa_block(qg, k, v).reshape(B, L, ATTN_WIDTH)

def expert_choice_ffn(h, w_router, w_gate, w_up, w_down):
    B, N, D = h.shape
    cap = EC_CAPACITY_FACTOR * N // N_EXPERTS
    aff = jax.nn.softmax(jnp.einsum('bnd,de->bne', h, w_router).astype(jnp.float32), axis=-1)
    gates, idx = lax.top_k(aff.swapaxes(1, 2), cap)
    bidx = jnp.arange(B)[:, None, None]
    xe = h[bidx, idx]
    hid = jax.nn.silu(jnp.einsum('becd,edf->becf', xe, w_gate)) * jnp.einsum('becd,edf->becf', xe, w_up)
    ye = jnp.einsum('becf,efd->becd', hid, w_down) * gates[..., None].astype(h.dtype)
    return jnp.zeros_like(h).at[bidx, idx].add(ye)

def setup_inputs(seed: int = 0) -> dict:
    key = jax.random.key(seed)
    ks = jax.random.split(key, 20)
    f32 = jnp.float32
    nrm = lambda k, shp, s: jax.random.normal(k, shp, f32) * s
    return {
        "x": nrm(ks[0], (BATCH, SEQ, D_MODEL), 1.0),
        "c": nrm(ks[1], (BATCH, D_MODEL), 1.0),
        "ctx": nrm(ks[2], (BATCH, CTX_LEN, D_MODEL), 1.0),
        "c_ctx": nrm(ks[3], (D_MODEL,), 1.0),
        "w_mod": nrm(ks[4], (DEPTH, D_MODEL, N_MOD * D_MODEL), 0.5 * D_MODEL ** -0.5),
        "b_mod": nrm(ks[5], (DEPTH, N_MOD * D_MODEL), 0.02),
        "norm_mix_g": 1.0 + nrm(ks[6], (DEPTH, D_MODEL), 0.1),
        "norm_ffn_g": 1.0 + nrm(ks[7], (DEPTH, D_MODEL), 0.1),
        "w_in": nrm(ks[8], (DEPTH, D_MODEL, IN_WIDTH), D_MODEL ** -0.5),
        "w_four": nrm(ks[9], (DEPTH, N_FOURIER_GROUPS, FOURIER_GROUP_DIM, FOURIER_GROUP_DIM), FOURIER_GROUP_DIM ** -0.5),
        "q_norm_g": 1.0 + nrm(ks[10], (DEPTH, HEAD_DIM), 0.1),
        "k_norm_g": 1.0 + nrm(ks[11], (DEPTH, HEAD_DIM), 0.1),
        "w_out": nrm(ks[12], (DEPTH, MIX_WIDTH, D_MODEL), MIX_WIDTH ** -0.5),
        "w_router": nrm(ks[13], (DEPTH, D_MODEL, N_EXPERTS), D_MODEL ** -0.5),
        "w_gate": nrm(ks[14], (DEPTH, N_EXPERTS, D_MODEL, D_EXPERT), D_MODEL ** -0.5),
        "w_up": nrm(ks[15], (DEPTH, N_EXPERTS, D_MODEL, D_EXPERT), D_MODEL ** -0.5),
        "w_down": nrm(ks[16], (DEPTH, N_EXPERTS, D_EXPERT, D_MODEL), D_EXPERT ** -0.5),
        "final_norm_g": 1.0 + nrm(ks[17], (D_MODEL,), 0.1),
    }

def reference(x, c, ctx, c_ctx, w_mod, b_mod, norm_mix_g, norm_ffn_g, w_in, w_four,
              q_norm_g, k_norm_g, w_out, w_router, w_gate, w_up, w_down, final_norm_g):
    B, N, _ = x.shape
    rows = N // GRID_W
    row = jnp.repeat(jnp.arange(rows, dtype=jnp.int32), GRID_W)
    col = jnp.tile(jnp.arange(GRID_W, dtype=jnp.int32), rows)

    for l in range(DEPTH):
        last = l == DEPTH - 1
        mod_x = (jax.nn.silu(c) @ w_mod[l] + b_mod[l])[:, None, :]
        mod_c = (jax.nn.silu(c_ctx) @ w_mod[l] + b_mod[l])[None, None, :]
        sh1, sc1, g1, sh2, sc2, g2 = jnp.split(mod_x, N_MOD, axis=-1)
        csh1, csc1, cg1, csh2, csc2, cg2 = jnp.split(mod_c, N_MOD, axis=-1)

        hx = modulate(x, norm_mix_g[l], sh1, sc1)
        hc = modulate(ctx, norm_mix_g[l], csh1, csc1)
        fx, qx, kx, vx = split_projection(hx @ w_in[l])
        fc, qc, kc, vc = split_projection(hc @ w_in[l])

        qx = axial_rope(heads(qx, N_Q_HEADS, q_norm_g[l]), row, col)
        kx = axial_rope(heads(kx, N_KV_HEADS, k_norm_g[l]), row, col)
        vx = vx.reshape(B, N, N_KV_HEADS, HEAD_DIM)
        kc = heads(kc, N_KV_HEADS, k_norm_g[l])
        vc = vc.reshape(B, ctx.shape[1], N_KV_HEADS, HEAD_DIM)

        attn_x = latent_attention(qx, kx, vx, kc, vc)
        four_x = fourier_mix(fx, w_four[l])
        x = x + g1 * (jnp.concatenate([four_x, attn_x], axis=-1) @ w_out[l])

        x = x + g2 * expert_choice_ffn(modulate(x, norm_ffn_g[l], sh2, sc2),
                                       w_router[l], w_gate[l], w_up[l], w_down[l])

        if not last:
            qc = heads(qc, N_Q_HEADS, q_norm_g[l])
            attn_c = context_attention(qc, kc, vc)
            four_c = fourier_mix(fc, w_four[l])
            ctx = ctx + cg1 * (jnp.concatenate([four_c, attn_c], axis=-1) @ w_out[l])
            ctx = ctx + cg2 * expert_choice_ffn(modulate(ctx, norm_ffn_g[l], csh2, csc2),
                                                w_router[l], w_gate[l], w_up[l], w_down[l])

    return rms_norm(x, final_norm_g)


_drawn_inputs = setup_inputs


def setup_inputs(seed=0):
    import zlib

    import numpy as np

    out = dict(_drawn_inputs(seed))
    spreads = {}
    factors = {'ctx': 8.0,
     'c_ctx': 3.504,
     'b_mod': 4.156,
     'norm_mix_g': 4.409,
     'norm_ffn_g': 3.05,
     'q_norm_g': 8.0,
     'k_norm_g': 8.0}
    for name, (base, spread) in spreads.items():
        noise = np.random.default_rng([zlib.crc32(name.encode()), seed]).standard_normal(out[name].shape)
        drawn = base * np.exp(spread * noise) if base else spread * noise
        out[name] = __import__('jax').numpy.asarray(drawn.astype(out[name].dtype))
    for name, factor in factors.items():
        out[name] = (out[name] * factor).astype(out[name].dtype)
    return out
```

```python
from contextlib import ExitStack

import numpy as np

import concourse.bass as bass
from concourse import mybir

P = 128
D = 1024
N = 1024
L = 256
HD = 64
NQ, NKV = 12, 4
REP = NQ // NKV
FG, FD = 4, 64
FW = FG * FD
QW, KW = NQ * HD, NKV * HD
IN = FW + QW + 2 * KW
QK = QW + KW
NH = NQ + NKV
E = 16
DE = 2048
CAP = 2 * N // E
GRID = 64
EPS = 1e-6
ROOT = float(D) ** 0.5
KD = D // P
TL, TC = N // P, L // P
TS = TL + TC
KEYS = N + L
HALF = N // 2 + 1
UC = 512
UM = 256
SCALE = HD ** -0.5 * HD

F32 = mybir.dt.float32
F32R = mybir.dt.float32r
U32 = mybir.dt.uint32
ALU = mybir.AluOpType
ACT = mybir.ActivationFunctionType
AX = mybir.AxisListType.X


INPUTS = ["x", "c", "ctx", "c_ctx", "w_mod", "b_mod", "norm_mix_g", "norm_ffn_g", "w_in", "w_four",
          "q_norm_g", "k_norm_g", "w_out", "w_router", "w_gate", "w_up", "w_down", "final_norm_g"]


def constants():
    n, m = np.arange(N)[:, None], np.arange(HALF)[None, :]
    turn = 2 * np.pi * ((n * m) % N) / N
    dft = np.stack([np.cos(turn), np.sin(turn)]).astype(np.float32)
    a = 2 * np.pi * np.outer(np.arange(FD), np.arange(FD)) / FD
    scale = 1 / np.sqrt(N * FD)
    two = np.eye(P // FD)
    chan = np.stack([np.kron(two, np.cos(a) * scale), np.kron(two, -np.sin(a) * scale),
                     np.kron(two, np.sin(a) * scale)]).astype(np.float32)
    half = HD // 4
    freqs = (10000.0 ** (-np.arange(half, dtype=np.float32) / np.float32(half))).astype(np.float32)
    pos = np.arange(N)
    ang = [np.float32(p)[:, None] * freqs[None] for p in (pos // GRID, pos % GRID)]
    cos = np.concatenate([f(x.astype(np.float32)) for x in ang for f in (np.cos, np.cos)], 1)
    sin = np.concatenate([s * np.sin(x.astype(np.float32)) for x in ang for s in (-1, 1)], 1)
    rope = np.stack([cos, sin]).astype(np.float32)
    return {"dft": dft, "chan": chan, "rope": rope}


def build(nc, a, out):
    ctx = ExitStack()

    def dram(name, shape, dt):
        return nc.dram_tensor(name, shape, dt, kind="Internal").ap()

    def sem(name):
        return ctx.enter_context(nc.semaphore(name))

    def sb(name, shape, dt=F32, where=ctx):
        return where.enter_context(nc.sbuf_tensor(name, shape, dt))

    x_d = a["x"].rearrange("b (t p) d -> (b t) p d", p=P)
    ctx_d = a["ctx"].rearrange("b (t p) d -> (b t) p d", p=P)
    out_d = out.rearrange("b (t p) d -> (b t) p d", p=P)
    w_mod = a["w_mod"][0].rearrange("(k p) n -> p k n", p=P)
    w_in = a["w_in"][0].rearrange("(k p) n -> p k n", p=P)
    w_gate = a["w_gate"][0].rearrange("e (k p) f -> e p k f", p=P)
    w_up = a["w_up"][0].rearrange("e (k p) f -> e p k f", p=P)
    w_down = a["w_down"][0].rearrange("e (k p) d -> e p k d", p=P)

    def row(v):
        return v.partition_broadcast(P)

    q_d = dram("q_scratch", [TL, P, NQ * 2 * P], F32)
    h2_d = dram("h2_scratch", [N, D], F32)
    acc_d = dram("acc_scratch", [N, D], F32)

    with ctx:
        psum = ctx.enter_context(nc.psum_tensor("banks", [P, 8, 512], F32))

        ident = sb("ident", [P, P])
        ones = sb("ones", [P, P])
        rows = sb("rows", [P, 4, D])
        G1, SH2, SC2, G2 = range(4)
        aff = sb("aff", [E, N])
        eps_c = sb("eps_c", [P, 2])
        K = ExitStack()
        ks = sb("ks", [P, NKV, KEYS], F32R, K)
        vs = sb("vs", [P, TS, NKV, 2, HD], F32R, K)
        f_tok = sb("f_tok", [P, TL, FW], F32, K)
        y_t = sb("y_t", [P, 2, N], F32, K)

        A = ExitStack()
        unit = [sb(f"unit{i}", [P, KD, UM], F32, A) for i in range(2)]
        win = sb("win", [P, KD, IN], F32, A)
        vec = sb("vec", [5 * KD, P], F32, A)
        c_sig = sb("c_sig", [P, KD, 2], F32, A)
        bg_col = sb("bg_col", [P, 3 * KD], F32, A)
        bm_col, g_col = bg_col[:, 0:2 * KD], bg_col[:, 2 * KD:3 * KD]
        mod_col = sb("mod_col", [P, 2, 2, KD], F32, A)
        xt = sb("xt", [P, D], F32, A)
        xn = sb("xn", [P, D], F32, A)
        junk = sb("junk", [P, D], mybir.dt.bfloat16, A)
        ht = [sb(f"ht{i}", [P, KD, P], F32, A) for i in range(2)]
        stat = sb("stat", [P, 4], F32, A)
        prj = sb("prj", [P, IN], F32, A)
        g_qk = sb("g_qk", [P, 2, HD], F32, A)
        rope = sb("rope", [P, 2, TL, HD], F32, A)
        sq = sb("sq", [P, QK], F32, A)
        ss = sb("ss", [P, 4, NH], F32, A)
        qkn = sb("qkn", [P, QK], F32, A)
        rot = sq
        c_wide = prj[:, 0:KD * P].rearrange("p (k n) -> p k n", n=P)
        hlq = sb("hlq", [P, NQ, 2, 2, HD], F32R, A)
        hlk = sb("hlk", [P, NKV, 2, HD], F32R, A)
        qst = sb("qst", [P, NQ, 2, P], F32, A)

        s = {n: sem(n) for n in (
            "ident_done", "f_done", "small_in", "tables_in", "vec_t", "silu_done", "wide_done", "cols_done",
            "win_in", "x_in", "ss_done", "rstd_done", "xn_done", "xT_done", "hTa", "hTb", "proj_done",
            "prj_done", "pool_qk", "ss16_done", "rstd16_done", "hl_done", "pool_v", "v_done", "qkt_done",
            "qkt_act", "qkt_dve", "q_out", "row_mm", "row_done", "unit_used", "norm_row_in",
            "mean_done", "dve_order", "pool_order", "eps_done")}
        unit_in = [sem(f"unit_in{i}") for i in range(2)]
        NC_UNITS, NR_UNITS = 2 * D // UM, 4 * D // UM

        def pipeline(eng, one, two, three, early=False):
            def step(s_, par, first, mid, last):
                if first:
                    one(s_ + 1, 1 - par, first)
                if last and early:
                    three(s_ - 1, 1 - par, last)
                if mid:
                    two(s_, par, mid)
                if last and not early:
                    three(s_ - 1, 1 - par, last)
            step(-1, 1, "ctx", None, None)
            step(0, 0, "ctx", "ctx", None)
            step(1, 1, "lat", "ctx", "ctx")
            step(2, 0, "lat", "lat", "ctx")
            step(3, 1, "lat", "lat", "lat")
            step(4, 0, "lat", "lat", "lat")
            with eng.Fori(0, (TS - 6) // 2) as pair:
                step(2 * pair + 5, 1, "lat", "lat", "lat")
                step(2 * pair + 6, 0, "lat", "lat", "lat")
            step(TS - 1, 1, None, "lat", "lat")
            step(TS, 0, None, None, "lat")

        def after(eng, sem_, v):
            if not (isinstance(v, int) and v <= 0):
                eng.wait_ge(sem_, v)

        XT, PJ, QT = 0, 2, 5
        QTG = 7

        with nc.Block() as block:

            @block.sync
            def _(sp):
                for r, v in ((0, a["c"].rearrange("b (k p) -> (b k) p", p=P)), (KD, a["c_ctx"].rearrange("(k p) -> k p", p=P)),
                             (2 * KD, a["b_mod"][0][0:2 * D].rearrange("(k p) -> k p", p=P)),
                             (4 * KD, a["norm_mix_g"][0].rearrange("(k p) -> k p", p=P))):
                    sp.dma_start(vec[r:r + v.shape[0], :], v).then_inc(s["small_in"], 16)
                for u in range(NC_UNITS):
                    if u >= 2:
                        sp.wait_ge(s["unit_used"], u - 1)
                    sp.dma_start(unit[u % 2][:, :, :], w_mod[:, :, u * UM:(u + 1) * UM]).then_inc(unit_in[u % 2], 16)
                    if u == 1:
                        sp.dma_start(g_qk[:, 0, :], row(a["q_norm_g"][0])).then_inc(s["tables_in"], 16)
                        sp.dma_start(g_qk[:, 1, :], row(a["k_norm_g"][0])).then_inc(s["tables_in"], 16)
                        sp.dma_start(rope[:, :, :, :], a["rope"].rearrange("a (t p) d -> p a t d", p=P)).then_inc(s["tables_in"], 16)

                def one(n, par, kind):
                    after(sp, s["xn_done"], n)
                    src = ctx_d[n] if kind == "ctx" else x_d[n - TC]
                    sp.dma_start(xt[:, :], src).then_inc(s["x_in"], 16)
                    if isinstance(n, int) and n == 0:
                        sp.dma_start(win[:, :, :], w_in).then_inc(s["win_in"], 16)

                def two(n, par, kind):
                    pass

                def three(n, par, kind):
                    if kind == "lat":
                        t = n - TC
                        sp.wait_ge(s["qkt_act"], (n + 1) * 4)
                        sp.wait_ge(s["qkt_dve"], t * 3 + 3)
                        sp.dma_start(q_d[t], qst[:, :, :, :].rearrange("p h a n -> p (h a n)")).then_inc(s["q_out"], 16)

                pipeline(sp, one, two, three)
                sp.dma_start(rows[:, :, :].rearrange("p a d -> p (a d)"), row(a["b_mod"][0][2 * D:6 * D])).then_inc(s["norm_row_in"], 16)
                sp.wait_ge(s["hl_done"], TS)
                sp.dma_start(sq[:, 0:D], row(a["norm_ffn_g"][0])).then_inc(s["norm_row_in"], 16)
                for u in range(NC_UNITS, NC_UNITS + NR_UNITS):
                    if u < NC_UNITS + 2:
                        sp.wait_ge(s["unit_used"], u - 1)
                    else:
                        sp.wait_ge(s["row_mm"], u - 1 - NC_UNITS)
                    sp.dma_start(unit[u % 2][:, :, :], w_mod[:, :, u * UM:(u + 1) * UM]).then_inc(unit_in[u % 2], 16)
                sp.wait_ge(s["q_out"], 16 * TL)

            @block.gpsimd
            def _(pool):
                pool.memset(ident[:, :], 0.0).then_inc(s["pool_order"], 1)
                pool.memset(ones[:, :], 1.0)
                pool.memset(eps_c[:, 0:1], -0.5)
                pool.memset(eps_c[:, 1:2], EPS * D)
                pool.wait_ge(s["pool_order"], 1)
                pool.affine_select(out=ident[:, :], in_=ident[:, :], compare_op=ALU.not_equal, fill=1.0,
                                   base=0, pattern=[[-1, P]], channel_multiplier=1).then_inc(s["ident_done"], 1)
                pool.memset(ss[:, 2, :], -0.5)
                pool.memset(ss[:, 3, :], EPS * HD).then_inc(s["eps_done"], 1)
                pool.wait_ge(s["eps_done"], 1)

                def one(n, par, kind):
                    pool.wait_ge(s["ss_done"], n + 1)
                    after(pool, s["xn_done"], n)
                    pool.tensor_tensor(stat[:, 1:2], stat[:, 0:1], eps_c[:, 1:2], ALU.add).then_inc(s["mean_done"], 1)
                    pool.wait_ge(s["mean_done"], n + 1)
                    pool.tensor_tensor(stat[:, 2:3], stat[:, 1:2], eps_c[:, 0:1], ALU.pow).then_inc(s["rstd_done"], 1)

                def two(n, par, kind):
                    c0 = 0 if kind == "lat" else QW
                    h0 = c0 // HD
                    pool.wait_ge(s["prj_done"], n + 1)
                    after(pool, s["hl_done"], n)
                    pool.tensor_tensor(sq[:, c0:QK], prj[:, FW + c0:FW + QK], prj[:, FW + c0:FW + QK], ALU.mult).then_inc(s["pool_qk"], 1)
                    pool.tensor_copy(vs[:, n, :, 0, :], prj[:, FW + QK:IN].rearrange("p (h d) -> p h d", d=HD)).then_inc(s["pool_v"], 1)
                    if kind == "lat":
                        pool.tensor_copy(f_tok[:, n - TC, :], prj[:, 0:FW]).then_inc(s["f_done"], 1)
                    pool.wait_ge(s["ss16_done"], n + 1)
                    after(pool, s["hl_done"], n)
                    pool.tensor_tensor(ss[:, 1, h0:NH], ss[:, 0, h0:NH], ss[:, 3, h0:NH], ALU.add).then_inc(s["eps_done"], 1)
                    pool.wait_ge(s["eps_done"], n + 2)
                    pool.tensor_tensor(ss[:, 0, h0:NH], ss[:, 1, h0:NH], ss[:, 2, h0:NH], ALU.pow).then_inc(s["rstd16_done"], 1)

                pipeline(pool, one, two, lambda n, par, kind: None)

            @block.scalar
            def _(act):
                act.wait_ge(s["vec_t"], 1)
                act.activation(c_sig[:, :, :].rearrange("p k j -> p j k"),
                               psum[:, 6, 0:2 * KD].rearrange("p (j k) -> p j k", k=KD), ACT.Silu).then_inc(s["silu_done"], 1)

                def one(n, par, kind):
                    act.wait_ge(s["x_in"], 16 * (n + 1))
                    after(act, s["rstd_done"], n)
                    act.activation(junk[:, :], xt[:, :], ACT.Square, accum_out=stat[:, 0:1]).then_inc(s["ss_done"], 1)
                    act.wait_ge(s["xT_done"], 2 * n + 1)
                    after(act, s["proj_done"], n - 1)
                    if isinstance(n, int) and n == 0:
                        act.wait_ge(s["cols_done"], 2)
                    j = 1 if kind == "ctx" else 0
                    for k in range(KD // 2):
                        i = act.activation(ht[par][:, k, :], psum[:, XT, k * P:(k + 1) * P], ACT.Identity,
                                           scale=mod_col[:, 0, j, k:k + 1], bias=mod_col[:, 1, j, k:k + 1])
                    i.then_inc(s["hTa"], 1)

                def two(n, par, kind):
                    act.wait_ge(s["proj_done"], n + 1)
                    c0 = 0 if kind == "lat" else FW + QW
                    after(act, s["pool_v"], n)
                    after(act, s["v_done"], n)
                    if not isinstance(n, int) or n > TC:
                        act.wait_ge(s["f_done"], n - TC)
                    pj = psum[:, PJ:PJ + 3, :].rearrange("p a n -> p (a n)")
                    act.activation(prj[:, c0:IN], pj[:, c0:IN], ACT.Copy).then_inc(s["prj_done"], 1)

                def three(n, par, kind):
                    base = (n - TC) * QTG + TC
                    if kind == "ctx":
                        act.wait_ge(s["qkt_done"], n + 1)
                        act.activation(ks[:, :, bass.ds(n * P, P)],
                                       psum[:, QT + 0, :].rearrange("p (h n) -> p h n", n=P), ACT.Copy).then_inc(s["qkt_act"], 4)
                        return
                    if not (isinstance(n, int) and n == TC):
                        act.wait_ge(s["q_out"], (n - TC) * 16)
                    for j in range(0, QTG, 2):
                        act.wait_ge(s["qkt_done"], base + j + 1)
                        src = psum[:, QT, :].rearrange("p (h n) -> p h n", n=P)
                        dst = ks[:, :, bass.ds(n * P, P)] if j == 0 else \
                            qst[:, 2 * (j - 1):2 * j, :, :].rearrange("p h a n -> p (h a) n")
                        act.activation(dst, src, ACT.Copy).then_inc(s["qkt_act"], 1)

                pipeline(act, one, two, three)

            @block.vector
            def _(dve):
                order = [0]

                def link(ins):
                    order[0] += 1
                    ins.then_inc(s["dve_order"], 1)
                    dve.wait_ge(s["dve_order"], order[0])

                dve.wait_ge(s["silu_done"], 1)
                link(dve.tensor_copy(bg_col[:, :], psum[:, 6, 2 * KD:5 * KD]))
                dve.wait_ge(s["unit_used"], NC_UNITS)
                cols = psum[:, 7, 0:4 * KD].rearrange("p (m k j) -> p m j k", k=KD, j=2)
                for j in range(2):
                    dve.tensor_tensor(mod_col[:, 1, j, :], cols[:, 0, j, :], bg_col[:, 0:KD], ALU.add)
                    link(dve.tensor_tensor(mod_col[:, 0, j, :], cols[:, 1, j, :], bg_col[:, KD:2 * KD], ALU.add))
                    i = dve.scalar_tensor_tensor(out=mod_col[:, 0, j, :], in0=mod_col[:, 0, j, :], scalar=1.0,
                                                 in1=g_col, op0=ALU.add, op1=ALU.mult)
                    i.then_inc(s["cols_done"], 1)
                dve.wait_ge(s["cols_done"], 2)
                dve.wait_ge(s["tables_in"], 16 * 3)
                first_order = order[0]
                CH = {"lat": 5, "ctx": 2}

                def one(n, par, kind):
                    dve.wait_ge(s["rstd_done"], n + 1)
                    after(dve, s["xT_done"], 2 * n)
                    dve.tensor_scalar(xn[:, :], xt[:, :], stat[:, 2:3], ROOT, ALU.mult, ALU.mult).then_inc(s["xn_done"], 1)
                    dve.wait_ge(s["xT_done"], 2 * n + 2)
                    after(dve, s["proj_done"], n - 1)
                    j = 1 if kind == "ctx" else 0
                    for k in range(KD // 2, KD):
                        i = dve.tensor_scalar(ht[par][:, k, :], psum[:, XT + 1, (k - KD // 2) * P:(k - KD // 2 + 1) * P],
                                              mod_col[:, 0, j, k:k + 1], mod_col[:, 1, j, k:k + 1], ALU.mult, ALU.add)
                    i.then_inc(s["hTb"], 1)

                def two(n, par, kind):
                    c0 = 0 if kind == "lat" else QW
                    h0 = c0 // HD
                    nh = NH - h0
                    if kind == "ctx":
                        base = first_order + n * CH["ctx"]
                    else:
                        base = first_order + TC * CH["ctx"] + (n - TC) * CH["lat"]
                    count = [0]

                    def chain(ins):
                        count[0] += 1
                        ins.then_inc(s["dve_order"], 1)
                        dve.wait_ge(s["dve_order"], base + count[0])

                    def hv(ap):
                        return ap.rearrange("p (h d) -> p h d", d=HD)
                    dve.wait_ge(s["prj_done"], n + 1)
                    dve.wait_ge(s["pool_v"], n + 1)
                    dve.tensor_tensor(vs[:, n, :, 1, :], hv(prj[:, FW + QK:IN]), vs[:, n, :, 0, :].bitcast(F32), ALU.subtract)
                    if kind == "lat":
                        dve.tensor_tensor(hv(qkn[:, 0:QW]), hv(prj[:, FW:FW + QW]),
                                          g_qk[:, 0, :].unsqueeze(1).broadcast_to([P, NQ, HD]), ALU.mult)
                    dve.tensor_tensor(hv(qkn[:, QW:QK]), hv(prj[:, FW + QW:FW + QK]),
                                      g_qk[:, 1, :].unsqueeze(1).broadcast_to([P, NKV, HD]), ALU.mult).then_inc(s["v_done"], 1)
                    dve.wait_ge(s["pool_qk"], n + 1)
                    dve.tensor_reduce(ss[:, 0, h0:NH], hv(sq[:, c0:QK]), AX, ALU.add).then_inc(s["ss16_done"], 1)
                    dve.wait_ge(s["rstd16_done"], n + 1)
                    chain(dve.tensor_tensor(hv(qkn[:, c0:QK]), hv(qkn[:, c0:QK]),
                                            ss[:, 0, h0:NH].unsqueeze(2).broadcast_to([P, nh, HD]), ALU.mult))
                    v = qkn
                    if kind == "lat":
                        t = n - TC
                        q5 = qkn[:, :].rearrange("p (h g s d) -> p h g s d", g=2, s=2, d=HD // 4)
                        r5 = rot[:, :].rearrange("p (h g s d) -> p h g s d", g=2, s=2, d=HD // 4)
                        for half in range(2):
                            tab = rope[:, 1, t, :].rearrange("p (g s d) -> p g s d", g=2, s=2)[:, :, half, :]
                            i = dve.tensor_tensor(r5[:, :, :, half, :], q5[:, :, :, 1 - half, :],
                                                  tab.unsqueeze(1).broadcast_to([P, NH, 2, HD // 4]), ALU.mult)
                        chain(i)
                        chain(dve.tensor_tensor(hv(qkn[:, :]), hv(qkn[:, :]),
                                                rope[:, 0, t, :].unsqueeze(1).broadcast_to([P, NH, HD]), ALU.mult))
                        chain(dve.tensor_tensor(rot[:, :], rot[:, :], qkn[:, :], ALU.add))
                        v = rot
                    if kind == "ctx":
                        after(dve, s["qkt_done"], n)
                    else:
                        after(dve, s["qkt_done"], (n - TC) * QTG + TC)
                    if kind == "lat":
                        vq = hv(v[:, 0:QW]).unsqueeze(2).broadcast_to([P, NQ, 2, HD])
                        dve.tensor_copy(hlq[:, :, 0, :, :], vq)
                    chain(dve.tensor_copy(hlk[:, :, 0, :], hv(v[:, QW:QK])))
                    if kind == "lat":
                        dve.tensor_tensor(hlq[:, :, 1, :, :], vq, hlq[:, :, 0, :, :].bitcast(F32), ALU.subtract)
                    dve.tensor_tensor(hlk[:, :, 1, :], hv(v[:, QW:QK]), hlk[:, :, 0, :].bitcast(F32), ALU.subtract).then_inc(s["hl_done"], 1)
                    assert count[0] == CH[kind]

                def three(n, par, kind):
                    if kind == "ctx":
                        return
                    base = (n - TC) * QTG + TC
                    if not (isinstance(n, int) and n == TC):
                        dve.wait_ge(s["q_out"], (n - TC) * 16)
                    for j in range(1, QTG, 2):
                        dve.wait_ge(s["qkt_done"], base + j + 1)
                        dve.tensor_copy(qst[:, 2 * (j - 1):2 * j, :, :].rearrange("p h a n -> p (h a n)"),
                                        psum[:, QT + 1, :]).then_inc(s["qkt_dve"], 1)

                pipeline(dve, one, two, three, early=True)
                dve.wait_ge(s["f_done"], TL)
                dve.tensor_copy(c_wide, c_sig[:, :, 0:1].broadcast_to([P, KD, P])).then_inc(s["wide_done"], 1)
                dve.wait_ge(s["norm_row_in"], 32)
                end = first_order + TC * CH["ctx"] + TL * CH["lat"]
                order[0] = end
                for u in range(NR_UNITS):
                    r = rows[:, u * UM // D, u * UM % D:u * UM % D + UM]
                    dve.wait_ge(s["row_mm"], u + 1)
                    i = dve.tensor_tensor(r, psum[:, u % 2, 0:UM], r, ALU.add).then_inc(s["row_done"], 1)
                dve.wait_ge(s["row_done"], NR_UNITS)
                dve.scalar_tensor_tensor(out=rows[:, SC2, :], in0=rows[:, SC2, :], scalar=1.0, in1=sq[:, 0:D],
                                         op0=ALU.add, op1=ALU.mult).then_inc(s["row_done"], 1)
                dve.wait_ge(s["row_done"], NR_UNITS + 1)
                dve.tensor_scalar(rows[:, SC2, :], rows[:, SC2, :], ROOT, None, ALU.mult)

            @block.tensor
            def _(pe):
                pe.wait_ge(s["ident_done"], 1)
                pe.wait_ge(s["small_in"], 16 * 4)
                pe.transpose(psum[:, 6, 0:5 * KD], vec[:, :], ident[0:5 * KD, 0:5 * KD]).then_inc(s["vec_t"], 1)
                pe.wait_ge(s["silu_done"], 1)
                for u in range(NC_UNITS):
                    pe.wait_ge(unit_in[u % 2], 16 * (u // 2 + 1))
                    for j in range(UM // P):
                        col = (u * (UM // P) + j) * 2
                        for k in range(KD):
                            i = pe.matmul(psum[:, 7, col:col + 2], unit[u % 2][:, k, j * P:(j + 1) * P], c_sig[:, k, :],
                                          start=(k == 0), stop=(k == KD - 1))
                    i.then_inc(s["unit_used"], 1)

                def one(n, par, kind):
                    pe.wait_ge(s["xn_done"], n + 1)
                    after(pe, s["hTa"], n)
                    after(pe, s["hTb"], n)
                    for k in range(KD):
                        i = pe.transpose(psum[:, XT + k // 4, (k % 4) * P:(k % 4 + 1) * P], xn[:, k * P:(k + 1) * P], ident[:, :])
                        if k % 4 == 3:
                            i.then_inc(s["xT_done"], 1)

                def two(n, par, kind):
                    pe.wait_ge(s["hTa"], n + 1)
                    pe.wait_ge(s["hTb"], n + 1)
                    if isinstance(n, int) and n == 0:
                        pe.wait_ge(s["win_in"], 16)
                    after(pe, s["prj_done"], n)
                    for c in ((1, 0, 2) if kind == "lat" else (2,)):
                        for k in range(KD):
                            i = pe.matmul(psum[:, PJ + c, :], ht[par][:, k, :], win[:, k, c * 512:(c + 1) * 512],
                                          start=(k == 0), stop=(k == KD - 1))
                    i.then_inc(s["proj_done"], 1)

                def three(n, par, kind):
                    pe.wait_ge(s["hl_done"], n + 1)
                    q32 = hlq[:, :, :, :, :].rearrange("p h a b d -> p (h a b d)").bitcast(F32)
                    k32 = hlk[:, :, :, :].rearrange("p h a d -> p (h a d)").bitcast(F32)
                    for j in range(QTG if kind == "lat" else 1):
                        if j % 2 == 0:
                            if j == 0:
                                after(pe, s["qkt_act"], n * 4)
                            else:
                                pe.wait_ge(s["qkt_act"], n * 4 + j // 2)
                        elif j == 1:
                            after(pe, s["qkt_dve"], (n - TC) * 3)
                        else:
                            pe.wait_ge(s["qkt_dve"], (n - TC) * 3 + j // 2)
                        for b in range(4):
                            if j == 0:
                                src = k32[:, b * P:(b + 1) * P]
                            else:
                                src = q32[:, (4 * (j - 1) + b) * P:(4 * (j - 1) + b + 1) * P]
                            i = pe.transpose(psum[:, QT + j % 2, b * P:(b + 1) * P], src, ident[:, :])
                        i.then_inc(s["qkt_done"], 1)

                pipeline(pe, one, two, three)
                pe.wait_ge(s["wide_done"], 1)
                for u in range(NR_UNITS):
                    pe.wait_ge(unit_in[u % 2], 16 * ((u + NC_UNITS) // 2 + 1))
                    if u >= 2:
                        pe.wait_ge(s["row_done"], u - 1)
                    else:
                        pe.wait_ge(s["hTa"], TS)
                        pe.wait_ge(s["hTb"], TS)
                    for k in range(KD):
                        i = pe.matmul(psum[:, u % 2, 0:UM], c_wide[:, k, :], unit[u % 2][:, k, :], start=(k == 0), stop=(k == KD - 1))
                    i.then_inc(s["row_mm"], 1)
        A.close()
        nc_phase_b(nc, ctx, sem, sb, a, K, psum, ident, ones, rows, aff, eps_c, ks, vs, f_tok, y_t,
                   q_d, h2_d, acc_d, x_d)
        K.close()
        nc_phase_m(nc, ctx, sem, sb, a, psum, ident, rows, aff, eps_c, h2_d, acc_d, w_gate, w_up, w_down, out_d)


def after(eng, sem_, v):
    if not (isinstance(v, int) and v <= 0):
        eng.wait_ge(sem_, v)


def nc_phase_b(nc, ctx, sem, sb, a, K, psum, ident, ones, rows, aff, eps_c, ks, vs, f_tok, y_t,
               q_d, h2_d, acc_d, x_d):
    G1, SH2, SC2, G2 = range(4)

    F = ExitStack()
    dft = sb("dft", [P, 2, TL, HALF + 1], F32, F)
    chan = sb("chan", [P, 3, P], F32, F)
    wf = sb("wf", [P, 2, P], F32, F)
    ab = sb("ab", [P, 2, 3, P], F32, F)
    gt = sb("gt", [P, 2, 2, HALF + 1], F32, F)
    s = {n: sem("f_" + n) for n in ("wf_zero", "chan_in", "dft_in", "ab_mm", "ab_done", "g_mm", "g_done", "y_mm", "y_done")}
    with nc.Block() as block:
        @block.sync
        def _(sp):
            for i in range(2):
                for h in range(4):
                    sp.dma_start(dft[:, i, 2 * h:2 * h + 2, 0:HALF],
                                 a["dft"][i].rearrange("(t p) m -> p t m", p=P)[:, 2 * h:2 * h + 2, :]).then_inc(s["dft_in"], 16)
            sp.dma_start(chan[:, :, :], a["chan"].rearrange("a p n -> p a n")).then_inc(s["chan_in"], 16)
            sp.wait_ge(s["wf_zero"], 1)
            for g in range(FG):
                h = g % 2
                sp.dma_start(wf[h * FD:(h + 1) * FD, g // 2, h * FD:(h + 1) * FD], a["w_four"][0, g]).then_inc(s["chan_in"], 16)

        @block.vector
        def _(dve):
            dve.memset(wf[:, :, :], 0.0).then_inc(s["wf_zero"], 1)
            for c in range(2):
                dve.wait_ge(s["ab_mm"], c + 1)
                dve.tensor_copy(ab[:, c, :, :].rearrange("p a n -> p (a n)"), psum[:, 4 + c, 0:3 * P]).then_inc(s["ab_done"], 1)
            dve.wait_ge(s["g_mm"], 4)
            dve.tensor_copy(gt[:, :, :, HALF - 1], psum[:, 6, 0:4].rearrange("p (c i) -> p c i", i=2)).then_inc(s["g_done"], 1)
            for c in range(2):
                dve.wait_ge(s["y_mm"], 3 * c + 2)
                dve.tensor_copy(y_t[:, c, N - 1:HALF - 1:-1], psum[:, 2 * c + 1, 0:HALF - 2]).then_inc(s["y_done"], 1)
            dve.wait_ge(s["y_mm"], 6)
            dve.tensor_copy(y_t[:, :, HALF - 1], psum[:, 7, 0:2]).then_inc(s["y_done"], 1)

        @block.scalar
        def _(act):
            for c in range(2):
                for i in range(2):
                    act.wait_ge(s["g_mm"], 2 * c + i + 1)
                    act.activation(gt[:, c, i, 0:HALF - 1], psum[:, 2 * c + i, :], ACT.Copy).then_inc(s["g_done"], 1)
            for c in range(2):
                act.wait_ge(s["y_mm"], 3 * c + 1)
                act.activation(y_t[:, c, 0:HALF - 1], psum[:, 2 * c, :], ACT.Copy).then_inc(s["y_done"], 1)

        @block.tensor
        def _(pe):
            pe.wait_ge(s["chan_in"], 16 * 5)
            for c in range(2):
                for j in range(3):
                    i = pe.matmul(psum[:, 4 + c, j * P:(j + 1) * P], chan[:, j, :], wf[:, c, :], start=True, stop=True)
                i.then_inc(s["ab_mm"], 1)
            pe.wait_ge(s["dft_in"], 16 * 8)
            for c in range(2):
                for i in range(2):
                    for t in range(TL):
                        pe.matmul(psum[:, 2 * c + i, :], f_tok[:, t, c * P:(c + 1) * P], dft[:, i, t, 0:512],
                                  start=(t == 0), stop=(t == TL - 1))
                    for t in range(TL):
                        m = pe.matmul(psum[:, 6, 2 * c + i:2 * c + i + 1], f_tok[:, t, c * P:(c + 1) * P], dft[:, i, t, 512:513],
                                      start=(t == 0), stop=(t == TL - 1))
                    m.then_inc(s["g_mm"], 1)
            pe.wait_ge(s["ab_done"], 2)
            pe.wait_ge(s["g_done"], 5)
            for c in range(2):
                for (bank, lo, hi, b) in ((2 * c, 0, 512, 1), (2 * c + 1, 1, 512, 2), (7, 512, 513, 1)):
                    o = psum[:, bank, 0:hi - lo] if bank < 7 else psum[:, 7, c:c + 1]
                    pe.matmul(o, ab[:, c, 0, :], gt[:, c, 0, lo:hi], start=True, stop=False)
                    pe.matmul(o, ab[:, c, b, :], gt[:, c, 1, lo:hi], start=False, stop=True).then_inc(s["y_mm"], 1)
    F.close()

    B = ExitStack()
    wout = sb("wout", [P, KD, D], F32, B)
    wrt = sb("wrt", [P, KD, E], F32, B)
    qt = sb("qt", [P, NQ, 2, P], F32R, B)
    pr = [sb(f"pr{i}", [P, KEYS], F32, B) for i in range(6)]
    pth = sb("pth", [P, 4, REP * P], F32R, B)
    ptl = sb("ptl", [P, 4, REP * P], F32R, B)
    diag = [sb(f"diag{i}", [P, REP, P], F32, B) for i in range(2)]
    rbc = sb("rbc", [P, REP * P], F32, B)
    oth = sb("oth", [P, REP * P], F32, B)
    osum = sb("osum", [P, REP * P], F32, B)
    mix = sb("mix", [P, KD, P], F32, B)
    mx = sb("mx", [P, NQ, 4], F32, B)
    nb = sb("nb", [P, NQ], F32, B)
    den = sb("den", [P, NQ, 4], F32, B)
    rden = sb("rden", [P, NQ], F32, B)
    xr = sb("xr", [P, D], F32, B)
    x2 = sb("x2", [P, D], F32, B)
    h2 = sb("h2", [P, D], F32, B)
    junk2 = sb("junk2", [P, D], F32, B)
    h2t = sb("h2t", [P, KD, P], F32, B)
    st2 = sb("st2", [P, 4], F32, B)
    lg = sb("lg", [P, 4, E], F32, B)
    s = {n: sem("b_" + n) for n in (
        "w_in", "q_in", "s_done", "nb_done", "exp_done", "t_done", "hi_done", "lo_done", "pv_done", "osum_done",
        "rden_done", "diag_done", "misc_mm", "misc_free", "oth_done", "rbc_done", "mix_done", "ymix_done", "x_in",
        "x2_done", "ss_done", "rstd_done", "mean", "h2a", "h2b", "h2_out", "x2_out", "h2t_done", "neg_done", "lexp", "aff_rows",
        "dve_order", "op_sum")}
    CH = [(0, 512), (512, 1024), (1024, KEYS)]
    NCH = len(CH)
    NS = NCH * NQ
    KT = TS
    NT = KT * NKV
    PTB, OB, MB = 4, 6, 7
    MISC0 = 2

    def misc(t, j):
        return j if isinstance(t, int) and t == 0 else MISC0 + 10 * (t - 1) + j

    def schedule(eng_step, eng):
        eng_step(0, False, True)
        eng_step(1, True, True)
        with eng.Fori(2, TL) as t:
            eng_step(t, True, True)
        eng_step(TL, True, False)

    def use_numbers(prev, cur):
        names = []
        if prev:
            names += ["R0", "R3", "OP0", "OP1"]
        if cur:
            names += ["R6"]
        if prev:
            names += ["HT0"]
        if cur:
            names += ["R9"]
        if prev:
            names += ["HT1", "RT", "AF"]
        return {n: i for i, n in enumerate(names)}

    def flushes(prev, cur):
        return {sl: sl // 3 - 2 for sl in (0, 3, 6, 9) if (prev if sl < 6 else cur)}

    def items(i, prev, cur):
        g = i // 3 - 1
        if (g < 0 and not prev) or (g >= 0 and not cur):
            return []
        lo, hi = ((0, 4), (4, 7), (7, 10))[i % 3]
        return [KT * g + k for k in range(lo, hi)]

    with nc.Block() as block:
        @block.sync
        def _(sp):
            sp.dma_start(wrt[:, :, :], a["w_router"][0].rearrange("(k p) e -> p k e", p=P)).then_inc(s["w_in"], 16)
            wo = a["w_out"][0]
            for g in range(NKV):
                half = (g % 2) * HD
                sp.dma_start(wout[half:half + HD, 3 * (g // 2):3 * (g // 2) + REP, :],
                             wo[FW + g * REP * HD:FW + (g + 1) * REP * HD, :].rearrange("(r p) n -> p r n", p=HD)).then_inc(s["w_in"], 16)
            sp.dma_start(wout[:, 6:8, :], wo[0:FW, :].rearrange("(k p) n -> p k n", p=P)).then_inc(s["w_in"], 16)

            def step(t, prev, cur):
                if cur:
                    after(sp, s["s_done"], t * NS)
                    sp.dma_start(qt[:, :, :, :].rearrange("p h a n -> p (h a n)").bitcast(F32), q_d[t]).then_inc(s["q_in"], 16)
                if prev:
                    after(sp, s["x2_done"], (t - 1) * 2)
                    sp.dma_start(xr[:, :], x_d[t - 1]).then_inc(s["x_in"], 16)
                    sp.wait_ge(s["x2_done"], t * 2)
                    sp.dma_start(acc_d.rearrange("(t p) d -> t p d", p=P)[t - 1], x2[:, :]).then_inc(s["x2_out"], 16)
                    sp.wait_ge(s["h2b"], t)
                    sp.dma_start(h2_d.rearrange("(t p) d -> t p d", p=P)[t - 1], h2[:, :]).then_inc(s["h2_out"], 16)
            schedule(step, sp)
            sp.wait_ge(s["x2_out"], 16 * TL)
            sp.wait_ge(s["h2_out"], 16 * TL)

        @block.gpsimd
        def _(pool):
            def step(t, prev, cur):
                use = use_numbers(prev, cur)
                if prev:
                    after(pool, s["x2_done"], 2 * (t - 1))
                    pool.tensor_copy(mix[:, 6:8, :], y_t[:, :, bass.ds((t - 1) * P, P)]).then_inc(s["ymix_done"], 1)
                for i in range(NQ):
                    if cur:
                        g, r = i // 3, i % 3
                        if r == 0:
                            if f"R{i}" in use:
                                pool.wait_ge(s["misc_mm"], misc(t, use[f"R{i}"]) + 1)
                        pool.wait_ge(s["rden_done"], NQ * t + i + 1)
                        pool.tensor_tensor(diag[g % 2][:, r, :], ident[:, :], rden[:, i:i + 1].broadcast_to([P, P]), ALU.mult).then_inc(s["diag_done"], 1)
                    if prev and i == 6:
                        pool.wait_ge(s["ss_done"], t)
                        pool.tensor_tensor(st2[:, 1:2], st2[:, 0:1], eps_c[:, 1:2], ALU.add).then_inc(s["mean"], 1)
                        pool.wait_ge(s["mean"], t)
                        pool.tensor_tensor(st2[:, 2:3], st2[:, 1:2], eps_c[:, 0:1], ALU.pow).then_inc(s["rstd_done"], 1)
            schedule(step, pool)

        @block.scalar
        def _(act):
            def step(t, prev, cur):
                use = use_numbers(prev, cur)
                fl = flushes(prev, cur)
                for i in range(NQ):
                    if i in fl:
                        G = 4 * t + fl[i]
                        act.wait_ge(s["pv_done"], KT * (G + 1))
                        after(act, s["osum_done"], G)
                        if fl[i] % 2 == 0:
                            act.activation(oth[0:HD, :], psum[HD:P, OB, 0:REP * P], ACT.Copy).then_inc(s["oth_done"], 1)
                        else:
                            act.activation(oth[HD:P, :], psum[0:HD, OB, 0:REP * P], ACT.Copy).then_inc(s["oth_done"], 1)
                        act.wait_ge(s["misc_mm"], misc(t, use[f"R{i}"]) + 1)
                        after(act, s["mix_done"], G)
                        act.activation(rbc[:, :], psum[:, MB, 0:REP * P], ACT.Copy).then_inc(s["misc_free"], 1)
                    ex = list(range(NCH)) if cur else []
                    its = items(i, prev, cur)
                    while ex or its:
                        if its:
                            k = its.pop(0)
                            n = NT * t + k
                            act.wait_ge(s["t_done"], n + 1)
                            if not (isinstance(t, int) and t == 0 and k < 4):
                                act.wait_ge(s["pv_done"], n - 3)
                            act.activation(pth[:, k % 4, :], psum[:, PTB + k % 2, 0:REP * P], ACT.Copy).then_inc(s["hi_done"], 1)
                        if ex:
                            c = ex.pop(0)
                            lo, hi = CH[c]
                            b = (NCH * i + c) % 4
                            if c == 0:
                                act.wait_ge(s["nb_done"], NQ * t + i + 1)
                                g = i // 3
                                if not (isinstance(t, int) and t == 0 and g < 2):
                                    act.wait_ge(s["t_done"], KT * (4 * t + g - 1))
                            act.activation(pr[(i // 3 % 2) * 3 + i % 3][:, lo:hi], psum[:, b, 0:hi - lo], ACT.Exp,
                                           bias=nb[:, i:i + 1], scale=SCALE, accum_out=den[:, i, c:c + 1]).then_inc(s["exp_done"], 1)
                    if prev and i == 8:
                        act.wait_ge(s["misc_mm"], misc(t, use["HT0"]) + 1)
                        after(act, s["neg_done"], t - 1)
                        act.activation(h2t[:, 0:4, :].rearrange("p k n -> p (k n)"), psum[:, MB, :], ACT.Copy).then_inc(s["misc_free"], 1)
                    if prev and i == 9:
                        act.wait_ge(s["misc_mm"], misc(t, use["HT1"]) + 1)
                        act.activation(h2t[:, 4:8, :].rearrange("p k n -> p (k n)"), psum[:, MB, :], ACT.Copy).then_inc(s["misc_free"], 1)
                    if prev and i == 5:
                        act.wait_ge(s["x2_done"], 2 * t)
                        after(act, s["rstd_done"], t - 1)
                        act.activation(junk2[:, :], x2[:, :], ACT.Square, accum_out=st2[:, 0:1]).then_inc(s["ss_done"], 1)
                    if prev and i == 10:
                        act.wait_ge(s["neg_done"], t)
                        act.activation(lg[:, 1, :], psum[:, MB, 0:E], ACT.Exp, bias=st2[:, 3:4], scale=1.0,
                                       accum_out=lg[:, 2, 0:1]).then_inc(s["lexp"], 1)
                    if prev and i == 11:
                        act.wait_ge(s["misc_mm"], misc(t, use["AF"]) + 1)
                        act.activation(aff[:, bass.ds((t - 1) * P, P)], psum[0:E, MB, 0:P], ACT.Copy).then_inc(s["misc_free"], 1)
            schedule(step, act)

        @block.vector
        def _(dve):
            def step(t, prev, cur):
                use = use_numbers(prev, cur)
                fl = flushes(prev, cur)
                PER0, PER = 2 * NQ, 2 * NQ + 2
                base = 0 if isinstance(t, int) and t == 0 else PER0 + (t - 1) * PER
                count = [0]

                def chain(ins):
                    count[0] += 1
                    ins.then_inc(s["dve_order"], 1)
                    dve.wait_ge(s["dve_order"], base + count[0])
                for i in range(NQ):
                    if cur:
                        for c, (lo, hi) in enumerate(CH):
                            b = (NCH * i + c) % 4
                            dve.wait_ge(s["s_done"], NS * t + NCH * i + c + 1)
                            ins = dve.tensor_reduce(mx[:, i, c:c + 1], psum[:, b, 0:hi - lo], AX, ALU.max)
                        chain(ins)
                        chain(dve.tensor_reduce(mx[:, i, 3:4], mx[:, i, 0:3], AX, ALU.max))
                        dve.tensor_scalar(nb[:, i:i + 1], mx[:, i, 3:4], -SCALE, None, ALU.mult).then_inc(s["nb_done"], 1)
                    if i in fl:
                        G = 4 * t + fl[i]
                        par = fl[i] % 2
                        h = slice(par * HD, (par + 1) * HD)
                        g = fl[i] % 4
                        dve.wait_ge(s["oth_done"], G + 1)
                        dve.tensor_tensor(osum[h, :], psum[h, OB, 0:REP * P], oth[h, :], ALU.add).then_inc(s["osum_done"], 1)
                        dve.wait_ge(s["osum_done"], G + 1)
                        dve.wait_ge(s["misc_free"], misc(t, use[f"R{i}"]) + 1)
                        dve.tensor_tensor(mix[h, 3 * (g // 2):3 * (g // 2) + REP, :].rearrange("p r n -> p (r n)"),
                                          osum[h, :], rbc[h, :], ALU.mult).then_inc(s["mix_done"], 1)
                    for k in items(i, prev, cur):
                        n = NT * t + k
                        dve.wait_ge(s["hi_done"], n + 1)
                        dve.tensor_tensor(ptl[:, k % 4, :], psum[:, PTB + k % 2, 0:REP * P], pth[:, k % 4, :].bitcast(F32),
                                          ALU.subtract).then_inc(s["lo_done"], 1)
                    if cur:
                        dve.wait_ge(s["exp_done"], NS * t + NCH * (i + 1))
                        ins = dve.tensor_reduce(den[:, i, 3:4], den[:, i, 0:3], AX, ALU.add)
                        if not (isinstance(t, int) and t == 0):
                            dve.wait_ge(s["diag_done"], NQ * (t - 1) + i + 1)
                        ins.then_inc(s["op_sum"], 1)
                        dve.wait_ge(s["op_sum"], NQ * t + i + 1)
                        dve.reciprocal(rden[:, i:i + 1], den[:, i, 3:4]).then_inc(s["rden_done"], 1)
                    if prev and i in (4, 5):
                        j = i - 4
                        c = slice(j * 512, (j + 1) * 512)
                        dve.wait_ge(s["misc_mm"], misc(t, use[f"OP{j}"]) + 1)
                        if j == 0:
                            dve.wait_ge(s["x_in"], 16 * t)
                            after(dve, s["x2_out"], 16 * (t - 1))
                            after(dve, s["h2a"], t - 1)
                        dve.tensor_tensor(x2[:, c], psum[:, MB, :], rows[:, G1, c], ALU.mult).then_inc(s["misc_free"], 1)
                        dve.wait_ge(s["misc_free"], misc(t, use[f"OP{j}"]) + 1)
                        dve.tensor_tensor(x2[:, c], x2[:, c], xr[:, c], ALU.add).then_inc(s["x2_done"], 1)
                    if prev and i == 6:
                        dve.wait_ge(s["rstd_done"], t)
                        after(dve, s["h2_out"], 16 * (t - 1))
                        dve.scalar_tensor_tensor(out=h2[:, :], in0=x2[:, :], scalar=st2[:, 2:3], in1=rows[:, SC2, :],
                                                 op0=ALU.mult, op1=ALU.mult).then_inc(s["h2a"], 1)
                        dve.wait_ge(s["h2a"], t)
                        dve.tensor_tensor(h2[:, :], h2[:, :], rows[:, SH2, :], ALU.add).then_inc(s["h2b"], 1)
                    if prev and i == 10:
                        dve.wait_ge(s["misc_mm"], misc(t, use["RT"]) + 1)
                        chain(dve.tensor_reduce(lg[:, 2, 1:2], psum[:, MB, 0:E], AX, ALU.max))
                        dve.tensor_scalar(st2[:, 3:4], lg[:, 2, 1:2], -1.0, None, ALU.mult).then_inc(s["neg_done"], 1)
                    if prev and i == 11:
                        dve.wait_ge(s["lexp"], t)
                        chain(dve.reciprocal(lg[:, 2, 2:3], lg[:, 2, 0:1]))
                        dve.tensor_scalar(lg[:, 0, :], lg[:, 1, :], lg[:, 2, 2:3], None, ALU.mult).then_inc(s["misc_free"], 1)
            schedule(step, dve)

        @block.tensor
        def _(pe):
            pe.wait_ge(s["w_in"], 16 * 6)

            def step(t, prev, cur):
                use = use_numbers(prev, cur)
                fl = flushes(prev, cur)

                def times(k):
                    n = NT * t + k
                    g, kt = k // KT, k % KT
                    pe.wait_ge(s["lo_done"], n + 1)
                    if kt == 0:
                        after(pe, s["osum_done"], 4 * t + g)
                    v = vs[:, kt, g % 4, :, :].rearrange("p a d -> p (a d)")
                    pe.matmul(psum[:, OB, 0:REP * P], v, pth[:, k % 4, :], start=(kt == 0), stop=False)
                    ins = pe.matmul(psum[:, OB, 0:REP * P], v, ptl[:, k % 4, :], start=False, stop=(kt == KT - 1))
                    ins.then_inc(s["pv_done"], 1)

                def misc_free(name):
                    after(pe, s["misc_free"], misc(t, use[name]))

                if cur:
                    pe.wait_ge(s["q_in"], 16 * (t + 1))
                for i in range(NQ):
                    if cur:
                        for c, (lo, hi) in enumerate(CH):
                            n = NCH * i + c
                            if not (isinstance(t, int) and t == 0 and n < 4):
                                pe.wait_ge(s["exp_done"], NS * t + n - 3)
                            o = psum[:, n % 4, 0:hi - lo]
                            pe.matmul(o, qt[:, i, 0, :], ks[:, i // 3, lo:hi], start=True, stop=False)
                            pe.matmul(o, qt[:, i, 1, :], ks[:, i // 3, lo:hi], start=False, stop=True).then_inc(s["s_done"], 1)
                    if i in fl:
                        k0 = KT * (fl[i] + 1)
                        times(k0 - 2)
                        times(k0 - 1)
                        G = 4 * t + fl[i]
                        pe.wait_ge(s["diag_done"], 3 * (G + 1))
                        misc_free(f"R{i}")
                        pe.matmul(psum[:, MB, 0:REP * P], ones[:, :], diag[fl[i] % 2][:, :, :].rearrange("p r n -> p (r n)"),
                                  start=True, stop=True).then_inc(s["misc_mm"], 1)
                    for k in items(i, prev, cur):
                        n = NT * t + k
                        g, kt = k // KT, k % KT
                        if kt == 0:
                            pe.wait_ge(s["exp_done"], 9 * (4 * t + g + 1))
                        if not (isinstance(t, int) and t == 0 and k < 2):
                            pe.wait_ge(s["lo_done"], n - 1)
                        for r in range(REP):
                            ins = pe.transpose(psum[:, PTB + k % 2, r * P:(r + 1) * P],
                                               pr[(g % 2) * 3 + r][:, kt * P:(kt + 1) * P], ident[:, :])
                        ins.then_inc(s["t_done"], 1)
                        if kt >= 2:
                            times(k - 2)
                    if prev and i in (4, 5):
                        j = i - 4
                        pe.wait_ge(s["mix_done"], 4 * t)
                        pe.wait_ge(s["ymix_done"], t)
                        misc_free(f"OP{j}")
                        for k in range(KD):
                            ins = pe.matmul(psum[:, MB, :], mix[:, k, :], wout[:, k, j * 512:(j + 1) * 512],
                                            start=(k == 0), stop=(k == KD - 1))
                        ins.then_inc(s["misc_mm"], 1)
                    if prev and i in (8, 9):
                        j = i - 8
                        pe.wait_ge(s["h2b"], t)
                        misc_free(f"HT{j}")
                        for k in range(4):
                            ins = pe.transpose(psum[:, MB, k * P:(k + 1) * P], h2[:, (4 * j + k) * P:(4 * j + k + 1) * P], ident[:, :])
                        ins.then_inc(s["misc_mm"], 1)
                    if prev and i == 10:
                        misc_free("RT")
                        for k in range(KD):
                            ins = pe.matmul(psum[:, MB, 0:E], h2t[:, k, :], wrt[:, k, :], start=(k == 0), stop=(k == KD - 1))
                        ins.then_inc(s["misc_mm"], 1)
                    if prev and i == 11:
                        misc_free("AF")
                        pe.transpose(psum[0:E, MB, 0:P], lg[:, 0, :], ident[:, :]).then_inc(s["misc_mm"], 1)
            schedule(step, pe)
    B.close()


def nc_phase_m(nc, ctx, sem, sb, a, psum, ident, rows, aff, eps_c, h2_d, acc_d, w_gate, w_up, w_down, out_d):
    G1, SH2, SC2, G2 = range(4)

    M = ExitStack()
    NU = 6
    NJ = DE // UC
    unit = [sb(f"munit{i}", [P, KD * UC], F32, M) for i in range(NU)]
    top = sb("top", [E, CAP], F32, M)
    topi = sb("topi", [E, CAP], U32, M)
    topf = sb("topf", [E, CAP], F32, M)
    icol = sb("icol", [P, E], U32, M)
    gcol = sb("gcol", [P, E], F32, M)
    idx_g = sb("idx_g", [P, 1], U32, M)
    idx_s = sb("idx_s", [P, 1], U32, M)
    gate_s = sb("gate_s", [P, 1], F32, M)
    xe = sb("xe", [P, D], F32, M)
    xet = sb("xet", [P, KD, P], F32, M)
    sil = [sb(f"sil{i}", [P, UC], F32, M) for i in range(2)]
    hid = [sb(f"hid{i}", [P, UC], F32, M) for i in range(2)]
    hidt = [sb(f"hidt{i}", [P, UC // P, P], F32, M) for i in range(2)]
    ysc = sb("ysc", [P, D], F32, M)
    carry = sb("carry", [P, 2], F32, M)
    fgain = sb("fgain", [P, D], F32, M)
    xa = [sb(f"xa{i}", [P, D], F32, M) for i in range(4)]
    sqj = sb("sqj", [P, D], F32, M)
    fst = sb("fst", [P, TL, 3], F32, M)
    s = {n: sem("m_" + n) for n in (
        "top_order", "carried", "top_done", "top_t", "cols_done", "idx_g", "x_in", "x_mm", "x_a", "x_b",
        "gate_mm", "up_mm", "sil_done", "hid_done", "ht_mm", "ht_done", "down_mm", "y_done", "y_out", "sel_done",
        "fg_in", "a_done", "mean", "rstd", "norm_done", "out_done")}
    unit_in = [sem(f"munit_in{i}") for i in range(NU)]
    NX = 4
    xa_in = [sem(f"xa_in{i}") for i in range(NX)]
    xa_out = [sem(f"xa_out{i}") for i in range(NX)]
    Y, HB, XB = 4, 6, 7

    def arrived(e, k):
        v = 2 * e + k // NU + 1
        return 16 * (v - 1 if k % NU == 2 and not (isinstance(e, int) and e == 0 and k <= 2) else v)

    with nc.Block() as block:
        @block.sync
        def _(sp):
            def load(e, k, src, cols):
                dst = unit[k % NU][:, :].rearrange("p (k n) -> p k n", n=cols)
                if k >= NU or not (isinstance(e, int) and e == 0):
                    le, lk = (e, k - NU) if k >= NU else (e - 1, k + NU)
                    if lk % 3 == 2:
                        after(sp, s["down_mm"], NJ * le + lk // 3)
                    else:
                        sp.wait_ge(s[("gate_mm", "up_mm")[lk % 3]], NJ * le + lk // 3 + 1)
                sp.dma_start(dst, src).then_inc(unit_in[k % NU], 16)

            def expert(e, first):
                for j in range(NJ):
                    c = slice(j * UC, (j + 1) * UC)
                    load(e, 3 * j, w_gate[e][:, :, c], UC)
                    load(e, 3 * j + 1, w_up[e][:, :, c], UC)
                    if j > 0:
                        load(e, 3 * j + 2, w_down[e][:, 4 * (j - 1):4 * j, :], D)
                    elif not first:
                        load(e, 2, w_down[e - 1][:, 4 * (NJ - 1):4 * NJ, :], D)
            sp.dma_start(fgain[:, :], a["final_norm_g"].partition_broadcast(P)).then_inc(s["fg_in"], 16)
            expert(0, True)
            with sp.Fori(1, E) as e:
                expert(e, False)
            load(E, 0, w_down[E - 1][:, 4 * (NJ - 1):4 * NJ, :], D)
            sp.wait_ge(s["y_out"], 16 * E)
            for t in range(TL):
                if t >= NX:
                    sp.wait_ge(xa_out[t % NX], 16 * (t // NX))
                sp.dma_start(xa[t % NX][:, :], acc_d.rearrange("(t p) d -> t p d", p=P)[t]).then_inc(xa_in[t % NX], 16)

        @block.gpsimd
        def _(pool):
            pool.wait_ge(s["cols_done"], 2)

            pool.memset(carry[:, :], 0.0).then_inc(s["carried"], 1)

            def carrier(n):
                pool.wait_ge(s["carried"], n + 1)
                pool.tensor_tensor(carry[:, 1:2], carry[:, 0:1], carry[:, 0:1], ALU.add).then_inc(s["carried"], 1)

            def gather(e):
                after(pool, s["x_in"], 16 * e)
                pool.tensor_copy(idx_g[:, :], icol[:, bass.ds(e, 1)]).then_inc(s["idx_g"], 1)
                pool.wait_ge(s["idx_g"], e + 1)
                after(pool, s["x_mm"], 2 * e)
                carrier(2 * e - 1 if not (isinstance(e, int) and e == 0) else 0)
                pool.indirect_dma_start(out=xe[:, :], out_offset=None, in_=h2_d,
                                        in_offset=bass.IndirectOffsetOnAxis(ap=idx_g[:, 0:1], axis=0)).then_inc(s["x_in"], 16)

            def scatter(e):
                after(pool, s["y_out"], 16 * e)
                pool.tensor_copy(idx_s[:, :], icol[:, bass.ds(e, 1)])
                pool.tensor_copy(gate_s[:, :], gcol[:, bass.ds(e, 1)]).then_inc(s["sel_done"], 1)
                pool.wait_ge(s["sel_done"], e + 1)
                pool.wait_ge(s["y_done"], e + 1)
                carrier(2 * e + 2 if not (isinstance(e, int) and e == E - 1) else 2 * e + 1)
                pool.indirect_dma_start(out=acc_d, out_offset=bass.IndirectOffsetOnAxis(ap=idx_s[:, 0:1], axis=0),
                                        in_=ysc[:, :], in_offset=None, compute_op=ALU.add).then_inc(s["y_out"], 16)
            gather(0)
            gather(1)
            scatter(0)
            with pool.Fori(1, E - 1) as e:
                gather(e + 1)
                scatter(e)
            scatter(E - 1)
            for t in range(TL):
                pool.wait_ge(s["a_done"], t + 1)
                pool.tensor_tensor(fst[:, t, 1:2], fst[:, t, 0:1], eps_c[:, 1:2], ALU.add).then_inc(s["mean"], 1)
                pool.wait_ge(s["mean"], t + 1)
                pool.tensor_tensor(fst[:, t, 2:3], fst[:, t, 1:2], eps_c[:, 0:1], ALU.pow).then_inc(s["rstd"], 1)

        @block.scalar
        def _(act):
            def x_part(e):
                act.wait_ge(s["x_mm"], 2 * e + 1)
                after(act, s["up_mm"], NJ * e)
                act.activation(xet[:, 0:4, :].rearrange("p k n -> p (k n)"), psum[:, XB, :], ACT.Copy).then_inc(s["x_a"], 1)

            def gate(e, j):
                st = NJ * e + j
                act.wait_ge(s["gate_mm"], st + 1)
                if not (isinstance(e, int) and e == 0 and j < 2):
                    act.wait_ge(s["hid_done"], st - 1)
                act.activation(sil[j % 2][:, :], psum[:, 2 * (j % 2), :], ACT.Silu).then_inc(s["sil_done"], 1)

            def turn(e, j):
                st = NJ * e + j
                act.wait_ge(s["ht_mm"], st + 1)
                if not (isinstance(e, int) and e == 0 and j < 2):
                    act.wait_ge(s["down_mm"], st - 1)
                act.activation(hidt[j % 2][:, :, :].rearrange("p k n -> p (k n)"), psum[:, HB, :], ACT.Copy).then_inc(s["ht_done"], 1)

            def expert(e, first, last):
                for j in range(NJ):
                    gate(e, j)
                    if j > 0:
                        turn(e, j - 1)
                    elif not first:
                        turn(e - 1, NJ - 1)
                    if j == NJ - 1 and not last:
                        x_part(e + 1)
            x_part(0)
            expert(0, True, False)
            with act.Fori(1, E - 1) as e:
                expert(e, False, False)
            expert(E - 1, False, True)
            turn(E - 1, NJ - 1)

            def store(t):
                act.wait_ge(s["norm_done"], t + 1)
                act.dma_start(out_d[t], xa[t % NX][:, :]).then_inc(xa_out[t % NX], 16)
            for t in range(TL):
                act.wait_ge(xa_in[t % NX], 16 * (t // NX + 1))
                after(act, s["a_done"], t)
                act.activation(sqj[:, :], xa[t % NX][:, :], ACT.Square, accum_out=fst[:, t, 0:1]).then_inc(s["a_done"], 1)
                if t >= 1:
                    store(t - 1)
            store(TL - 1)
            for i in range(NX):
                act.wait_ge(xa_out[i], 16 * (TL // NX))

        @block.vector
        def _(dve):
            dve.wait_ge(s["fg_in"], 16)
            dve.tensor_scalar(fgain[:, :], fgain[:, :], ROOT, None, ALU.mult)
            for r in range(CAP // 8):
                v = slice(8 * r, 8 * r + 8)
                dve.max(top[:, v], aff[:, :]).then_inc(s["top_order"], 1)
                dve.wait_ge(s["top_order"], 2 * r + 1)
                dve.max_index(topi[:, v], top[:, v], aff[:, :])
                dve.match_replace(aff[:, :], top[:, v], aff[:, :], -1.0).then_inc(s["top_order"], 1)
                dve.wait_ge(s["top_order"], 2 * r + 2)
            dve.tensor_copy(topf[:, :], topi[:, :]).then_inc(s["top_done"], 1)
            dve.wait_ge(s["top_t"], 2)
            dve.tensor_copy(gcol[:, :], psum[:, 0, 0:E]).then_inc(s["cols_done"], 1)
            dve.tensor_copy(icol[:, :], psum[:, 1, 0:E]).then_inc(s["cols_done"], 1)

            def x_part(e):
                dve.wait_ge(s["x_mm"], 2 * e + 2)
                after(dve, s["up_mm"], NJ * e)
                dve.tensor_copy(xet[:, 4:8, :].rearrange("p k n -> p (k n)"), psum[:, XB, :]).then_inc(s["x_b"], 1)

            def hidden(e, j):
                st = NJ * e + j
                dve.wait_ge(s["sil_done"], st + 1)
                dve.wait_ge(s["up_mm"], st + 1)
                if not (isinstance(e, int) and e == 0 and j < 2):
                    dve.wait_ge(s["ht_mm"], st - 1)
                dve.tensor_tensor(hid[j % 2][:, :], sil[j % 2][:, :], psum[:, 2 * (j % 2) + 1, :], ALU.mult).then_inc(s["hid_done"], 1)

            def result(e):
                dve.wait_ge(s["down_mm"], NJ * (e + 1))
                dve.wait_ge(s["sel_done"], e + 1)
                after(dve, s["y_out"], 16 * e)
                dve.scalar_tensor_tensor(out=ysc[:, :], in0=psum[:, Y:Y + 2, :].rearrange("p a n -> p (a n)"), scalar=gate_s[:, 0:1],
                                         in1=rows[:, G2, :], op0=ALU.mult, op1=ALU.mult).then_inc(s["y_done"], 1)

            def expert(e, first, last):
                for j in range(NJ):
                    hidden(e, j)
                    if j == 0 and not first:
                        result(e - 1)
                    if j == NJ - 1 and not last:
                        x_part(e + 1)
            x_part(0)
            expert(0, True, False)
            with dve.Fori(1, E - 1) as e:
                expert(e, False, False)
            expert(E - 1, False, True)
            result(E - 1)
            for t in range(TL):
                dve.wait_ge(s["rstd"], t + 1)
                dve.scalar_tensor_tensor(out=xa[t % NX][:, :], in0=xa[t % NX][:, :], scalar=fst[:, t, 2:3], in1=fgain[:, :],
                                         op0=ALU.mult, op1=ALU.mult).then_inc(s["norm_done"], 1)

        @block.tensor
        def _(pe):
            pe.wait_ge(s["top_done"], 1)
            pe.transpose(psum[:, 0, 0:E], top[:, :], ident[0:E, 0:E]).then_inc(s["top_t"], 1)
            pe.transpose(psum[:, 1, 0:E], topf[:, :], ident[0:E, 0:E]).then_inc(s["top_t"], 1)

            def x_turn(e, half):
                if half == 0:
                    pe.wait_ge(s["x_in"], 16 * (e + 1))
                    after(pe, s["x_b"], e)
                else:
                    pe.wait_ge(s["x_a"], e + 1)
                for k in range(4):
                    i = pe.transpose(psum[:, XB, k * P:(k + 1) * P], xe[:, (4 * half + k) * P:(4 * half + k + 1) * P], ident[:, :])
                i.then_inc(s["x_mm"], 1)

            def project(e, j, which):
                k0 = 3 * j + which
                st = NJ * e + j
                pe.wait_ge(unit_in[k0 % NU], arrived(e, k0))
                if which == 0:
                    if j == 0:
                        pe.wait_ge(s["x_a"], e + 1)
                        pe.wait_ge(s["x_b"], e + 1)
                    if not (isinstance(e, int) and e == 0 and j < 2):
                        pe.wait_ge(s["sil_done"], st - 1)
                    elif j == 0:
                        pe.wait_ge(s["cols_done"], 2)
                elif not (isinstance(e, int) and e == 0 and j < 2):
                    pe.wait_ge(s["hid_done"], st - 1)
                u = unit[k0 % NU][:, :].rearrange("p (k n) -> p k n", n=UC)
                for k in range(KD):
                    i = pe.matmul(psum[:, 2 * (j % 2) + which, :], xet[:, k, :], u[:, k, :], start=(k == 0), stop=(k == KD - 1))
                i.then_inc(s["up_mm" if which else "gate_mm"], 1)

            def turn(e, j):
                st = NJ * e + j
                pe.wait_ge(s["hid_done"], st + 1)
                after(pe, s["ht_done"], st)
                for k in range(4):
                    i = pe.transpose(psum[:, HB, k * P:(k + 1) * P], hid[j % 2][:, k * P:(k + 1) * P], ident[:, :])
                i.then_inc(s["ht_mm"], 1)

            def down(e, j, en, kn, parts):
                st = NJ * e + j
                if 0 in parts:
                    pe.wait_ge(s["ht_done"], st + 1)
                    pe.wait_ge(unit_in[kn % NU], arrived(en, kn))
                    if j == 0:
                        after(pe, s["y_done"], e)
                u = unit[kn % NU][:, :].rearrange("p (k n) -> p k n", n=D)
                for h in parts:
                    for k in range(4):
                        i = pe.matmul(psum[:, Y + h, :], hidt[j % 2][:, k, :], u[:, k, h * 512:(h + 1) * 512],
                                      start=(j == 0 and k == 0), stop=(j == NJ - 1 and k == 3))
                if 1 in parts:
                    i.then_inc(s["down_mm"], 1)

            def expert(e, first, last):
                for j in range(NJ):
                    project(e, j, 0)
                    if j > 0:
                        turn(e, j - 1)
                    elif not first:
                        turn(e - 1, NJ - 1)
                    project(e, j, 1)
                    if j == NJ - 1 and not last:
                        x_turn(e + 1, 0)
                        down(e, j - 1, e, 3 * j + 2, (0,))
                        x_turn(e + 1, 1)
                        down(e, j - 1, e, 3 * j + 2, (1,))
                    elif j > 0:
                        down(e, j - 1, e, 3 * j + 2, (0, 1))
                    elif not first:
                        down(e - 1, NJ - 1, e, 2, (0, 1))
            x_turn(0, 0)
            x_turn(0, 1)
            expert(0, True, False)
            with pe.Fori(1, E - 1) as e:
                expert(e, False, False)
            expert(E - 1, False, True)
            turn(E - 1, NJ - 1)
            down(E - 1, NJ - 1, E, 0, (0, 1))

    M.close()


def kernel(**inputs):
    import concourse.bacc as bacc
    from concourse.bass_utils import run_bass_kernel_spmd

    nc = bacc.Bacc("TRN2", target_bir_lowering=False, num_devices=1)
    arrays, args = {}, {}
    for name, v in {**{n: inputs[n] for n in INPUTS}, **constants()}.items():
        v = np.ascontiguousarray(v)
        arrays[f"in_{name}"] = v
        args[name] = nc.dram_tensor(f"in_{name}", v.shape, mybir.dt.from_np(v.dtype), kind="ExternalInput").ap()
    out = nc.dram_tensor("out", (1, N, D), F32, kind="ExternalOutput").ap()
    build(nc, args, out)
    return run_bass_kernel_spmd(nc, [arrays], core_ids=[0]).results[0]["out"]
```

```python
from contextlib import ExitStack

import numpy as np

import concourse.bass as bass
from concourse import mybir

P = 128
D = 1024
N = 1024
L = 256
HD = 64
NQ, NKV = 12, 4
REP = NQ // NKV
FG, FD = 4, 64
FW = FG * FD
QW, KW = NQ * HD, NKV * HD
IN = FW + QW + 2 * KW
QK = QW + KW
NH = NQ + NKV
E = 16
DE = 2048
CAP = 2 * N // E
GRID = 64
EPS = 1e-6
ROOT = float(D) ** 0.5
KD = D // P
TL, TC = N // P, L // P
TS = TL + TC
KEYS = N + L
HALF = N // 2 + 1
UC = 512
UM = 256
SCALE = HD ** -0.5 * HD

F32 = mybir.dt.float32
F32R = mybir.dt.float32r
U32 = mybir.dt.uint32
ALU = mybir.AluOpType
ACT = mybir.ActivationFunctionType
AX = mybir.AxisListType.X


INPUTS = ["x", "c", "ctx", "c_ctx", "w_mod", "b_mod", "norm_mix_g", "norm_ffn_g", "w_in", "w_four",
          "q_norm_g", "k_norm_g", "w_out", "w_router", "w_gate", "w_up", "w_down", "final_norm_g"]


def constants():
    n, m = np.arange(N)[:, None], np.arange(HALF)[None, :]
    turn = 2 * np.pi * ((n * m) % N) / N
    dft = np.stack([np.cos(turn), np.sin(turn)]).astype(np.float32)
    a = 2 * np.pi * np.outer(np.arange(FD), np.arange(FD)) / FD
    scale = 1 / np.sqrt(N * FD)
    two = np.eye(P // FD)
    chan = np.stack([np.kron(two, np.cos(a) * scale), np.kron(two, -np.sin(a) * scale),
                     np.kron(two, np.sin(a) * scale)]).astype(np.float32)
    half = HD // 4
    freqs = (10000.0 ** (-np.arange(half, dtype=np.float32) / np.float32(half))).astype(np.float32)
    pos = np.arange(N)
    ang = [np.float32(p)[:, None] * freqs[None] for p in (pos // GRID, pos % GRID)]
    cos = np.concatenate([f(x.astype(np.float32)) for x in ang for f in (np.cos, np.cos)], 1)
    sin = np.concatenate([s * np.sin(x.astype(np.float32)) for x in ang for s in (-1, 1)], 1)
    rope = np.stack([cos, sin]).astype(np.float32)
    return {"dft": dft, "chan": chan, "rope": rope}


def build(nc, a, out):
    ctx = ExitStack()

    def dram(name, shape, dt):
        return nc.dram_tensor(name, shape, dt, kind="Internal").ap()

    def sem(name):
        return ctx.enter_context(nc.semaphore(name))

    def sb(name, shape, dt=F32, where=ctx):
        return where.enter_context(nc.sbuf_tensor(name, shape, dt))

    x_d = a["x"].rearrange("b (t p) d -> (b t) p d", p=P)
    ctx_d = a["ctx"].rearrange("b (t p) d -> (b t) p d", p=P)
    out_d = out.rearrange("b (t p) d -> (b t) p d", p=P)
    w_mod = a["w_mod"][0].rearrange("(k p) n -> p k n", p=P)
    w_in = a["w_in"][0].rearrange("(k p) n -> p k n", p=P)
    w_gate = a["w_gate"][0].rearrange("e (k p) f -> e p k f", p=P)
    w_up = a["w_up"][0].rearrange("e (k p) f -> e p k f", p=P)
    w_down = a["w_down"][0].rearrange("e (k p) d -> e p k d", p=P)

    def row(v):
        return v.partition_broadcast(P)

    q_d = dram("q_scratch", [TL, P, NQ * 2 * P], F32)
    h2_d = dram("h2_scratch", [N, D], F32)
    acc_d = dram("acc_scratch", [N, D], F32)

    with ctx:
        psum = ctx.enter_context(nc.psum_tensor("banks", [P, 8, 512], F32))

        ident = sb("ident", [P, P])
        ones = sb("ones", [P, P])
        rows = sb("rows", [P, 4, D])
        G1, SH2, SC2, G2 = range(4)
        aff = sb("aff", [E, N])
        eps_c = sb("eps_c", [P, 2])
        K = ExitStack()
        ks = sb("ks", [P, NKV, KEYS], F32R, K)
        vs = sb("vs", [P, TS, NKV, 2, HD], F32R, K)
        f_tok = sb("f_tok", [P, TL, FW], F32, K)
        y_t = sb("y_t", [P, 2, N], F32, K)

        A = ExitStack()
        unit = [sb(f"unit{i}", [P, KD, UM], F32, A) for i in range(2)]
        win = sb("win", [P, KD, IN], F32, A)
        vec = sb("vec", [5 * KD, P], F32, A)
        c_sig = sb("c_sig", [P, KD, 2], F32, A)
        bg_col = sb("bg_col", [P, 3 * KD], F32, A)
        bm_col, g_col = bg_col[:, 0:2 * KD], bg_col[:, 2 * KD:3 * KD]
        mod_col = sb("mod_col", [P, 2, 2, KD], F32, A)
        xt = sb("xt", [P, D], F32, A)
        xn = sb("xn", [P, D], F32, A)
        junk = sb("junk", [P, D], mybir.dt.bfloat16, A)
        ht = [sb(f"ht{i}", [P, KD, P], F32, A) for i in range(2)]
        stat = sb("stat", [P, 4], F32, A)
        prj = sb("prj", [P, IN], F32, A)
        g_qk = sb("g_qk", [P, 2, HD], F32, A)
        rope = sb("rope", [P, 2, TL, HD], F32, A)
        sq = sb("sq", [P, QK], F32, A)
        ss = sb("ss", [P, 4, NH], F32, A)
        qkn = sb("qkn", [P, QK], F32, A)
        rot = sq
        c_wide = xt[:, :].rearrange("p (k n) -> p k n", n=P)
        hlq = sb("hlq", [P, NQ, 2, 2, HD], F32R, A)
        hlk = sb("hlk", [P, NKV, 2, HD], F32R, A)
        qst = sb("qst", [P, NQ, 2, P], F32, A)
        c_rows = qst[0:2, :, :, :].rearrange("p h a n -> p (h a n)")
        row_unit = [unit[i][:, :, :] for i in range(2)] + [win[:, :, i * UM:(i + 1) * UM] for i in range(6)]

        s = {n: sem(n) for n in (
            "ident_done", "f_done", "small_in", "tables_in", "vec_t", "silu_done", "wide_done", "c_row_done", "c_col_done", "cols_done",
            "win_in", "x_in", "ss_done", "rstd_done", "xn_done", "xT_done", "hTa", "hTb", "proj_done",
            "prj_done", "pool_qk", "ss16_done", "rstd16_done", "hl_done", "pool_v", "v_done", "qkt_done",
            "qkt_act", "qkt_dve", "q_out", "row_mm", "row_done", "unit_used", "norm_row_in",
            "mean_done", "dve_order", "pool_order", "eps_done")}
        unit_in = [sem(f"unit_in{i}") for i in range(2)]
        row_in = [sem(f"row_in{i}") for i in range(8)]
        NC_UNITS, NR_UNITS = 2 * D // UM, 4 * D // UM

        def pipeline(eng, stages):
            def step(s_, par):
                for stage, ahead in stages:
                    n = s_ + ahead
                    if not isinstance(n, int):
                        stage(n, (par + ahead) % 2, "lat")
                    elif 0 <= n < TS:
                        stage(n, n % 2, "ctx" if n < TC else "lat")
            for s_ in range(-2, 4):
                step(s_, s_ % 2)
            with eng.Fori(0, (TS - 6) // 2) as pair:
                step(2 * pair + 4, 0)
                step(2 * pair + 5, 1)
            for s_ in range(TS - 2, TS + 2):
                step(s_, s_ % 2)

        def after(eng, sem_, v):
            if not (isinstance(v, int) and v <= 0):
                eng.wait_ge(sem_, v)

        XT, PJ, QT = 0, 2, 5
        ROW_BANKS = (0, 1, 7, 2, 3, 4)
        EARLY = 5
        QTG = 7

        with nc.Block() as block:

            @block.sync
            def _(sp):
                for r, v in ((0, a["c"].rearrange("b (k p) -> (b k) p", p=P)), (KD, a["c_ctx"].rearrange("(k p) -> k p", p=P)),
                             (2 * KD, a["b_mod"][0][0:2 * D].rearrange("(k p) -> k p", p=P)),
                             (4 * KD, a["norm_mix_g"][0].rearrange("(k p) -> k p", p=P))):
                    sp.dma_start(vec[r:r + v.shape[0], :], v).then_inc(s["small_in"], 16)
                sp.dma_start(xt[:, :], ctx_d[0]).then_inc(s["x_in"], 16)
                for u in range(NC_UNITS):
                    if u >= 2:
                        sp.wait_ge(s["unit_used"], u - 1)
                    sp.dma_start(unit[u % 2][:, :, :], w_mod[:, :, u * UM:(u + 1) * UM]).then_inc(unit_in[u % 2], 16)
                for c in (2, 1, 0):
                    sp.dma_start(win[:, :, c * 512:(c + 1) * 512], w_in[:, :, c * 512:(c + 1) * 512]).then_inc(s["win_in"], 16)
                    if c == 2:
                        sp.dma_start(g_qk[:, 0, :], row(a["q_norm_g"][0])).then_inc(s["tables_in"], 16)
                        sp.dma_start(g_qk[:, 1, :], row(a["k_norm_g"][0])).then_inc(s["tables_in"], 16)
                        sp.dma_start(rope[:, :, :, :], a["rope"].rearrange("a (t p) d -> p a t d", p=P)).then_inc(s["q_out"], 16)

                def mod_unit(u):
                    sp.dma_start(row_unit[u % 8], w_mod[:, :, (NC_UNITS + u) * UM:(NC_UNITS + u + 1) * UM]).then_inc(row_in[u % 8], 16)

                def prep(n, par, kind):
                    if isinstance(n, int) and n == 0:
                        return
                    src = ctx_d[n] if kind == "ctx" else x_d[n - TC]
                    sp.wait_ge(s["xn_done"], n)
                    sp.dma_start(xt[:, :], src).then_inc(s["x_in"], 16)
                    if isinstance(n, int) and n == TC + 1:
                        sp.dma_start(rows[:, :, :].rearrange("p a d -> p (a d)"), row(a["b_mod"][0][2 * D:6 * D])).then_inc(s["norm_row_in"], 16)
                        sp.wait_ge(s["unit_used"], NC_UNITS)
                        mod_unit(0)
                        mod_unit(1)

                def three(n, par, kind):
                    if kind == "lat":
                        dst, count = q_d[n - TC], (n + 1) * 4
                        sp.wait_ge(s["qkt_act"], count)
                        sp.wait_ge(s["qkt_dve"], count)
                        sp.dma_start(dst, qst[:, :, :, :].rearrange("p h a n -> p (h a n)")).then_inc(s["q_out"], 16)
                    if isinstance(n, int) and n == TS - 2:
                        sp.wait_ge(s["proj_done"], TS)
                        for u in range(2, 8):
                            mod_unit(u)
                        sp.wait_ge(s["xT_done"], 2 * TS)
                        sp.dma_start(xn[:, :], row(a["norm_ffn_g"][0])).then_inc(s["norm_row_in"], 16)

                pipeline(sp, ((prep, 2), (three, -2)))
                for u in range(8, NR_UNITS):
                    sp.wait_ge(s["row_mm"], u - 7)
                    mod_unit(u)
                sp.wait_ge(s["q_out"], 16 * (TL + 1))

            @block.gpsimd
            def _(pool):
                pool.memset(ident[:, :], 0.0).then_inc(s["pool_order"], 1)
                pool.memset(ones[:, :], 1.0)
                pool.memset(eps_c[:, 0:1], -0.5)
                pool.memset(eps_c[:, 1:2], EPS * D)
                pool.wait_ge(s["pool_order"], 1)
                pool.affine_select(out=ident[:, :], in_=ident[:, :], compare_op=ALU.not_equal, fill=1.0,
                                   base=0, pattern=[[-1, P]], channel_multiplier=1).then_inc(s["ident_done"], 1)
                pool.memset(ss[:, 2, :], -0.5)
                pool.memset(ss[:, 3, :], EPS * HD).then_inc(s["eps_done"], 1)
                pool.wait_ge(s["eps_done"], 1)

                def prep(n, par, kind):
                    pool.wait_ge(s["ss_done"], n + 1)
                    after(pool, s["xn_done"], n)
                    pool.tensor_tensor(stat[:, 1:2], stat[:, 0:1], eps_c[:, 1:2], ALU.add).then_inc(s["mean_done"], 1)
                    pool.wait_ge(s["mean_done"], n + 1)
                    pool.tensor_tensor(stat[:, 2:3], stat[:, 1:2], eps_c[:, 0:1], ALU.pow).then_inc(s["rstd_done"], 1)

                def norm(n, par, kind):
                    c0 = 0 if kind == "lat" else QW
                    h0 = c0 // HD
                    pool.wait_ge(s["prj_done"], n + 1)
                    after(pool, s["hl_done"], n)
                    pool.tensor_tensor(sq[:, c0:QK], prj[:, FW + c0:FW + QK], prj[:, FW + c0:FW + QK], ALU.mult).then_inc(s["pool_qk"], 1)
                    pool.tensor_copy(vs[:, n, :, 0, :], prj[:, FW + QK:IN].rearrange("p (h d) -> p h d", d=HD)).then_inc(s["pool_v"], 1)
                    if kind == "lat":
                        pool.tensor_copy(f_tok[:, n - TC, :], prj[:, 0:FW]).then_inc(s["f_done"], 1)
                    pool.wait_ge(s["ss16_done"], n + 1)
                    after(pool, s["hl_done"], n)
                    pool.tensor_tensor(ss[:, 1, h0:NH], ss[:, 0, h0:NH], ss[:, 3, h0:NH], ALU.add).then_inc(s["eps_done"], 1)
                    pool.wait_ge(s["eps_done"], n + 2)
                    pool.tensor_tensor(ss[:, 0, h0:NH], ss[:, 1, h0:NH], ss[:, 2, h0:NH], ALU.pow).then_inc(s["rstd16_done"], 1)

                pipeline(pool, ((norm, -1), (prep, 2)))

            @block.scalar
            def _(act):
                act.wait_ge(s["vec_t"], 1)
                act.activation(c_sig[:, :, :].rearrange("p k j -> p j k"),
                               psum[:, 6, 0:2 * KD].rearrange("p (j k) -> p j k", k=KD), ACT.Silu).then_inc(s["silu_done"], 1)
                for u in range(NC_UNITS):
                    act.wait_ge(s["unit_used"], u + 1)
                    act.activation(c_rows[:, u * UM:(u + 1) * UM], psum[0:2, u % 2, 0:UM], ACT.Copy).then_inc(s["c_row_done"], 1)

                def prep(n, par, kind):
                    act.wait_ge(s["x_in"], 16 * (n + 1))
                    after(act, s["rstd_done"], n)
                    act.activation(junk[:, :], xt[:, :], ACT.Square, accum_out=stat[:, 0:1]).then_inc(s["ss_done"], 1)

                def turn(n, par, kind):
                    act.wait_ge(s["xT_done"], 2 * n + 1)
                    after(act, s["proj_done"], n - 1)
                    if isinstance(n, int) and n == 0:
                        act.wait_ge(s["cols_done"], 2)
                    j = 1 if kind == "ctx" else 0
                    for k in range(KD // 2):
                        i = act.activation(ht[par][:, k, :], psum[:, XT, k * P:(k + 1) * P], ACT.Identity,
                                           scale=mod_col[:, 0, j, k:k + 1], bias=mod_col[:, 1, j, k:k + 1])
                    i.then_inc(s["hTa"], 1)

                def two(n, par, kind):
                    act.wait_ge(s["proj_done"], n + 1)
                    c0 = 0 if kind == "lat" else FW + QW
                    after(act, s["pool_v"], n)
                    after(act, s["v_done"], n)
                    if not isinstance(n, int) or n > TC:
                        act.wait_ge(s["f_done"], n - TC)
                    pj = psum[:, PJ:PJ + 3, :].rearrange("p a n -> p (a n)")
                    act.activation(prj[:, c0:IN], pj[:, c0:IN], ACT.Copy).then_inc(s["prj_done"], 1)

                def three(n, par, kind):
                    base = (n - TC) * QTG + TC
                    if kind == "ctx":
                        act.wait_ge(s["qkt_done"], n + 1)
                        act.activation(ks[:, 0:2, bass.ds(n * P, P)],
                                       psum[:, QT, 0:2 * P].rearrange("p (h n) -> p h n", n=P), ACT.Copy).then_inc(s["qkt_act"], 4)
                        return
                    act.wait_ge(s["q_out"], (n - TC + 1) * 16)
                    for j in range(0, QTG, 2):
                        act.wait_ge(s["qkt_done"], base + j + 1)
                        src = psum[:, QT, :].rearrange("p (h n) -> p h n", n=P)
                        dst = ks[:, :, bass.ds(n * P, P)] if j == 0 else \
                            qst[:, 2 * (j - 1):2 * j, :, :].rearrange("p h a n -> p (h a) n")
                        act.activation(dst, src, ACT.Copy).then_inc(s["qkt_act"], 1)

                pipeline(act, ((three, -2), (turn, 1), (prep, 2), (two, 0)))

            @block.vector
            def _(dve):
                order = [0]

                def link(ins):
                    order[0] += 1
                    ins.then_inc(s["dve_order"], 1)
                    dve.wait_ge(s["dve_order"], order[0])

                dve.wait_ge(s["silu_done"], 1)
                link(dve.tensor_copy(bg_col[:, :], psum[:, 6, 2 * KD:5 * KD]))
                dve.wait_ge(s["c_col_done"], 1)
                cols = psum[:, 7, 0:4 * KD].rearrange("p (m k j) -> p m j k", k=KD, j=2)
                for j in range(2):
                    dve.tensor_tensor(mod_col[:, 1, j, :], cols[:, 0, j, :], bg_col[:, 0:KD], ALU.add)
                    link(dve.tensor_tensor(mod_col[:, 0, j, :], cols[:, 1, j, :], bg_col[:, KD:2 * KD], ALU.add))
                    i = dve.scalar_tensor_tensor(out=mod_col[:, 0, j, :], in0=mod_col[:, 0, j, :], scalar=1.0,
                                                 in1=g_col, op0=ALU.add, op1=ALU.mult)
                    i.then_inc(s["cols_done"], 1)
                dve.wait_ge(s["cols_done"], 2)
                first_order = order[0]
                CH = {"lat": 5, "ctx": 2}

                def prep(n, par, kind):
                    dve.wait_ge(s["rstd_done"], n + 1)
                    after(dve, s["xT_done"], 2 * n)
                    dve.tensor_scalar(xn[:, :], xt[:, :], stat[:, 2:3], ROOT, ALU.mult, ALU.mult).then_inc(s["xn_done"], 1)

                def turn(n, par, kind):
                    dve.wait_ge(s["xT_done"], 2 * n + 2)
                    after(dve, s["proj_done"], n - 1)
                    j = 1 if kind == "ctx" else 0
                    for k in range(KD // 2, KD):
                        i = dve.tensor_scalar(ht[par][:, k, :], psum[:, XT + 1, (k - KD // 2) * P:(k - KD // 2 + 1) * P],
                                              mod_col[:, 0, j, k:k + 1], mod_col[:, 1, j, k:k + 1], ALU.mult, ALU.add)
                    i.then_inc(s["hTb"], 1)

                def norm(n, par, kind):
                    if isinstance(n, int) and n == 0:
                        dve.wait_ge(s["tables_in"], 16 * 2)
                        dve.wait_ge(s["q_out"], 16)
                    if isinstance(n, int) and n == TS - 2:
                        dve.wait_ge(s["xn_done"], TS)
                        dve.tensor_copy(c_wide, c_sig[:, :, 0:1].broadcast_to([P, KD, P])).then_inc(s["wide_done"], 1)
                    c0 = 0 if kind == "lat" else QW
                    h0 = c0 // HD
                    nh = NH - h0
                    if kind == "ctx":
                        base = first_order + n * CH["ctx"]
                    else:
                        base = first_order + TC * CH["ctx"] + (n - TC) * CH["lat"]
                    count = [0]

                    def chain(ins):
                        count[0] += 1
                        ins.then_inc(s["dve_order"], 1)
                        dve.wait_ge(s["dve_order"], base + count[0])

                    def hv(ap):
                        return ap.rearrange("p (h d) -> p h d", d=HD)
                    dve.wait_ge(s["prj_done"], n + 1)
                    dve.wait_ge(s["pool_v"], n + 1)
                    dve.tensor_tensor(vs[:, n, :, 1, :], hv(prj[:, FW + QK:IN]), vs[:, n, :, 0, :].bitcast(F32), ALU.subtract)
                    if kind == "lat":
                        dve.tensor_tensor(hv(qkn[:, 0:QW]), hv(prj[:, FW:FW + QW]),
                                          g_qk[:, 0, :].unsqueeze(1).broadcast_to([P, NQ, HD]), ALU.mult)
                    dve.tensor_tensor(hv(qkn[:, QW:QK]), hv(prj[:, FW + QW:FW + QK]),
                                      g_qk[:, 1, :].unsqueeze(1).broadcast_to([P, NKV, HD]), ALU.mult).then_inc(s["v_done"], 1)
                    dve.wait_ge(s["pool_qk"], n + 1)
                    dve.tensor_reduce(ss[:, 0, h0:NH], hv(sq[:, c0:QK]), AX, ALU.add).then_inc(s["ss16_done"], 1)
                    dve.wait_ge(s["rstd16_done"], n + 1)
                    chain(dve.tensor_tensor(hv(qkn[:, c0:QK]), hv(qkn[:, c0:QK]),
                                            ss[:, 0, h0:NH].unsqueeze(2).broadcast_to([P, nh, HD]), ALU.mult))
                    v = qkn
                    if kind == "lat":
                        t = n - TC
                        q5 = qkn[:, :].rearrange("p (h g s d) -> p h g s d", g=2, s=2, d=HD // 4)
                        r5 = rot[:, :].rearrange("p (h g s d) -> p h g s d", g=2, s=2, d=HD // 4)
                        for half in range(2):
                            tab = rope[:, 1, t, :].rearrange("p (g s d) -> p g s d", g=2, s=2)[:, :, half, :]
                            i = dve.tensor_tensor(r5[:, :, :, half, :], q5[:, :, :, 1 - half, :],
                                                  tab.unsqueeze(1).broadcast_to([P, NH, 2, HD // 4]), ALU.mult)
                        chain(i)
                        chain(dve.tensor_tensor(hv(qkn[:, :]), hv(qkn[:, :]),
                                                rope[:, 0, t, :].unsqueeze(1).broadcast_to([P, NH, HD]), ALU.mult))
                        chain(dve.tensor_tensor(rot[:, :], rot[:, :], qkn[:, :], ALU.add))
                        v = rot
                    if kind == "ctx":
                        after(dve, s["qkt_done"], n)
                    else:
                        after(dve, s["qkt_done"], (n - TC) * QTG + TC)
                    if kind == "lat":
                        vq = hv(v[:, 0:QW]).unsqueeze(2).broadcast_to([P, NQ, 2, HD])
                        dve.tensor_copy(hlq[:, :, 0, :, :], vq)
                    chain(dve.tensor_copy(hlk[:, :, 0, :], hv(v[:, QW:QK])))
                    if kind == "lat":
                        dve.tensor_tensor(hlq[:, :, 1, :, :], vq, hlq[:, :, 0, :, :].bitcast(F32), ALU.subtract)
                    dve.tensor_tensor(hlk[:, :, 1, :], hv(v[:, QW:QK]), hlk[:, :, 0, :].bitcast(F32), ALU.subtract).then_inc(s["hl_done"], 1)
                    assert count[0] == CH[kind]

                def three(n, par, kind):
                    base = (n - TC) * QTG + TC
                    if kind == "ctx":
                        dve.wait_ge(s["qkt_done"], n + 1)
                        dve.tensor_copy(ks[:, 2:4, bass.ds(n * P, P)],
                                        psum[:, QT + 1, 0:2 * P].rearrange("p (h n) -> p h n", n=P)).then_inc(s["qkt_dve"], 4)
                        return
                    dve.wait_ge(s["q_out"], (n - TC + 1) * 16)
                    for j in range(1, QTG, 2):
                        dve.wait_ge(s["qkt_done"], base + j + 1)
                        dve.tensor_copy(qst[:, 2 * (j - 1):2 * j, :, :].rearrange("p h a n -> p (h a n)"),
                                        psum[:, QT + 1, :]).then_inc(s["qkt_dve"], 2 if j == QTG - 2 else 1)

                pipeline(dve, ((three, -2), (turn, 1), (norm, -1), (prep, 2)))
                dve.wait_ge(s["norm_row_in"], 32)
                end = first_order + TC * CH["ctx"] + TL * CH["lat"]
                order[0] = end
                for u in range(NR_UNITS):
                    r = rows[:, u * UM // D, u * UM % D:u * UM % D + UM]
                    dve.wait_ge(s["row_mm"], u + 1)
                    i = dve.tensor_tensor(r, psum[:, ROW_BANKS[u % 6], 0:UM], r, ALU.add).then_inc(s["row_done"], 1)
                dve.wait_ge(s["row_done"], NR_UNITS)
                dve.scalar_tensor_tensor(out=rows[:, SC2, :], in0=rows[:, SC2, :], scalar=1.0, in1=xn[:, :],
                                         op0=ALU.add, op1=ALU.mult).then_inc(s["row_done"], 1)
                dve.wait_ge(s["row_done"], NR_UNITS + 1)
                dve.tensor_scalar(rows[:, SC2, :], rows[:, SC2, :], ROOT, None, ALU.mult)

            @block.tensor
            def _(pe):
                pe.wait_ge(s["ident_done"], 1)
                pe.wait_ge(s["small_in"], 16 * 4)
                pe.transpose(psum[:, 6, 0:5 * KD], vec[:, :], ident[0:5 * KD, 0:5 * KD]).then_inc(s["vec_t"], 1)
                pe.wait_ge(s["silu_done"], 1)
                for u in range(NC_UNITS):
                    pe.wait_ge(unit_in[u % 2], 16 * (u // 2 + 1))
                    if u >= 2:
                        pe.wait_ge(s["c_row_done"], u - 1)
                    for k in range(KD):
                        i = pe.matmul(psum[0:2, u % 2, 0:UM], c_sig[:, k, :], unit[u % 2][:, k, :],
                                      start=(k == 0), stop=(k == KD - 1))
                    i.then_inc(s["unit_used"], 1)
                pe.wait_ge(s["c_row_done"], NC_UNITS)
                for b in range(2 * KD):
                    i = pe.transpose(psum[:, 7, 2 * b:2 * b + 2], c_rows[:, b * P:(b + 1) * P], ident[0:2, 0:2])
                i.then_inc(s["c_col_done"], 1)

                def turn(n, par, kind):
                    pe.wait_ge(s["xn_done"], n + 1)
                    after(pe, s["hTa"], n)
                    after(pe, s["hTb"], n)
                    for k in range(KD):
                        i = pe.transpose(psum[:, XT + k // 4, (k % 4) * P:(k % 4 + 1) * P], xn[:, k * P:(k + 1) * P], ident[:, :])
                        if k % 4 == 3:
                            i.then_inc(s["xT_done"], 1)

                def two(n, par, kind):
                    pe.wait_ge(s["hTa"], n + 1)
                    pe.wait_ge(s["hTb"], n + 1)
                    if isinstance(n, int) and n in (0, TC):
                        pe.wait_ge(s["win_in"], 16 if n == 0 else 48)
                    after(pe, s["prj_done"], n)
                    for c in ((1, 0, 2) if kind == "lat" else (2,)):
                        for k in range(KD):
                            i = pe.matmul(psum[:, PJ + c, :], ht[par][:, k, :], win[:, k, c * 512:(c + 1) * 512],
                                          start=(k == 0), stop=(k == KD - 1))
                    i.then_inc(s["proj_done"], 1)

                def mod_row(u):
                    if u == 0:
                        pe.wait_ge(s["wide_done"], 1)
                        pe.wait_ge(s["hTa"], TS)
                        pe.wait_ge(s["hTb"], TS)
                    if u == 3:
                        pe.wait_ge(s["prj_done"], TS)
                    pe.wait_ge(row_in[u % 8], 16 * (u // 8 + 1))
                    if u >= 6:
                        pe.wait_ge(s["row_done"], u - 5)
                    for k in range(KD):
                        i = pe.matmul(psum[:, ROW_BANKS[u % 6], 0:UM], c_wide[:, k, :], row_unit[u % 8][:, k, :],
                                      start=(k == 0), stop=(k == KD - 1))
                    i.then_inc(s["row_mm"], 1)

                def three(n, par, kind):
                    if isinstance(n, int) and n == TS - 1:
                        for u in range(EARLY):
                            mod_row(u)
                    pe.wait_ge(s["hl_done"], n + 1)
                    q32 = hlq[:, :, :, :, :].rearrange("p h a b d -> p (h a b d)").bitcast(F32)
                    k32 = hlk[:, :, :, :].rearrange("p h a d -> p (h a d)").bitcast(F32)
                    for j in range(QTG if kind == "lat" else 1):
                        if j == 0:
                            after(pe, s["qkt_act"], n * 4)
                            after(pe, s["qkt_dve"], n * 4)
                        elif j % 2 == 0:
                            pe.wait_ge(s["qkt_act"], n * 4 + j // 2)
                        elif j > 1:
                            pe.wait_ge(s["qkt_dve"], n * 4 + j // 2)
                        for b in range(4):
                            if j == 0:
                                src = k32[:, b * P:(b + 1) * P]
                            else:
                                src = q32[:, (4 * (j - 1) + b) * P:(4 * (j - 1) + b + 1) * P]
                            bank, col = (QT + b // 2, b % 2) if kind == "ctx" else (QT + j % 2, b)
                            i = pe.transpose(psum[:, bank, col * P:(col + 1) * P], src, ident[:, :])
                        i.then_inc(s["qkt_done"], 1)

                pipeline(pe, ((three, -2), (turn, 1), (two, 0)))
                for u in range(EARLY, NR_UNITS):
                    mod_row(u)
        A.close()
        nc_phase_b(nc, ctx, sem, sb, a, K, psum, ident, ones, rows, aff, eps_c, ks, vs, f_tok, y_t,
                   q_d, h2_d, acc_d, x_d)
        K.close()
        nc_phase_m(nc, ctx, sem, sb, a, psum, ident, rows, aff, eps_c, h2_d, acc_d, w_gate, w_up, w_down, out_d)


def after(eng, sem_, v):
    if not (isinstance(v, int) and v <= 0):
        eng.wait_ge(sem_, v)


def nc_phase_b(nc, ctx, sem, sb, a, K, psum, ident, ones, rows, aff, eps_c, ks, vs, f_tok, y_t,
               q_d, h2_d, acc_d, x_d):
    G1, SH2, SC2, G2 = range(4)

    F = ExitStack()
    dft = sb("dft", [P, 2, TL, HALF + 1], F32, F)
    chan = sb("chan", [P, 3, P], F32, F)
    wf = sb("wf", [P, 2, P], F32, F)
    ab = sb("ab", [P, 2, 3, P], F32, F)
    gt = sb("gt", [P, 2, 2, HALF + 1], F32, F)
    s = {n: sem("f_" + n) for n in ("wf_zero", "chan_in", "dft_in", "ab_mm", "ab_done", "g_mm", "g_done", "y_mm", "y_done")}
    with nc.Block() as block:
        @block.sync
        def _(sp):
            for i in range(2):
                for h in range(4):
                    sp.dma_start(dft[:, i, 2 * h:2 * h + 2, 0:HALF],
                                 a["dft"][i].rearrange("(t p) m -> p t m", p=P)[:, 2 * h:2 * h + 2, :]).then_inc(s["dft_in"], 16)
            sp.dma_start(chan[:, :, :], a["chan"].rearrange("a p n -> p a n")).then_inc(s["chan_in"], 16)
            sp.wait_ge(s["wf_zero"], 1)
            for g in range(FG):
                h = g % 2
                sp.dma_start(wf[h * FD:(h + 1) * FD, g // 2, h * FD:(h + 1) * FD], a["w_four"][0, g]).then_inc(s["chan_in"], 16)

        @block.vector
        def _(dve):
            dve.memset(wf[:, :, :], 0.0).then_inc(s["wf_zero"], 1)
            for c in range(2):
                dve.wait_ge(s["ab_mm"], c + 1)
                dve.tensor_copy(ab[:, c, :, :].rearrange("p a n -> p (a n)"), psum[:, 4 + c, 0:3 * P]).then_inc(s["ab_done"], 1)
            dve.wait_ge(s["g_mm"], 4)
            dve.tensor_copy(gt[:, :, :, HALF - 1], psum[:, 6, 0:4].rearrange("p (c i) -> p c i", i=2)).then_inc(s["g_done"], 1)
            for c in range(2):
                dve.wait_ge(s["y_mm"], 3 * c + 2)
                dve.tensor_copy(y_t[:, c, N - 1:HALF - 1:-1], psum[:, 2 * c + 1, 0:HALF - 2]).then_inc(s["y_done"], 1)
            dve.wait_ge(s["y_mm"], 6)
            dve.tensor_copy(y_t[:, :, HALF - 1], psum[:, 7, 0:2]).then_inc(s["y_done"], 1)

        @block.scalar
        def _(act):
            for c in range(2):
                for i in range(2):
                    act.wait_ge(s["g_mm"], 2 * c + i + 1)
                    act.activation(gt[:, c, i, 0:HALF - 1], psum[:, 2 * c + i, :], ACT.Copy).then_inc(s["g_done"], 1)
            for c in range(2):
                act.wait_ge(s["y_mm"], 3 * c + 1)
                act.activation(y_t[:, c, 0:HALF - 1], psum[:, 2 * c, :], ACT.Copy).then_inc(s["y_done"], 1)

        @block.tensor
        def _(pe):
            pe.wait_ge(s["chan_in"], 16 * 5)
            for c in range(2):
                for j in range(3):
                    i = pe.matmul(psum[:, 4 + c, j * P:(j + 1) * P], chan[:, j, :], wf[:, c, :], start=True, stop=True)
                i.then_inc(s["ab_mm"], 1)
            pe.wait_ge(s["dft_in"], 16 * 8)
            for c in range(2):
                for i in range(2):
                    for t in range(TL):
                        pe.matmul(psum[:, 2 * c + i, :], f_tok[:, t, c * P:(c + 1) * P], dft[:, i, t, 0:512],
                                  start=(t == 0), stop=(t == TL - 1))
                    for t in range(TL):
                        m = pe.matmul(psum[:, 6, 2 * c + i:2 * c + i + 1], f_tok[:, t, c * P:(c + 1) * P], dft[:, i, t, 512:513],
                                      start=(t == 0), stop=(t == TL - 1))
                    m.then_inc(s["g_mm"], 1)
            pe.wait_ge(s["ab_done"], 2)
            pe.wait_ge(s["g_done"], 5)
            for c in range(2):
                for (bank, lo, hi, b) in ((2 * c, 0, 512, 1), (2 * c + 1, 1, 512, 2), (7, 512, 513, 1)):
                    o = psum[:, bank, 0:hi - lo] if bank < 7 else psum[:, 7, c:c + 1]
                    pe.matmul(o, ab[:, c, 0, :], gt[:, c, 0, lo:hi], start=True, stop=False)
                    pe.matmul(o, ab[:, c, b, :], gt[:, c, 1, lo:hi], start=False, stop=True).then_inc(s["y_mm"], 1)
    F.close()

    B = ExitStack()
    wout = sb("wout", [P, KD, D], F32, B)
    wrt = sb("wrt", [P, KD, E], F32, B)
    qt = sb("qt", [P, NQ, 2, P], F32R, B)
    pr = [sb(f"pr{i}", [P, KEYS], F32, B) for i in range(6)]
    pth = sb("pth", [P, 4, REP * P], F32R, B)
    ptl = sb("ptl", [P, 4, REP * P], F32R, B)
    diag = [sb(f"diag{i}", [P, REP, P], F32, B) for i in range(2)]
    rbc = sb("rbc", [P, REP * P], F32, B)
    oth = sb("oth", [P, REP * P], F32, B)
    osum = sb("osum", [P, REP * P], F32, B)
    mix = sb("mix", [P, KD, P], F32, B)
    mx = sb("mx", [P, NQ, 4], F32, B)
    nb = sb("nb", [P, NQ], F32, B)
    den = sb("den", [P, NQ, 4], F32, B)
    rden = sb("rden", [P, NQ], F32, B)
    xr = sb("xr", [P, D], F32, B)
    x2 = sb("x2", [P, D], F32, B)
    h2 = sb("h2", [P, D], F32, B)
    junk2 = sb("junk2", [P, D], F32, B)
    h2t = sb("h2t", [P, KD, P], F32, B)
    st2 = sb("st2", [P, 4], F32, B)
    lg = sb("lg", [P, 4, E], F32, B)
    s = {n: sem("b_" + n) for n in (
        "w_in", "q_in", "s_done", "nb_done", "exp_done", "t_done", "hi_done", "lo_done", "pv_done", "osum_done",
        "rden_done", "diag_done", "misc_mm", "misc_free", "oth_done", "rbc_done", "mix_done", "ymix_done", "x_in",
        "x2_done", "ss_done", "rstd_done", "mean", "h2a", "h2b", "h2_out", "x2_out", "h2t_done", "neg_done", "lexp", "aff_rows",
        "dve_order", "op_sum")}
    CH = [(0, 512), (512, 1024), (1024, KEYS)]
    NCH = len(CH)
    NS = NCH * NQ
    KT = TS
    NT = KT * NKV
    PTB, OB, MB = 4, 6, 7
    MISC0 = 2

    def misc(t, j):
        return j if isinstance(t, int) and t == 0 else MISC0 + 10 * (t - 1) + j

    def schedule(eng_step, eng):
        eng_step(0, False, True)
        eng_step(1, True, True)
        with eng.Fori(2, TL) as t:
            eng_step(t, True, True)
        eng_step(TL, True, False)

    def use_numbers(prev, cur):
        names = []
        if prev:
            names += ["R0", "R3", "OP0", "OP1"]
        if cur:
            names += ["R6"]
        if prev:
            names += ["HT0"]
        if cur:
            names += ["R9"]
        if prev:
            names += ["HT1", "RT", "AF"]
        return {n: i for i, n in enumerate(names)}

    def flushes(prev, cur):
        return {sl: sl // 3 - 2 for sl in (0, 3, 6, 9) if (prev if sl < 6 else cur)}

    def items(i, prev, cur):
        g = i // 3 - 1
        if (g < 0 and not prev) or (g >= 0 and not cur):
            return []
        lo, hi = ((0, 4), (4, 7), (7, 10))[i % 3]
        return [KT * g + k for k in range(lo, hi)]

    with nc.Block() as block:
        @block.sync
        def _(sp):
            sp.dma_start(wrt[:, :, :], a["w_router"][0].rearrange("(k p) e -> p k e", p=P)).then_inc(s["w_in"], 16)
            wo = a["w_out"][0]
            for g in range(NKV):
                half = (g % 2) * HD
                sp.dma_start(wout[half:half + HD, 3 * (g // 2):3 * (g // 2) + REP, :],
                             wo[FW + g * REP * HD:FW + (g + 1) * REP * HD, :].rearrange("(r p) n -> p r n", p=HD)).then_inc(s["w_in"], 16)
            sp.dma_start(wout[:, 6:8, :], wo[0:FW, :].rearrange("(k p) n -> p k n", p=P)).then_inc(s["w_in"], 16)

            def step(t, prev, cur):
                if cur:
                    after(sp, s["s_done"], t * NS)
                    sp.dma_start(qt[:, :, :, :].rearrange("p h a n -> p (h a n)").bitcast(F32), q_d[t]).then_inc(s["q_in"], 16)
                if prev:
                    after(sp, s["x2_done"], (t - 1) * 2)
                    sp.dma_start(xr[:, :], x_d[t - 1]).then_inc(s["x_in"], 16)
                    sp.wait_ge(s["x2_done"], t * 2)
                    sp.dma_start(acc_d.rearrange("(t p) d -> t p d", p=P)[t - 1], x2[:, :]).then_inc(s["x2_out"], 16)
                    sp.wait_ge(s["h2b"], t)
                    sp.dma_start(h2_d.rearrange("(t p) d -> t p d", p=P)[t - 1], h2[:, :]).then_inc(s["h2_out"], 16)
            schedule(step, sp)
            sp.wait_ge(s["x2_out"], 16 * TL)
            sp.wait_ge(s["h2_out"], 16 * TL)

        @block.gpsimd
        def _(pool):
            def step(t, prev, cur):
                use = use_numbers(prev, cur)
                if prev:
                    after(pool, s["x2_done"], 2 * (t - 1))
                    pool.tensor_copy(mix[:, 6:8, :], y_t[:, :, bass.ds((t - 1) * P, P)]).then_inc(s["ymix_done"], 1)
                for i in range(NQ):
                    if cur:
                        g, r = i // 3, i % 3
                        if r == 0:
                            if f"R{i}" in use:
                                pool.wait_ge(s["misc_mm"], misc(t, use[f"R{i}"]) + 1)
                        pool.wait_ge(s["rden_done"], NQ * t + i + 1)
                        pool.tensor_tensor(diag[g % 2][:, r, :], ident[:, :], rden[:, i:i + 1].broadcast_to([P, P]), ALU.mult).then_inc(s["diag_done"], 1)
                    if prev and i == 6:
                        pool.wait_ge(s["ss_done"], t)
                        pool.tensor_tensor(st2[:, 1:2], st2[:, 0:1], eps_c[:, 1:2], ALU.add).then_inc(s["mean"], 1)
                        pool.wait_ge(s["mean"], t)
                        pool.tensor_tensor(st2[:, 2:3], st2[:, 1:2], eps_c[:, 0:1], ALU.pow).then_inc(s["rstd_done"], 1)
            schedule(step, pool)

        @block.scalar
        def _(act):
            def step(t, prev, cur):
                use = use_numbers(prev, cur)
                fl = flushes(prev, cur)
                for i in range(NQ):
                    if i in fl:
                        G = 4 * t + fl[i]
                        act.wait_ge(s["pv_done"], KT * (G + 1))
                        after(act, s["osum_done"], G)
                        if fl[i] % 2 == 0:
                            act.activation(oth[0:HD, :], psum[HD:P, OB, 0:REP * P], ACT.Copy).then_inc(s["oth_done"], 1)
                        else:
                            act.activation(oth[HD:P, :], psum[0:HD, OB, 0:REP * P], ACT.Copy).then_inc(s["oth_done"], 1)
                        act.wait_ge(s["misc_mm"], misc(t, use[f"R{i}"]) + 1)
                        after(act, s["mix_done"], G)
                        act.activation(rbc[:, :], psum[:, MB, 0:REP * P], ACT.Copy).then_inc(s["misc_free"], 1)
                    ex = list(range(NCH)) if cur else []
                    its = items(i, prev, cur)
                    while ex or its:
                        if its:
                            k = its.pop(0)
                            n = NT * t + k
                            act.wait_ge(s["t_done"], n + 1)
                            if not (isinstance(t, int) and t == 0 and k < 4):
                                act.wait_ge(s["pv_done"], n - 3)
                            act.activation(pth[:, k % 4, :], psum[:, PTB + k % 2, 0:REP * P], ACT.Copy).then_inc(s["hi_done"], 1)
                        if ex:
                            c = ex.pop(0)
                            lo, hi = CH[c]
                            b = (NCH * i + c) % 4
                            if c == 0:
                                act.wait_ge(s["nb_done"], NQ * t + i + 1)
                                g = i // 3
                                if not (isinstance(t, int) and t == 0 and g < 2):
                                    act.wait_ge(s["t_done"], KT * (4 * t + g - 1))
                            act.activation(pr[(i // 3 % 2) * 3 + i % 3][:, lo:hi], psum[:, b, 0:hi - lo], ACT.Exp,
                                           bias=nb[:, i:i + 1], scale=SCALE, accum_out=den[:, i, c:c + 1]).then_inc(s["exp_done"], 1)
                    if prev and i == 8:
                        act.wait_ge(s["misc_mm"], misc(t, use["HT0"]) + 1)
                        after(act, s["neg_done"], t - 1)
                        act.activation(h2t[:, 0:4, :].rearrange("p k n -> p (k n)"), psum[:, MB, :], ACT.Copy).then_inc(s["misc_free"], 1)
                    if prev and i == 9:
                        act.wait_ge(s["misc_mm"], misc(t, use["HT1"]) + 1)
                        act.activation(h2t[:, 4:8, :].rearrange("p k n -> p (k n)"), psum[:, MB, :], ACT.Copy).then_inc(s["misc_free"], 1)
                    if prev and i == 5:
                        act.wait_ge(s["x2_done"], 2 * t)
                        after(act, s["rstd_done"], t - 1)
                        act.activation(junk2[:, :], x2[:, :], ACT.Square, accum_out=st2[:, 0:1]).then_inc(s["ss_done"], 1)
                    if prev and i == 10:
                        act.wait_ge(s["neg_done"], t)
                        act.activation(lg[:, 1, :], psum[:, MB, 0:E], ACT.Exp, bias=st2[:, 3:4], scale=1.0,
                                       accum_out=lg[:, 2, 0:1]).then_inc(s["lexp"], 1)
                    if prev and i == 11:
                        act.wait_ge(s["misc_mm"], misc(t, use["AF"]) + 1)
                        act.activation(aff[:, bass.ds((t - 1) * P, P)], psum[0:E, MB, 0:P], ACT.Copy).then_inc(s["misc_free"], 1)
            schedule(step, act)

        @block.vector
        def _(dve):
            def step(t, prev, cur):
                use = use_numbers(prev, cur)
                fl = flushes(prev, cur)
                PER0, PER = 2 * NQ, 2 * NQ + 2
                base = 0 if isinstance(t, int) and t == 0 else PER0 + (t - 1) * PER
                count = [0]

                def chain(ins):
                    count[0] += 1
                    ins.then_inc(s["dve_order"], 1)
                    dve.wait_ge(s["dve_order"], base + count[0])
                for i in range(NQ):
                    if cur:
                        for c, (lo, hi) in enumerate(CH):
                            b = (NCH * i + c) % 4
                            dve.wait_ge(s["s_done"], NS * t + NCH * i + c + 1)
                            ins = dve.tensor_reduce(mx[:, i, c:c + 1], psum[:, b, 0:hi - lo], AX, ALU.max)
                        chain(ins)
                        chain(dve.tensor_reduce(mx[:, i, 3:4], mx[:, i, 0:3], AX, ALU.max))
                        dve.tensor_scalar(nb[:, i:i + 1], mx[:, i, 3:4], -SCALE, None, ALU.mult).then_inc(s["nb_done"], 1)
                    if i in fl:
                        G = 4 * t + fl[i]
                        par = fl[i] % 2
                        h = slice(par * HD, (par + 1) * HD)
                        g = fl[i] % 4
                        dve.wait_ge(s["oth_done"], G + 1)
                        dve.tensor_tensor(osum[h, :], psum[h, OB, 0:REP * P], oth[h, :], ALU.add).then_inc(s["osum_done"], 1)
                        dve.wait_ge(s["osum_done"], G + 1)
                        dve.wait_ge(s["misc_free"], misc(t, use[f"R{i}"]) + 1)
                        dve.tensor_tensor(mix[h, 3 * (g // 2):3 * (g // 2) + REP, :].rearrange("p r n -> p (r n)"),
                                          osum[h, :], rbc[h, :], ALU.mult).then_inc(s["mix_done"], 1)
                    for k in items(i, prev, cur):
                        n = NT * t + k
                        dve.wait_ge(s["hi_done"], n + 1)
                        dve.tensor_tensor(ptl[:, k % 4, :], psum[:, PTB + k % 2, 0:REP * P], pth[:, k % 4, :].bitcast(F32),
                                          ALU.subtract).then_inc(s["lo_done"], 1)
                    if cur:
                        dve.wait_ge(s["exp_done"], NS * t + NCH * (i + 1))
                        ins = dve.tensor_reduce(den[:, i, 3:4], den[:, i, 0:3], AX, ALU.add)
                        if not (isinstance(t, int) and t == 0):
                            dve.wait_ge(s["diag_done"], NQ * (t - 1) + i + 1)
                        ins.then_inc(s["op_sum"], 1)
                        dve.wait_ge(s["op_sum"], NQ * t + i + 1)
                        dve.reciprocal(rden[:, i:i + 1], den[:, i, 3:4]).then_inc(s["rden_done"], 1)
                    if prev and i in (4, 5):
                        j = i - 4
                        c = slice(j * 512, (j + 1) * 512)
                        dve.wait_ge(s["misc_mm"], misc(t, use[f"OP{j}"]) + 1)
                        if j == 0:
                            dve.wait_ge(s["x_in"], 16 * t)
                            after(dve, s["x2_out"], 16 * (t - 1))
                            after(dve, s["h2a"], t - 1)
                        dve.tensor_tensor(x2[:, c], psum[:, MB, :], rows[:, G1, c], ALU.mult).then_inc(s["misc_free"], 1)
                        dve.wait_ge(s["misc_free"], misc(t, use[f"OP{j}"]) + 1)
                        dve.tensor_tensor(x2[:, c], x2[:, c], xr[:, c], ALU.add).then_inc(s["x2_done"], 1)
                    if prev and i == 6:
                        dve.wait_ge(s["rstd_done"], t)
                        after(dve, s["h2_out"], 16 * (t - 1))
                        dve.scalar_tensor_tensor(out=h2[:, :], in0=x2[:, :], scalar=st2[:, 2:3], in1=rows[:, SC2, :],
                                                 op0=ALU.mult, op1=ALU.mult).then_inc(s["h2a"], 1)
                        dve.wait_ge(s["h2a"], t)
                        dve.tensor_tensor(h2[:, :], h2[:, :], rows[:, SH2, :], ALU.add).then_inc(s["h2b"], 1)
                    if prev and i == 10:
                        dve.wait_ge(s["misc_mm"], misc(t, use["RT"]) + 1)
                        chain(dve.tensor_reduce(lg[:, 2, 1:2], psum[:, MB, 0:E], AX, ALU.max))
                        dve.tensor_scalar(st2[:, 3:4], lg[:, 2, 1:2], -1.0, None, ALU.mult).then_inc(s["neg_done"], 1)
                    if prev and i == 11:
                        dve.wait_ge(s["lexp"], t)
                        chain(dve.reciprocal(lg[:, 2, 2:3], lg[:, 2, 0:1]))
                        dve.tensor_scalar(lg[:, 0, :], lg[:, 1, :], lg[:, 2, 2:3], None, ALU.mult).then_inc(s["misc_free"], 1)
            schedule(step, dve)

        @block.tensor
        def _(pe):
            pe.wait_ge(s["w_in"], 16 * 6)

            def step(t, prev, cur):
                use = use_numbers(prev, cur)
                fl = flushes(prev, cur)

                def times(k):
                    n = NT * t + k
                    g, kt = k // KT, k % KT
                    pe.wait_ge(s["lo_done"], n + 1)
                    if kt == 0:
                        after(pe, s["osum_done"], 4 * t + g)
                    v = vs[:, kt, g % 4, :, :].rearrange("p a d -> p (a d)")
                    pe.matmul(psum[:, OB, 0:REP * P], v, pth[:, k % 4, :], start=(kt == 0), stop=False)
                    ins = pe.matmul(psum[:, OB, 0:REP * P], v, ptl[:, k % 4, :], start=False, stop=(kt == KT - 1))
                    ins.then_inc(s["pv_done"], 1)

                def misc_free(name):
                    after(pe, s["misc_free"], misc(t, use[name]))

                if cur:
                    pe.wait_ge(s["q_in"], 16 * (t + 1))
                for i in range(NQ):
                    if cur:
                        for c, (lo, hi) in enumerate(CH):
                            n = NCH * i + c
                            if not (isinstance(t, int) and t == 0 and n < 4):
                                pe.wait_ge(s["exp_done"], NS * t + n - 3)
                            o = psum[:, n % 4, 0:hi - lo]
                            pe.matmul(o, qt[:, i, 0, :], ks[:, i // 3, lo:hi], start=True, stop=False)
                            pe.matmul(o, qt[:, i, 1, :], ks[:, i // 3, lo:hi], start=False, stop=True).then_inc(s["s_done"], 1)
                    if i in fl:
                        k0 = KT * (fl[i] + 1)
                        times(k0 - 2)
                        times(k0 - 1)
                        G = 4 * t + fl[i]
                        pe.wait_ge(s["diag_done"], 3 * (G + 1))
                        misc_free(f"R{i}")
                        pe.matmul(psum[:, MB, 0:REP * P], ones[:, :], diag[fl[i] % 2][:, :, :].rearrange("p r n -> p (r n)"),
                                  start=True, stop=True).then_inc(s["misc_mm"], 1)
                    for k in items(i, prev, cur):
                        n = NT * t + k
                        g, kt = k // KT, k % KT
                        if kt == 0:
                            pe.wait_ge(s["exp_done"], 9 * (4 * t + g + 1))
                        if not (isinstance(t, int) and t == 0 and k < 2):
                            pe.wait_ge(s["lo_done"], n - 1)
                        for r in range(REP):
                            ins = pe.transpose(psum[:, PTB + k % 2, r * P:(r + 1) * P],
                                               pr[(g % 2) * 3 + r][:, kt * P:(kt + 1) * P], ident[:, :])
                        ins.then_inc(s["t_done"], 1)
                        if kt >= 2:
                            times(k - 2)
                    if prev and i in (4, 5):
                        j = i - 4
                        pe.wait_ge(s["mix_done"], 4 * t)
                        pe.wait_ge(s["ymix_done"], t)
                        misc_free(f"OP{j}")
                        for k in range(KD):
                            ins = pe.matmul(psum[:, MB, :], mix[:, k, :], wout[:, k, j * 512:(j + 1) * 512],
                                            start=(k == 0), stop=(k == KD - 1))
                        ins.then_inc(s["misc_mm"], 1)
                    if prev and i in (8, 9):
                        j = i - 8
                        pe.wait_ge(s["h2b"], t)
                        misc_free(f"HT{j}")
                        for k in range(4):
                            ins = pe.transpose(psum[:, MB, k * P:(k + 1) * P], h2[:, (4 * j + k) * P:(4 * j + k + 1) * P], ident[:, :])
                        ins.then_inc(s["misc_mm"], 1)
                    if prev and i == 10:
                        misc_free("RT")
                        for k in range(KD):
                            ins = pe.matmul(psum[:, MB, 0:E], h2t[:, k, :], wrt[:, k, :], start=(k == 0), stop=(k == KD - 1))
                        ins.then_inc(s["misc_mm"], 1)
                    if prev and i == 11:
                        misc_free("AF")
                        pe.transpose(psum[0:E, MB, 0:P], lg[:, 0, :], ident[:, :]).then_inc(s["misc_mm"], 1)
            schedule(step, pe)
    B.close()


def nc_phase_m(nc, ctx, sem, sb, a, psum, ident, rows, aff, eps_c, h2_d, acc_d, w_gate, w_up, w_down, out_d):
    G1, SH2, SC2, G2 = range(4)

    M = ExitStack()
    NU = 4
    CH = KD * UC // 2
    NJ = DE // UC
    unit = [sb(f"munit{i}", [P, KD * UC], F32, M) for i in range(NU)]
    top = sb("top", [E, CAP], F32, M)
    topi = sb("topi", [E, CAP], U32, M)
    topf = sb("topf", [E, CAP], F32, M)
    icol = sb("icol", [P, E], U32, M)
    gcol = sb("gcol", [P, E], F32, M)
    idx_g = sb("idx_g", [P, 1], U32, M)
    idx_s = sb("idx_s", [P, 1], U32, M)
    gate_s = sb("gate_s", [P, 1], F32, M)
    xe = sb("xe", [P, D], F32, M)
    x_hi, x_lo = (sb(f"x_{n}", [P, KD, P], F32R, M) for n in ("hi", "lo"))
    w_hi, w_lo = ([[sb(f"w_{n}{i}{c}", [P, CH], F32R, M) for c in range(2)] for i in range(2)] for n in ("hi", "lo"))
    sil = [sb(f"sil{i}", [P, UC], F32, M) for i in range(2)]
    hid = [sb(f"hid{i}", [P, UC], F32, M) for i in range(2)]
    hidt = [sb(f"hidt{i}", [P, UC // P, P], F32, M) for i in range(2)]
    ysc = sb("ysc", [P, D], F32, M)
    carry = sb("carry", [P, 2], F32, M)
    fgain = sb("fgain", [P, D], F32, M)
    xa = [sb(f"xa{i}", [P, D], F32, M) for i in range(4)]
    sqj = sb("sqj", [P, D], F32, M)
    fst = sb("fst", [P, TL, 3], F32, M)
    s = {n: sem("m_" + n) for n in (
        "top_order", "carried", "top_done", "top_t", "cols_done", "idx_g", "x_in", "x_mm", "x_a", "x_b",
        "gate_mm", "up_mm", "sil_done", "hid_done", "ht_mm", "ht_done", "down_mm", "y_done", "y_out", "sel_done",
        "hi_done", "lo_done", "fg_in", "a_done", "mean", "rstd", "norm_done", "out_done")}
    unit_in = [sem(f"munit_in{i}") for i in range(NU)]
    NX = 4
    xa_in = [sem(f"xa_in{i}") for i in range(NX)]
    xa_out = [sem(f"xa_out{i}") for i in range(NX)]
    Y, HB, XB = 4, 6, 7

    def arrived(e, k):
        v = 3 * NJ // NU * e + k // NU + 1
        return 16 * (v - 1 if k % NU == 2 and not (isinstance(e, int) and e == 0 and k <= 2) else v)

    with nc.Block() as block:
        @block.sync
        def _(sp):
            def load(e, k, src, cols):
                dst = unit[k % NU][:, :].rearrange("p (k n) -> p k n", n=cols)
                if k >= NU or not (isinstance(e, int) and e == 0):
                    le, lk = (e, k - NU) if k >= NU else (e - 1, k + 3 * NJ - NU)
                    if lk % 3 == 2:
                        after(sp, s["down_mm"], NJ * le + lk // 3)
                    else:
                        sp.wait_ge(s["lo_done"], 4 * (NJ * le + lk // 3) + 2 * (lk % 3) + 2)
                sp.dma_start(dst, src).then_inc(unit_in[k % NU], 16)

            def expert(e, first):
                for j in range(NJ):
                    c = slice(j * UC, (j + 1) * UC)
                    load(e, 3 * j, w_gate[e][:, :, c], UC)
                    load(e, 3 * j + 1, w_up[e][:, :, c], UC)
                    if j > 0:
                        load(e, 3 * j + 2, w_down[e][:, 4 * (j - 1):4 * j, :], D)
                    elif not first:
                        load(e, 2, w_down[e - 1][:, 4 * (NJ - 1):4 * NJ, :], D)
            sp.dma_start(fgain[:, :], a["final_norm_g"].partition_broadcast(P)).then_inc(s["fg_in"], 16)
            expert(0, True)
            with sp.Fori(1, E) as e:
                expert(e, False)
            load(E, 0, w_down[E - 1][:, 4 * (NJ - 1):4 * NJ, :], D)
            sp.wait_ge(s["y_out"], 16 * E)
            for t in range(TL):
                if t >= NX:
                    sp.wait_ge(xa_out[t % NX], 16 * (t // NX))
                sp.dma_start(xa[t % NX][:, :], acc_d.rearrange("(t p) d -> t p d", p=P)[t]).then_inc(xa_in[t % NX], 16)

        @block.gpsimd
        def _(pool):
            pool.wait_ge(s["cols_done"], 2)

            pool.memset(carry[:, :], 0.0).then_inc(s["carried"], 1)

            def carrier(n):
                pool.wait_ge(s["carried"], n + 1)
                pool.tensor_tensor(carry[:, 1:2], carry[:, 0:1], carry[:, 0:1], ALU.add).then_inc(s["carried"], 1)

            def gather(e):
                after(pool, s["x_in"], 16 * e)
                pool.tensor_copy(idx_g[:, :], icol[:, bass.ds(e, 1)]).then_inc(s["idx_g"], 1)
                pool.wait_ge(s["idx_g"], e + 1)
                after(pool, s["x_mm"], 2 * e)
                carrier(2 * e - 1 if not (isinstance(e, int) and e == 0) else 0)
                pool.indirect_dma_start(out=xe[:, :], out_offset=None, in_=h2_d,
                                        in_offset=bass.IndirectOffsetOnAxis(ap=idx_g[:, 0:1], axis=0)).then_inc(s["x_in"], 16)

            def scatter(e):
                after(pool, s["y_out"], 16 * e)
                pool.tensor_copy(idx_s[:, :], icol[:, bass.ds(e, 1)])
                pool.tensor_copy(gate_s[:, :], gcol[:, bass.ds(e, 1)]).then_inc(s["sel_done"], 1)
                pool.wait_ge(s["sel_done"], e + 1)
                pool.wait_ge(s["y_done"], e + 1)
                carrier(2 * e + 2 if not (isinstance(e, int) and e == E - 1) else 2 * e + 1)
                pool.indirect_dma_start(out=acc_d, out_offset=bass.IndirectOffsetOnAxis(ap=idx_s[:, 0:1], axis=0),
                                        in_=ysc[:, :], in_offset=None, compute_op=ALU.add).then_inc(s["y_out"], 16)
            gather(0)
            gather(1)
            scatter(0)
            with pool.Fori(1, E - 1) as e:
                gather(e + 1)
                scatter(e)
            scatter(E - 1)
            for t in range(TL):
                pool.wait_ge(s["a_done"], t + 1)
                pool.tensor_tensor(fst[:, t, 1:2], fst[:, t, 0:1], eps_c[:, 1:2], ALU.add).then_inc(s["mean"], 1)
                pool.wait_ge(s["mean"], t + 1)
                pool.tensor_tensor(fst[:, t, 2:3], fst[:, t, 1:2], eps_c[:, 0:1], ALU.pow).then_inc(s["rstd"], 1)

        @block.scalar
        def _(act):
            def x_part(e, half):
                act.wait_ge(s["x_mm"], 2 * e + half + 1)
                after(act, s["up_mm"], NJ * e)
                act.activation(x_hi[:, 4 * half:4 * half + 4, :].rearrange("p k n -> p (k n)"), psum[:, XB, :], ACT.Copy).then_inc(s["x_a"], 1)

            def split(e, j, which, c):
                k0 = 3 * j + which
                if c == 0:
                    act.wait_ge(unit_in[k0 % NU], arrived(e, k0))
                    after(act, s["up_mm" if which else "gate_mm"], NJ * e + j)
                act.activation(w_hi[which][c][:, :], unit[k0 % NU][:, c * CH:(c + 1) * CH], ACT.Copy).then_inc(s["hi_done"], 1)

            def gate(e, j):
                st = NJ * e + j
                act.wait_ge(s["gate_mm"], st + 1)
                if not (isinstance(e, int) and e == 0 and j < 2):
                    act.wait_ge(s["hid_done"], st - 1)
                act.activation(sil[j % 2][:, :], psum[:, 2 * (j % 2), :], ACT.Silu).then_inc(s["sil_done"], 1)

            def turn(e, j):
                st = NJ * e + j
                act.wait_ge(s["ht_mm"], st + 1)
                if not (isinstance(e, int) and e == 0 and j < 2):
                    act.wait_ge(s["down_mm"], st - 1)
                act.activation(hidt[j % 2][:, :, :].rearrange("p k n -> p (k n)"), psum[:, HB, :], ACT.Copy).then_inc(s["ht_done"], 1)

            def expert(e, first, last):
                for j in range(NJ):
                    gate(e, j)
                    if j > 0:
                        turn(e, j - 1)
                    elif not first:
                        turn(e - 1, NJ - 1)
                    if j < NJ - 1 or not last:
                        en, jn = (e, j + 1) if j < NJ - 1 else (e + 1, 0)
                        for which, c in ((0, 0), (0, 1), (1, 0), (1, 1)):
                            if j == NJ - 1 and which == 1:
                                x_part(en, c)
                            split(en, jn, which, c)
            for which, c in ((0, 0), (0, 1), (1, 0), (1, 1)):
                if which == 0:
                    x_part(0, c)
                split(0, 0, which, c)
            expert(0, True, False)
            with act.Fori(1, E - 1) as e:
                expert(e, False, False)
            expert(E - 1, False, True)
            turn(E - 1, NJ - 1)

            def store(t):
                act.wait_ge(s["norm_done"], t + 1)
                act.dma_start(out_d[t], xa[t % NX][:, :]).then_inc(xa_out[t % NX], 16)
            for t in range(TL):
                act.wait_ge(xa_in[t % NX], 16 * (t // NX + 1))
                after(act, s["a_done"], t)
                act.activation(sqj[:, :], xa[t % NX][:, :], ACT.Square, accum_out=fst[:, t, 0:1]).then_inc(s["a_done"], 1)
                if t >= 1:
                    store(t - 1)
            store(TL - 1)
            for i in range(NX):
                act.wait_ge(xa_out[i], 16 * (TL // NX))

        @block.vector
        def _(dve):
            dve.wait_ge(s["fg_in"], 16)
            dve.tensor_scalar(fgain[:, :], fgain[:, :], ROOT, None, ALU.mult)
            for r in range(CAP // 8):
                v = slice(8 * r, 8 * r + 8)
                dve.max(top[:, v], aff[:, :]).then_inc(s["top_order"], 1)
                dve.wait_ge(s["top_order"], 2 * r + 1)
                dve.max_index(topi[:, v], top[:, v], aff[:, :])
                dve.match_replace(aff[:, :], top[:, v], aff[:, :], -1.0).then_inc(s["top_order"], 1)
                dve.wait_ge(s["top_order"], 2 * r + 2)
            dve.tensor_copy(topf[:, :], topi[:, :]).then_inc(s["top_done"], 1)
            dve.wait_ge(s["top_t"], 2)
            dve.tensor_copy(gcol[:, :], psum[:, 0, 0:E]).then_inc(s["cols_done"], 1)
            dve.tensor_copy(icol[:, :], psum[:, 1, 0:E]).then_inc(s["cols_done"], 1)

            def x_part(e, half):
                dve.wait_ge(s["x_a"], 2 * e + half + 1)
                k = slice(4 * half, 4 * half + 4)
                dve.tensor_tensor(x_lo[:, k, :].rearrange("p k n -> p (k n)"), psum[:, XB, :],
                                  x_hi[:, k, :].bitcast(F32).rearrange("p k n -> p (k n)"), ALU.subtract).then_inc(s["x_b"], 1)

            def split(e, j, which, c):
                dve.wait_ge(s["hi_done"], 4 * (NJ * e + j) + 2 * which + c + 1)
                dve.tensor_tensor(w_lo[which][c][:, :], unit[(3 * j + which) % NU][:, c * CH:(c + 1) * CH],
                                  w_hi[which][c][:, :].bitcast(F32), ALU.subtract).then_inc(s["lo_done"], 1)

            def hidden(e, j):
                st = NJ * e + j
                dve.wait_ge(s["sil_done"], st + 1)
                dve.wait_ge(s["up_mm"], st + 1)
                if not (isinstance(e, int) and e == 0 and j < 2):
                    dve.wait_ge(s["ht_mm"], st - 1)
                dve.tensor_tensor(hid[j % 2][:, :], sil[j % 2][:, :], psum[:, 2 * (j % 2) + 1, :], ALU.mult).then_inc(s["hid_done"], 1)

            def result(e):
                dve.wait_ge(s["down_mm"], NJ * (e + 1))
                dve.wait_ge(s["sel_done"], e + 1)
                after(dve, s["y_out"], 16 * e)
                dve.scalar_tensor_tensor(out=ysc[:, :], in0=psum[:, Y:Y + 2, :].rearrange("p a n -> p (a n)"), scalar=gate_s[:, 0:1],
                                         in1=rows[:, G2, :], op0=ALU.mult, op1=ALU.mult).then_inc(s["y_done"], 1)

            def expert(e, first, last):
                for j in range(NJ):
                    ahead = j < NJ - 1 or not last
                    en, jn = (e, j + 1) if j < NJ - 1 else (e + 1, 0)
                    if ahead:
                        split(en, jn, 0, 0)
                        split(en, jn, 0, 1)
                    hidden(e, j)
                    if ahead:
                        for c in range(2):
                            if j == NJ - 1:
                                x_part(en, c)
                            split(en, jn, 1, c)
                    if j == 0 and not first:
                        result(e - 1)
            for which, c in ((0, 0), (0, 1), (1, 0), (1, 1)):
                if which == 0:
                    x_part(0, c)
                split(0, 0, which, c)
            expert(0, True, False)
            with dve.Fori(1, E - 1) as e:
                expert(e, False, False)
            expert(E - 1, False, True)
            result(E - 1)
            for t in range(TL):
                dve.wait_ge(s["rstd"], t + 1)
                dve.scalar_tensor_tensor(out=xa[t % NX][:, :], in0=xa[t % NX][:, :], scalar=fst[:, t, 2:3], in1=fgain[:, :],
                                         op0=ALU.mult, op1=ALU.mult).then_inc(s["norm_done"], 1)

        @block.tensor
        def _(pe):
            pe.wait_ge(s["top_done"], 1)
            pe.transpose(psum[:, 0, 0:E], top[:, :], ident[0:E, 0:E]).then_inc(s["top_t"], 1)
            pe.transpose(psum[:, 1, 0:E], topf[:, :], ident[0:E, 0:E]).then_inc(s["top_t"], 1)

            def x_turn(e, half):
                if half == 0:
                    pe.wait_ge(s["x_in"], 16 * (e + 1))
                    after(pe, s["x_b"], 2 * e)
                else:
                    pe.wait_ge(s["x_b"], 2 * e + 1)
                for k in range(4):
                    i = pe.transpose(psum[:, XB, k * P:(k + 1) * P], xe[:, (4 * half + k) * P:(4 * half + k + 1) * P], ident[:, :])
                i.then_inc(s["x_mm"], 1)

            def project(e, j, which):
                st = NJ * e + j
                if which == 0:
                    if j == 0:
                        pe.wait_ge(s["x_b"], 2 * e + 2)
                    if not (isinstance(e, int) and e == 0 and j < 2):
                        pe.wait_ge(s["sil_done"], st - 1)
                    elif j == 0:
                        pe.wait_ge(s["cols_done"], 2)
                elif not (isinstance(e, int) and e == 0 and j < 2):
                    pe.wait_ge(s["hid_done"], st - 1)
                for k in range(KD):
                    if k % 4 == 0:
                        pe.wait_ge(s["lo_done"], 4 * st + 2 * which + k // 4 + 1)
                    hi, lo = (w[which][k // 4][:, (k % 4) * UC:(k % 4 + 1) * UC] for w in (w_hi, w_lo))
                    for x_, w_ in ((x_hi, hi), (x_hi, lo), (x_lo, hi)):
                        i = pe.matmul(psum[:, 2 * (j % 2) + which, :], x_[:, k, :], w_, start=(k == 0 and w_ is hi and x_ is x_hi),
                                      stop=(k == KD - 1 and x_ is x_lo))
                i.then_inc(s["up_mm" if which else "gate_mm"], 1)

            def turn(e, j):
                st = NJ * e + j
                pe.wait_ge(s["hid_done"], st + 1)
                after(pe, s["ht_done"], st)
                for k in range(4):
                    i = pe.transpose(psum[:, HB, k * P:(k + 1) * P], hid[j % 2][:, k * P:(k + 1) * P], ident[:, :])
                i.then_inc(s["ht_mm"], 1)

            def down(e, j, en, kn, parts):
                st = NJ * e + j
                if 0 in parts:
                    pe.wait_ge(s["ht_done"], st + 1)
                    pe.wait_ge(unit_in[kn % NU], arrived(en, kn))
                    if j == 0:
                        after(pe, s["y_done"], e)
                u = unit[kn % NU][:, :].rearrange("p (k n) -> p k n", n=D)
                for h in parts:
                    for k in range(4):
                        i = pe.matmul(psum[:, Y + h, :], hidt[j % 2][:, k, :], u[:, k, h * 512:(h + 1) * 512],
                                      start=(j == 0 and k == 0), stop=(j == NJ - 1 and k == 3))
                if 1 in parts:
                    i.then_inc(s["down_mm"], 1)

            def expert(e, first, last):
                for j in range(NJ):
                    project(e, j, 0)
                    if j > 0:
                        turn(e, j - 1)
                    elif not first:
                        turn(e - 1, NJ - 1)
                    project(e, j, 1)
                    if j == NJ - 1 and not last:
                        x_turn(e + 1, 0)
                        down(e, j - 1, e, 3 * j + 2, (0,))
                        x_turn(e + 1, 1)
                        down(e, j - 1, e, 3 * j + 2, (1,))
                    elif j > 0:
                        down(e, j - 1, e, 3 * j + 2, (0, 1))
                    elif not first:
                        down(e - 1, NJ - 1, e, 2, (0, 1))
            x_turn(0, 0)
            x_turn(0, 1)
            expert(0, True, False)
            with pe.Fori(1, E - 1) as e:
                expert(e, False, False)
            expert(E - 1, False, True)
            turn(E - 1, NJ - 1)
            down(E - 1, NJ - 1, E, 0, (0, 1))

    M.close()


def kernel(**inputs):
    import concourse.bacc as bacc
    from concourse.bass_utils import run_bass_kernel_spmd

    nc = bacc.Bacc("TRN2", target_bir_lowering=False, num_devices=1)
    arrays, args = {}, {}
    for name, v in {**{n: inputs[n] for n in INPUTS}, **constants()}.items():
        v = np.ascontiguousarray(v)
        arrays[f"in_{name}"] = v
        args[name] = nc.dram_tensor(f"in_{name}", v.shape, mybir.dt.from_np(v.dtype), kind="ExternalInput").ap()
    out = nc.dram_tensor("out", (1, N, D), F32, kind="ExternalOutput").ap()
    build(nc, args, out)
    return run_bass_kernel_spmd(nc, [arrays], core_ids=[0]).results[0]["out"]
```

```python
from contextlib import ExitStack

import numpy as np

import concourse.bass as bass
from concourse import mybir

P = 128
D = 1024
N = 1024
L = 256
HD = 64
NQ, NKV = 12, 4
REP = NQ // NKV
FG, FD = 4, 64
FW = FG * FD
QW, KW = NQ * HD, NKV * HD
IN = FW + QW + 2 * KW
QK = QW + KW
NH = NQ + NKV
E = 16
DE = 2048
CAP = 2 * N // E
GRID = 64
EPS = 1e-6
ROOT = float(D) ** 0.5
KD = D // P
TL, TC = N // P, L // P
TS = TL + TC
KEYS = N + L
HALF = N // 2 + 1
UC = 512
UM = 256
SCALE = HD ** -0.5 * HD

F32 = mybir.dt.float32
F32R = mybir.dt.float32r
U32 = mybir.dt.uint32
ALU = mybir.AluOpType
ACT = mybir.ActivationFunctionType
AX = mybir.AxisListType.X

INPUTS = ["x", "c", "ctx", "c_ctx", "w_mod", "b_mod", "norm_mix_g", "norm_ffn_g", "w_in", "w_four",
          "q_norm_g", "k_norm_g", "w_out", "w_router", "w_gate", "w_up", "w_down", "final_norm_g"]


def constants():
    n, m = np.arange(N)[:, None], np.arange(HALF)[None, :]
    turn = 2 * np.pi * ((n * m) % N) / N
    dft = np.stack([np.cos(turn), np.sin(turn)]).astype(np.float32)
    a = 2 * np.pi * np.outer(np.arange(FD), np.arange(FD)) / FD
    scale = 1 / np.sqrt(N * FD)
    two = np.eye(P // FD)
    chan = np.stack([np.kron(two, np.cos(a) * scale), np.kron(two, -np.sin(a) * scale),
                     np.kron(two, np.sin(a) * scale)]).astype(np.float32)
    half = HD // 4
    freqs = (10000.0 ** (-np.arange(half, dtype=np.float32) / np.float32(half))).astype(np.float32)
    pos = np.arange(N)
    ang = [np.float32(p)[:, None] * freqs[None] for p in (pos // GRID, pos % GRID)]
    cos = np.concatenate([f(x.astype(np.float32)) for x in ang for f in (np.cos, np.cos)], 1)
    sin = np.concatenate([s * np.sin(x.astype(np.float32)) for x in ang for s in (-1, 1)], 1)
    rope = np.stack([cos, sin]).astype(np.float32)
    return {"dft": dft, "chan": chan, "rope": rope}


def build(nc, a, out):
    ctx = ExitStack()

    def dram(name, shape, dt):
        return nc.dram_tensor(name, shape, dt, kind="Internal").ap()

    def sem(name):
        return ctx.enter_context(nc.semaphore(name))

    def sb(name, shape, dt=F32, where=ctx):
        return where.enter_context(nc.sbuf_tensor(name, shape, dt))

    x_d = a["x"].rearrange("b (t p) d -> (b t) p d", p=P)
    ctx_d = a["ctx"].rearrange("b (t p) d -> (b t) p d", p=P)
    out_d = out.rearrange("b (t p) d -> (b t) p d", p=P)
    w_mod = a["w_mod"][0].rearrange("(k p) n -> p k n", p=P)
    w_in = a["w_in"][0].rearrange("(k p) n -> p k n", p=P)
    w_gate = a["w_gate"][0].rearrange("e (k p) f -> e p k f", p=P)
    w_up = a["w_up"][0].rearrange("e (k p) f -> e p k f", p=P)
    w_down = a["w_down"][0].rearrange("e (k p) d -> e p k d", p=P)

    def row(v):
        return v.partition_broadcast(P)

    q_d = dram("q_scratch", [TL, P, NQ * 2 * P], F32)
    h2_d = dram("h2_scratch", [N, D], F32)
    acc_d = dram("acc_scratch", [N, D], F32)

    with ctx:
        psum = ctx.enter_context(nc.psum_tensor("banks", [P, 8, 512], F32))

        ident = sb("ident", [P, P])
        ones = sb("ones", [P, P])
        rows = sb("rows", [P, 4, D])
        G1, SH2, SC2, G2 = range(4)
        aff = sb("aff", [E, N])
        eps_c = sb("eps_c", [P, 2])
        K = ExitStack()
        ks = sb("ks", [P, NKV, KEYS], F32R, K)
        vs = sb("vs", [P, TS, NKV, 2, HD], F32R, K)
        f_tok = sb("f_tok", [P, TL, FW], F32, K)
        y_t = sb("y_t", [P, 2, N], F32, K)

        A = ExitStack()
        unit = [sb(f"unit{i}", [P, KD, UM], F32, A) for i in range(2)]
        win = sb("win", [P, KD, IN], F32, A)
        vec = sb("vec", [5 * KD, P], F32, A)
        c_sig = sb("c_sig", [P, KD, 2], F32, A)
        bg_col = sb("bg_col", [P, 3 * KD], F32, A)
        bm_col, g_col = bg_col[:, 0:2 * KD], bg_col[:, 2 * KD:3 * KD]
        mod_col = sb("mod_col", [P, 2, 2, KD], F32, A)
        xt = sb("xt", [P, D], F32, A)
        xn = sb("xn", [P, D], F32, A)
        junk = sb("junk", [P, D], mybir.dt.bfloat16, A)
        ht = [sb(f"ht{i}", [P, KD, P], F32, A) for i in range(2)]
        stat = sb("stat", [P, 4], F32, A)
        prj = sb("prj", [P, IN], F32, A)
        g_qk = sb("g_qk", [P, 2, HD], F32, A)
        rope = sb("rope", [P, 2, TL, HD], F32, A)
        sq = sb("sq", [P, QK], F32, A)
        ss = sb("ss", [P, 4, NH], F32, A)
        qkn = sb("qkn", [P, QK], F32, A)
        rot = sq
        c_wide = xt[:, :].rearrange("p (k n) -> p k n", n=P)
        hlq = sb("hlq", [P, NQ, 2, 2, HD], F32R, A)
        hlk = sb("hlk", [P, NKV, 2, HD], F32R, A)
        qst = sb("qst", [P, NQ, 2, P], F32, A)
        c_rows = qst[0:2, :, :, :].rearrange("p h a n -> p (h a n)")
        row_unit = [unit[i][:, :, :] for i in range(2)] + [win[:, :, i * UM:(i + 1) * UM] for i in range(6)]

        s = {n: sem(n) for n in (
            "ident_done", "f_done", "small_in", "tables_in", "vec_t", "silu_done", "wide_done", "c_row_done", "c_col_done", "cols_done",
            "win_in", "win_kv_in", "x_in", "ss_done", "rstd_done", "xn_done", "xT_done", "hTa", "hTb", "proj_done",
            "prj_done", "pool_qk", "ss16_done", "rstd16_done", "hl_done", "pool_v", "v_done", "qkt_done",
            "qkt_act", "qkt_dve", "q_out", "row_mm", "row_done", "unit_used", "norm_row_in",
            "mean_done", "dve_order", "pool_order", "eps_done")}
        unit_in = [sem(f"unit_in{i}") for i in range(2)]
        row_in = [sem(f"row_in{i}") for i in range(8)]
        NC_UNITS, NR_UNITS = 2 * D // UM, 4 * D // UM

        def pipeline(eng, stages):
            def step(s_, par):
                for stage, ahead in stages:
                    n = s_ + ahead
                    if not isinstance(n, int):
                        stage(n, (par + ahead) % 2, "lat")
                    elif 0 <= n < TS:
                        stage(n, n % 2, "ctx" if n < TC else "lat")
            for s_ in range(-2, 4):
                step(s_, s_ % 2)
            with eng.Fori(0, (TS - 6) // 2) as pair:
                step(2 * pair + 4, 0)
                step(2 * pair + 5, 1)
            for s_ in range(TS - 2, TS + 2):
                step(s_, s_ % 2)

        XT, PJ, QT = 0, 2, 5
        ROW_BANKS = (0, 1, 7, 2, 3, 4)
        EARLY = 5
        QTG = 7

        with nc.Block() as block:

            @block.sync
            def _(sp):
                for r, v in ((0, a["c"].rearrange("b (k p) -> (b k) p", p=P)), (KD, a["c_ctx"].rearrange("(k p) -> k p", p=P)),
                             (2 * KD, a["b_mod"][0][0:2 * D].rearrange("(k p) -> k p", p=P)),
                             (4 * KD, a["norm_mix_g"][0].rearrange("(k p) -> k p", p=P))):
                    sp.dma_start(vec[r:r + v.shape[0], :], v).then_inc(s["small_in"], 16)
                sp.dma_start(xt[:, :], ctx_d[0]).then_inc(s["x_in"], 16)
                for u in range(NC_UNITS):
                    if u >= 2:
                        sp.wait_ge(s["unit_used"], u - 1)
                    sp.dma_start(unit[u % 2][:, :, :], w_mod[:, :, u * UM:(u + 1) * UM]).then_inc(unit_in[u % 2], 16)
                for c in (1, 0):
                    sp.dma_start(win[:, :, c * 512:(c + 1) * 512], w_in[:, :, c * 512:(c + 1) * 512]).then_inc(s["win_in"], 16)
                    if c == 1:
                        sp.dma_start(g_qk[:, 0, :], row(a["q_norm_g"][0])).then_inc(s["tables_in"], 16)
                        sp.dma_start(g_qk[:, 1, :], row(a["k_norm_g"][0])).then_inc(s["tables_in"], 16)
                        sp.dma_start(rope[:, :, :, :], a["rope"].rearrange("a (t p) d -> p a t d", p=P)).then_inc(s["q_out"], 16)

                def mod_unit(u):
                    sp.dma_start(row_unit[u % 8], w_mod[:, :, (NC_UNITS + u) * UM:(NC_UNITS + u + 1) * UM]).then_inc(row_in[u % 8], 16)

                def prep(n, par, kind):
                    if isinstance(n, int) and n == 0:
                        return
                    src = ctx_d[n] if kind == "ctx" else x_d[n - TC]
                    sp.wait_ge(s["xn_done"], n)
                    sp.dma_start(xt[:, :], src).then_inc(s["x_in"], 16)
                    if isinstance(n, int) and n == TC + 1:
                        sp.dma_start(rows[:, :, :].rearrange("p a d -> p (a d)"), row(a["b_mod"][0][2 * D:6 * D])).then_inc(s["norm_row_in"], 16)
                        sp.wait_ge(s["unit_used"], NC_UNITS)
                        mod_unit(0)
                        mod_unit(1)

                def three(n, par, kind):
                    if kind == "lat":
                        dst, count = q_d[n - TC], (n + 1) * 4
                        sp.wait_ge(s["qkt_act"], count)
                        sp.wait_ge(s["qkt_dve"], count)
                        sp.dma_start(dst, qst[:, :, :, :].rearrange("p h a n -> p (h a n)")).then_inc(s["q_out"], 16)
                    if isinstance(n, int) and n == TS - 2:
                        sp.wait_ge(s["proj_done"], TS)
                        for u in range(2, 8):
                            mod_unit(u)
                        sp.wait_ge(s["xT_done"], 2 * TS)
                        sp.dma_start(xn[:, :], row(a["norm_ffn_g"][0])).then_inc(s["norm_row_in"], 16)

                pipeline(sp, ((prep, 2), (three, -2)))
                for u in range(8, NR_UNITS):
                    sp.wait_ge(s["row_mm"], u - 7)
                    mod_unit(u)
                sp.wait_ge(s["q_out"], 16 * (TL + 1))

            @block.gpsimd
            def _(pool):
                pool.memset(ident[:, :], 0.0).then_inc(s["pool_order"], 1)
                pool.memset(ones[:, :], 1.0)
                pool.memset(eps_c[:, 0:1], -0.5)
                pool.memset(eps_c[:, 1:2], EPS * D)
                pool.wait_ge(s["pool_order"], 1)
                pool.affine_select(out=ident[:, :], in_=ident[:, :], compare_op=ALU.not_equal, fill=1.0,
                                   base=0, pattern=[[-1, P]], channel_multiplier=1).then_inc(s["ident_done"], 1)
                pool.memset(ss[:, 2, :], -0.5)
                pool.memset(ss[:, 3, :], EPS * HD).then_inc(s["eps_done"], 1)
                pool.wait_ge(s["eps_done"], 1)

                def prep(n, par, kind):
                    pool.wait_ge(s["ss_done"], n + 1)
                    after(pool, s["xn_done"], n)
                    pool.tensor_tensor(stat[:, 1:2], stat[:, 0:1], eps_c[:, 1:2], ALU.add).then_inc(s["mean_done"], 1)
                    pool.wait_ge(s["mean_done"], n + 1)
                    pool.tensor_tensor(stat[:, 2:3], stat[:, 1:2], eps_c[:, 0:1], ALU.pow).then_inc(s["rstd_done"], 1)

                def norm(n, par, kind):
                    c0 = 0 if kind == "lat" else QW
                    h0 = c0 // HD
                    pool.wait_ge(s["prj_done"], n + 1)
                    after(pool, s["hl_done"], n)
                    pool.tensor_tensor(sq[:, c0:QK], prj[:, FW + c0:FW + QK], prj[:, FW + c0:FW + QK], ALU.mult).then_inc(s["pool_qk"], 1)
                    pool.tensor_copy(vs[:, n, :, 0, :], prj[:, FW + QK:IN].rearrange("p (h d) -> p h d", d=HD)).then_inc(s["pool_v"], 1)
                    if kind == "lat":
                        pool.tensor_copy(f_tok[:, n - TC, :], prj[:, 0:FW]).then_inc(s["f_done"], 1)
                    pool.wait_ge(s["ss16_done"], n + 1)
                    after(pool, s["hl_done"], n)
                    pool.tensor_tensor(ss[:, 1, h0:NH], ss[:, 0, h0:NH], ss[:, 3, h0:NH], ALU.add).then_inc(s["eps_done"], 1)
                    pool.wait_ge(s["eps_done"], n + 2)
                    pool.tensor_tensor(ss[:, 0, h0:NH], ss[:, 1, h0:NH], ss[:, 2, h0:NH], ALU.pow).then_inc(s["rstd16_done"], 1)

                pipeline(pool, ((norm, -1), (prep, 2)))

            @block.scalar
            def _(act):
                act.dma_start(win[:, :, 1024:IN], w_in[:, :, 1024:IN]).then_inc(s["win_kv_in"], 16)
                act.wait_ge(s["vec_t"], 1)
                act.activation(c_sig[:, :, :].rearrange("p k j -> p j k"),
                               psum[:, 6, 0:2 * KD].rearrange("p (j k) -> p j k", k=KD), ACT.Silu).then_inc(s["silu_done"], 1)
                for u in range(NC_UNITS):
                    act.wait_ge(s["unit_used"], u + 1)
                    act.activation(c_rows[:, u * UM:(u + 1) * UM], psum[0:2, u % 2, 0:UM], ACT.Copy).then_inc(s["c_row_done"], 1)

                def prep(n, par, kind):
                    act.wait_ge(s["x_in"], 16 * (n + 1))
                    after(act, s["rstd_done"], n)
                    act.activation(junk[:, :], xt[:, :], ACT.Square, accum_out=stat[:, 0:1]).then_inc(s["ss_done"], 1)

                def turn(n, par, kind):
                    act.wait_ge(s["xT_done"], 2 * n + 1)
                    after(act, s["proj_done"], n - 1)
                    if isinstance(n, int) and n == 0:
                        act.wait_ge(s["cols_done"], 2)
                    j = 1 if kind == "ctx" else 0
                    for k in range(KD // 2):
                        i = act.activation(ht[par][:, k, :], psum[:, XT, k * P:(k + 1) * P], ACT.Identity,
                                           scale=mod_col[:, 0, j, k:k + 1], bias=mod_col[:, 1, j, k:k + 1])
                    i.then_inc(s["hTa"], 1)

                def two(n, par, kind):
                    act.wait_ge(s["proj_done"], n + 1)
                    c0 = 0 if kind == "lat" else FW + QW
                    after(act, s["pool_v"], n)
                    after(act, s["v_done"], n)
                    if not isinstance(n, int) or n > TC:
                        act.wait_ge(s["f_done"], n - TC)
                    pj = psum[:, PJ:PJ + 3, :].rearrange("p a n -> p (a n)")
                    act.activation(prj[:, c0:IN], pj[:, c0:IN], ACT.Copy).then_inc(s["prj_done"], 1)

                def three(n, par, kind):
                    base = (n - TC) * QTG + TC
                    if kind == "ctx":
                        act.wait_ge(s["qkt_done"], n + 1)
                        act.activation(ks[:, 0:2, bass.ds(n * P, P)],
                                       psum[:, QT, 0:2 * P].rearrange("p (h n) -> p h n", n=P), ACT.Copy).then_inc(s["qkt_act"], 4)
                        return
                    act.wait_ge(s["q_out"], (n - TC + 1) * 16)
                    for j in range(0, QTG, 2):
                        act.wait_ge(s["qkt_done"], base + j + 1)
                        src = psum[:, QT, :].rearrange("p (h n) -> p h n", n=P)
                        dst = ks[:, :, bass.ds(n * P, P)] if j == 0 else \
                            qst[:, 2 * (j - 1):2 * j, :, :].rearrange("p h a n -> p (h a) n")
                        act.activation(dst, src, ACT.Copy).then_inc(s["qkt_act"], 1)

                pipeline(act, ((three, -2), (turn, 1), (prep, 2), (two, 0)))

            @block.vector
            def _(dve):
                order = [0]

                def link(ins):
                    order[0] += 1
                    ins.then_inc(s["dve_order"], 1)
                    dve.wait_ge(s["dve_order"], order[0])

                dve.wait_ge(s["silu_done"], 1)
                link(dve.tensor_copy(bg_col[:, :], psum[:, 6, 2 * KD:5 * KD]))
                dve.wait_ge(s["c_col_done"], 1)
                cols = psum[:, 7, 0:4 * KD].rearrange("p (m k j) -> p m j k", k=KD, j=2)
                for j in range(2):
                    dve.tensor_tensor(mod_col[:, 1, j, :], cols[:, 0, j, :], bg_col[:, 0:KD], ALU.add)
                    link(dve.tensor_tensor(mod_col[:, 0, j, :], cols[:, 1, j, :], bg_col[:, KD:2 * KD], ALU.add))
                    i = dve.scalar_tensor_tensor(out=mod_col[:, 0, j, :], in0=mod_col[:, 0, j, :], scalar=1.0,
                                                 in1=g_col, op0=ALU.add, op1=ALU.mult)
                    i.then_inc(s["cols_done"], 1)
                dve.wait_ge(s["cols_done"], 2)
                first_order = order[0]
                CH = {"lat": 5, "ctx": 2}

                def prep(n, par, kind):
                    dve.wait_ge(s["rstd_done"], n + 1)
                    after(dve, s["xT_done"], 2 * n)
                    dve.tensor_scalar(xn[:, :], xt[:, :], stat[:, 2:3], ROOT, ALU.mult, ALU.mult).then_inc(s["xn_done"], 1)

                def turn(n, par, kind):
                    dve.wait_ge(s["xT_done"], 2 * n + 2)
                    after(dve, s["proj_done"], n - 1)
                    j = 1 if kind == "ctx" else 0
                    for k in range(KD // 2, KD):
                        i = dve.tensor_scalar(ht[par][:, k, :], psum[:, XT + 1, (k - KD // 2) * P:(k - KD // 2 + 1) * P],
                                              mod_col[:, 0, j, k:k + 1], mod_col[:, 1, j, k:k + 1], ALU.mult, ALU.add)
                    i.then_inc(s["hTb"], 1)

                def norm(n, par, kind):
                    if isinstance(n, int) and n == 0:
                        dve.wait_ge(s["tables_in"], 16 * 2)
                        dve.wait_ge(s["q_out"], 16)
                    if isinstance(n, int) and n == TS - 2:
                        dve.wait_ge(s["xn_done"], TS)
                        dve.tensor_copy(c_wide, c_sig[:, :, 0:1].broadcast_to([P, KD, P])).then_inc(s["wide_done"], 1)
                    c0 = 0 if kind == "lat" else QW
                    h0 = c0 // HD
                    nh = NH - h0
                    if kind == "ctx":
                        base = first_order + n * CH["ctx"]
                    else:
                        base = first_order + TC * CH["ctx"] + (n - TC) * CH["lat"]
                    count = [0]

                    def chain(ins):
                        count[0] += 1
                        ins.then_inc(s["dve_order"], 1)
                        dve.wait_ge(s["dve_order"], base + count[0])

                    def hv(ap):
                        return ap.rearrange("p (h d) -> p h d", d=HD)
                    dve.wait_ge(s["prj_done"], n + 1)
                    dve.wait_ge(s["pool_v"], n + 1)
                    dve.tensor_tensor(vs[:, n, :, 1, :], hv(prj[:, FW + QK:IN]), vs[:, n, :, 0, :].bitcast(F32), ALU.subtract)
                    if kind == "lat":
                        dve.tensor_tensor(hv(qkn[:, 0:QW]), hv(prj[:, FW:FW + QW]),
                                          g_qk[:, 0, :].unsqueeze(1).broadcast_to([P, NQ, HD]), ALU.mult)
                    dve.tensor_tensor(hv(qkn[:, QW:QK]), hv(prj[:, FW + QW:FW + QK]),
                                      g_qk[:, 1, :].unsqueeze(1).broadcast_to([P, NKV, HD]), ALU.mult).then_inc(s["v_done"], 1)
                    dve.wait_ge(s["pool_qk"], n + 1)
                    dve.tensor_reduce(ss[:, 0, h0:NH], hv(sq[:, c0:QK]), AX, ALU.add).then_inc(s["ss16_done"], 1)
                    dve.wait_ge(s["rstd16_done"], n + 1)
                    chain(dve.tensor_tensor(hv(qkn[:, c0:QK]), hv(qkn[:, c0:QK]),
                                            ss[:, 0, h0:NH].unsqueeze(2).broadcast_to([P, nh, HD]), ALU.mult))
                    v = qkn
                    if kind == "lat":
                        t = n - TC
                        q5 = qkn[:, :].rearrange("p (h g s d) -> p h g s d", g=2, s=2, d=HD // 4)
                        r5 = rot[:, :].rearrange("p (h g s d) -> p h g s d", g=2, s=2, d=HD // 4)
                        for half in range(2):
                            tab = rope[:, 1, t, :].rearrange("p (g s d) -> p g s d", g=2, s=2)[:, :, half, :]
                            i = dve.tensor_tensor(r5[:, :, :, half, :], q5[:, :, :, 1 - half, :],
                                                  tab.unsqueeze(1).broadcast_to([P, NH, 2, HD // 4]), ALU.mult)
                        chain(i)
                        chain(dve.tensor_tensor(hv(qkn[:, :]), hv(qkn[:, :]),
                                                rope[:, 0, t, :].unsqueeze(1).broadcast_to([P, NH, HD]), ALU.mult))
                        chain(dve.tensor_tensor(rot[:, :], rot[:, :], qkn[:, :], ALU.add))
                        v = rot
                    if kind == "ctx":
                        after(dve, s["qkt_done"], n)
                    else:
                        after(dve, s["qkt_done"], (n - TC) * QTG + TC)
                    if kind == "lat":
                        vq = hv(v[:, 0:QW]).unsqueeze(2).broadcast_to([P, NQ, 2, HD])
                        dve.tensor_copy(hlq[:, :, 0, :, :], vq)
                    chain(dve.tensor_copy(hlk[:, :, 0, :], hv(v[:, QW:QK])))
                    if kind == "lat":
                        dve.tensor_tensor(hlq[:, :, 1, :, :], vq, hlq[:, :, 0, :, :].bitcast(F32), ALU.subtract)
                    dve.tensor_tensor(hlk[:, :, 1, :], hv(v[:, QW:QK]), hlk[:, :, 0, :].bitcast(F32), ALU.subtract).then_inc(s["hl_done"], 1)
                    assert count[0] == CH[kind]

                def three(n, par, kind):
                    base = (n - TC) * QTG + TC
                    if kind == "ctx":
                        dve.wait_ge(s["qkt_done"], n + 1)
                        dve.tensor_copy(ks[:, 2:4, bass.ds(n * P, P)],
                                        psum[:, QT + 1, 0:2 * P].rearrange("p (h n) -> p h n", n=P)).then_inc(s["qkt_dve"], 4)
                        return
                    dve.wait_ge(s["q_out"], (n - TC + 1) * 16)
                    for j in range(1, QTG, 2):
                        dve.wait_ge(s["qkt_done"], base + j + 1)
                        dve.tensor_copy(qst[:, 2 * (j - 1):2 * j, :, :].rearrange("p h a n -> p (h a n)"),
                                        psum[:, QT + 1, :]).then_inc(s["qkt_dve"], 2 if j == QTG - 2 else 1)

                pipeline(dve, ((three, -2), (turn, 1), (norm, -1), (prep, 2)))
                dve.wait_ge(s["norm_row_in"], 32)
                end = first_order + TC * CH["ctx"] + TL * CH["lat"]
                order[0] = end
                for u in range(NR_UNITS):
                    r = rows[:, u * UM // D, u * UM % D:u * UM % D + UM]
                    dve.wait_ge(s["row_mm"], u + 1)
                    i = dve.tensor_tensor(r, psum[:, ROW_BANKS[u % 6], 0:UM], r, ALU.add).then_inc(s["row_done"], 1)
                dve.wait_ge(s["row_done"], NR_UNITS)
                dve.scalar_tensor_tensor(out=rows[:, SC2, :], in0=rows[:, SC2, :], scalar=1.0, in1=xn[:, :],
                                         op0=ALU.add, op1=ALU.mult).then_inc(s["row_done"], 1)
                dve.wait_ge(s["row_done"], NR_UNITS + 1)
                dve.tensor_scalar(rows[:, SC2, :], rows[:, SC2, :], ROOT, None, ALU.mult)

            @block.tensor
            def _(pe):
                pe.wait_ge(s["ident_done"], 1)
                pe.wait_ge(s["small_in"], 16 * 4)
                pe.transpose(psum[:, 6, 0:5 * KD], vec[:, :], ident[0:5 * KD, 0:5 * KD]).then_inc(s["vec_t"], 1)
                pe.wait_ge(s["silu_done"], 1)
                for u in range(NC_UNITS):
                    pe.wait_ge(unit_in[u % 2], 16 * (u // 2 + 1))
                    if u >= 2:
                        pe.wait_ge(s["c_row_done"], u - 1)
                    for k in range(KD):
                        i = pe.matmul(psum[0:2, u % 2, 0:UM], c_sig[:, k, :], unit[u % 2][:, k, :],
                                      start=(k == 0), stop=(k == KD - 1))
                    i.then_inc(s["unit_used"], 1)
                pe.wait_ge(s["c_row_done"], NC_UNITS)
                for b in range(2 * KD):
                    i = pe.transpose(psum[:, 7, 2 * b:2 * b + 2], c_rows[:, b * P:(b + 1) * P], ident[0:2, 0:2])
                i.then_inc(s["c_col_done"], 1)

                def turn(n, par, kind):
                    pe.wait_ge(s["xn_done"], n + 1)
                    after(pe, s["hTa"], n)
                    after(pe, s["hTb"], n)
                    for k in range(KD):
                        i = pe.transpose(psum[:, XT + k // 4, (k % 4) * P:(k % 4 + 1) * P], xn[:, k * P:(k + 1) * P], ident[:, :])
                        if k % 4 == 3:
                            i.then_inc(s["xT_done"], 1)

                def two(n, par, kind):
                    pe.wait_ge(s["hTa"], n + 1)
                    pe.wait_ge(s["hTb"], n + 1)
                    if isinstance(n, int) and n in (0, TC):
                        pe.wait_ge(s["win_kv_in" if n == 0 else "win_in"], 16 if n == 0 else 32)
                    after(pe, s["prj_done"], n)
                    for c in ((1, 0, 2) if kind == "lat" else (2,)):
                        for k in range(KD):
                            i = pe.matmul(psum[:, PJ + c, :], ht[par][:, k, :], win[:, k, c * 512:(c + 1) * 512],
                                          start=(k == 0), stop=(k == KD - 1))
                    i.then_inc(s["proj_done"], 1)

                def mod_row(u):
                    if u == 0:
                        pe.wait_ge(s["wide_done"], 1)
                        pe.wait_ge(s["hTa"], TS)
                        pe.wait_ge(s["hTb"], TS)
                    if u == 3:
                        pe.wait_ge(s["prj_done"], TS)
                    pe.wait_ge(row_in[u % 8], 16 * (u // 8 + 1))
                    if u >= 6:
                        pe.wait_ge(s["row_done"], u - 5)
                    for k in range(KD):
                        i = pe.matmul(psum[:, ROW_BANKS[u % 6], 0:UM], c_wide[:, k, :], row_unit[u % 8][:, k, :],
                                      start=(k == 0), stop=(k == KD - 1))
                    i.then_inc(s["row_mm"], 1)

                def three(n, par, kind):
                    if isinstance(n, int) and n == TS - 1:
                        for u in range(EARLY):
                            mod_row(u)
                    pe.wait_ge(s["hl_done"], n + 1)
                    q32 = hlq[:, :, :, :, :].rearrange("p h a b d -> p (h a b d)").bitcast(F32)
                    k32 = hlk[:, :, :, :].rearrange("p h a d -> p (h a d)").bitcast(F32)
                    for j in range(QTG if kind == "lat" else 1):
                        if j == 0:
                            after(pe, s["qkt_act"], n * 4)
                            after(pe, s["qkt_dve"], n * 4)
                        elif j % 2 == 0:
                            pe.wait_ge(s["qkt_act"], n * 4 + j // 2)
                        elif j > 1:
                            pe.wait_ge(s["qkt_dve"], n * 4 + j // 2)
                        for b in range(4):
                            if j == 0:
                                src = k32[:, b * P:(b + 1) * P]
                            else:
                                src = q32[:, (4 * (j - 1) + b) * P:(4 * (j - 1) + b + 1) * P]
                            bank, col = (QT + b // 2, b % 2) if kind == "ctx" else (QT + j % 2, b)
                            i = pe.transpose(psum[:, bank, col * P:(col + 1) * P], src, ident[:, :])
                        i.then_inc(s["qkt_done"], 1)

                pipeline(pe, ((three, -2), (turn, 1), (two, 0)))
                for u in range(EARLY, NR_UNITS):
                    mod_row(u)
        A.close()
        nc_phase_b(nc, ctx, sem, sb, a, K, psum, ident, ones, rows, aff, eps_c, ks, vs, f_tok, y_t,
                   q_d, h2_d, acc_d, x_d)
        K.close()
        nc_phase_m(nc, ctx, sem, sb, a, psum, ident, rows, aff, eps_c, h2_d, acc_d, w_gate, w_up, w_down, out_d)


def after(eng, sem_, v):
    if not (isinstance(v, int) and v <= 0):
        eng.wait_ge(sem_, v)


def nc_phase_b(nc, ctx, sem, sb, a, K, psum, ident, ones, rows, aff, eps_c, ks, vs, f_tok, y_t,
               q_d, h2_d, acc_d, x_d):
    G1, SH2, SC2, G2 = range(4)

    F = ExitStack()
    dft = sb("dft", [P, 2, TL, HALF + 1], F32, F)
    chan = sb("chan", [P, 3, P], F32, F)
    wf = sb("wf", [P, 2, P], F32, F)
    ab = sb("ab", [P, 2, 3, P], F32, F)
    gt = sb("gt", [P, 2, 2, HALF + 1], F32, F)
    s = {n: sem("f_" + n) for n in ("wf_zero", "chan_in", "ab_mm", "ab_done", "g_mm", "g_done", "y_mm", "y_done")}
    dft_in = [sem(f"f_dft_in{i}") for i in range(4)]
    with nc.Block() as block:
        @block.sync
        def _(sp):
            for i in range(2):
                for h in range(2):
                    sp.dma_start(dft[:, i, 4 * h:4 * h + 4, 0:HALF],
                                 a["dft"][i].rearrange("(t p) m -> p t m", p=P)[:, 4 * h:4 * h + 4, :]).then_inc(dft_in[2 * i + h], 16)

        @block.vector
        def _(dve):
            dve.memset(wf[:, :, :], 0.0).then_inc(s["wf_zero"], 1)
            for c in range(2):
                dve.wait_ge(s["ab_mm"], c + 1)
                dve.tensor_copy(ab[:, c, :, :].rearrange("p a n -> p (a n)"), psum[:, 4 + c, 0:3 * P]).then_inc(s["ab_done"], 1)
            dve.wait_ge(s["g_mm"], 4)
            dve.tensor_copy(gt[:, :, :, HALF - 1], psum[:, 6, 0:4].rearrange("p (c i) -> p c i", i=2)).then_inc(s["g_done"], 1)
            for c in range(2):
                dve.wait_ge(s["y_mm"], 3 * c + 2)
                dve.tensor_copy(y_t[:, c, N - 1:HALF - 1:-1], psum[:, 2 * c + 1, 0:HALF - 2]).then_inc(s["y_done"], 1)
            dve.wait_ge(s["y_mm"], 6)
            dve.tensor_copy(y_t[:, :, HALF - 1], psum[:, 7, 0:2]).then_inc(s["y_done"], 1)

        @block.scalar
        def _(act):
            act.dma_start(chan[:, :, :], a["chan"].rearrange("a p n -> p a n")).then_inc(s["chan_in"], 16)
            act.wait_ge(s["wf_zero"], 1)
            for g in range(FG):
                h = g % 2
                act.dma_start(wf[h * FD:(h + 1) * FD, g // 2, h * FD:(h + 1) * FD], a["w_four"][0, g]).then_inc(s["chan_in"], 16)
            for i in range(2):
                for c in range(2):
                    act.wait_ge(s["g_mm"], 2 * i + c + 1)
                    act.activation(gt[:, c, i, 0:HALF - 1], psum[:, 2 * c + i, :], ACT.Copy).then_inc(s["g_done"], 1)
            for c in range(2):
                act.wait_ge(s["y_mm"], 3 * c + 1)
                act.activation(y_t[:, c, 0:HALF - 1], psum[:, 2 * c, :], ACT.Copy).then_inc(s["y_done"], 1)

        @block.tensor
        def _(pe):
            for i in range(2):
                for c in range(2):
                    for t in range(TL):
                        if c == 0 and t % 4 == 0:
                            pe.wait_ge(dft_in[2 * i + t // 4], 16)
                        pe.matmul(psum[:, 2 * c + i, :], f_tok[:, t, c * P:(c + 1) * P], dft[:, i, t, 0:512],
                                  start=(t == 0), stop=(t == TL - 1))
                    for t in range(TL):
                        m = pe.matmul(psum[:, 6, 2 * c + i:2 * c + i + 1], f_tok[:, t, c * P:(c + 1) * P], dft[:, i, t, 512:513],
                                      start=(t == 0), stop=(t == TL - 1))
                    m.then_inc(s["g_mm"], 1)
            pe.wait_ge(s["chan_in"], 16 * 5)
            for c in range(2):
                for j in range(3):
                    i = pe.matmul(psum[:, 4 + c, j * P:(j + 1) * P], chan[:, j, :], wf[:, c, :], start=True, stop=True)
                i.then_inc(s["ab_mm"], 1)
            pe.wait_ge(s["ab_done"], 2)
            pe.wait_ge(s["g_done"], 5)
            for c in range(2):
                for (bank, lo, hi, b) in ((2 * c, 0, 512, 1), (2 * c + 1, 1, 512, 2), (7, 512, 513, 1)):
                    o = psum[:, bank, 0:hi - lo] if bank < 7 else psum[:, 7, c:c + 1]
                    pe.matmul(o, ab[:, c, 0, :], gt[:, c, 0, lo:hi], start=True, stop=False)
                    pe.matmul(o, ab[:, c, b, :], gt[:, c, 1, lo:hi], start=False, stop=True).then_inc(s["y_mm"], 1)
    F.close()

    B = ExitStack()
    wout = sb("wout", [P, KD, D], F32, B)
    wrt = sb("wrt", [P, KD, E], F32, B)
    qt = sb("qt", [P, NQ, 2, P], F32R, B)
    pr = [sb(f"pr{i}", [P, KEYS], F32, B) for i in range(6)]
    pth = sb("pth", [P, 4, REP * P], F32R, B)
    ptl = sb("ptl", [P, 4, REP * P], F32R, B)
    diag = [sb(f"diag{i}", [P, REP, P], F32, B) for i in range(2)]
    rbc = sb("rbc", [P, REP * P], F32, B)
    oth = sb("oth", [P, REP * P], F32, B)
    osum = sb("osum", [P, REP * P], F32, B)
    mix = sb("mix", [P, KD, P], F32, B)
    mx = sb("mx", [P, NQ, 4], F32, B)
    nb = sb("nb", [P, NQ], F32, B)
    den = sb("den", [P, NQ, 4], F32, B)
    rden = sb("rden", [P, NQ], F32, B)
    xr = sb("xr", [P, D], F32, B)
    x2 = sb("x2", [P, D], F32, B)
    h2 = sb("h2", [P, D], F32, B)
    junk2 = sb("junk2", [P, D], F32, B)
    h2t = sb("h2t", [P, KD, P], F32, B)
    st2 = sb("st2", [P, 4], F32, B)
    lg = sb("lg", [P, 4, E], F32, B)
    s = {n: sem("b_" + n) for n in (
        "w_in", "s_done", "nb_done", "exp_done", "t_done", "hi_done", "lo_done", "pv_done", "osum_done",
        "rden_done", "diag_done", "misc_mm", "misc_free", "oth_done", "mix_done", "ymix_done", "x_in",
        "x2_done", "ss_done", "rstd_done", "mean", "h2a", "h2b", "h2_out", "x2_out", "neg_done", "lexp", 
        "dve_order", "op_sum")}
    q_in = [sem(f"b_q_in{g}") for g in range(NKV)]
    CH = [(0, 512), (512, 1024), (1024, KEYS)]
    NCH = len(CH)
    NS = NCH * NQ
    KT = TS
    NT = KT * NKV
    PTB, OB, MB = 4, 6, 7
    MISC0 = 2

    def misc(t, j):
        return j if isinstance(t, int) and t == 0 else MISC0 + 10 * (t - 1) + j

    def schedule(eng_step, eng):
        eng_step(0, False, True)
        eng_step(1, True, True)
        with eng.Fori(2, TL) as t:
            eng_step(t, True, True)
        eng_step(TL, True, False)

    def use_numbers(prev, cur):
        names = []
        if prev:
            names += ["R0", "R3", "OP0", "OP1"]
        if cur:
            names += ["R6"]
        if prev:
            names += ["HT0"]
        if cur:
            names += ["R9"]
        if prev:
            names += ["HT1", "RT", "AF"]
        return {n: i for i, n in enumerate(names)}

    def flushes(prev, cur):
        return {sl: sl // 3 - 2 for sl in (0, 3, 6, 9) if (prev if sl < 6 else cur)}

    def items(i, prev, cur):
        g = i // 3 - 1
        if (g < 0 and not prev) or (g >= 0 and not cur):
            return []
        lo, hi = ((0, 4), (4, 7), (7, 10))[i % 3]
        return [KT * g + k for k in range(lo, hi)]

    def behind(t, i, prev, cur):
        if i == 0:
            return (t - 1, NQ - 1) if prev else None
        return (t, i - 1) if cur else None

    with nc.Block() as block:
        @block.sync
        def _(sp):
            def queries(t):
                src = q_d[t].rearrange("p (g n) -> p g n", g=NKV)
                for g in range(NKV):
                    src_g = src[:, g, :]
                    if not (isinstance(t, int) and t == 0):
                        sp.wait_ge(s["s_done"], NS * (t - 1) + NCH * REP * (g + 1))
                    sp.dma_start(qt[:, REP * g:REP * (g + 1), :, :].rearrange("p h a n -> p (h a n)").bitcast(F32), src_g).then_inc(q_in[g], 16)
            queries(0)
            sp.dma_start(wrt[:, :, :], a["w_router"][0].rearrange("(k p) e -> p k e", p=P)).then_inc(s["w_in"], 16)
            wo = a["w_out"][0]
            for g in range(NKV):
                half = (g % 2) * HD
                sp.dma_start(wout[half:half + HD, 3 * (g // 2):3 * (g // 2) + REP, :],
                             wo[FW + g * REP * HD:FW + (g + 1) * REP * HD, :].rearrange("(r p) n -> p r n", p=HD)).then_inc(s["w_in"], 16)
            sp.dma_start(wout[:, 6:8, :], wo[0:FW, :].rearrange("(k p) n -> p k n", p=P)).then_inc(s["w_in"], 16)

            def step(t, prev, cur):
                if cur and prev:
                    queries(t)
                if prev:
                    after(sp, s["x2_done"], (t - 1) * 2)
                    sp.dma_start(xr[:, :], x_d[t - 1]).then_inc(s["x_in"], 16)
                    sp.wait_ge(s["x2_done"], t * 2)
                    sp.dma_start(acc_d.rearrange("(t p) d -> t p d", p=P)[t - 1], x2[:, :]).then_inc(s["x2_out"], 16)
                    sp.wait_ge(s["h2b"], t)
                    sp.dma_start(h2_d.rearrange("(t p) d -> t p d", p=P)[t - 1], h2[:, :]).then_inc(s["h2_out"], 16)
            schedule(step, sp)
            sp.wait_ge(s["x2_out"], 16 * TL)
            sp.wait_ge(s["h2_out"], 16 * TL)

        @block.gpsimd
        def _(pool):
            def step(t, prev, cur):
                use = use_numbers(prev, cur)
                fl = flushes(prev, cur)
                if prev:
                    after(pool, s["x2_done"], 2 * (t - 1))
                    pool.tensor_copy(mix[:, 6:8, :], y_t[:, :, bass.ds((t - 1) * P, P)]).then_inc(s["ymix_done"], 1)
                for i in range(NQ):
                    if i in fl:
                        G = 4 * t + fl[i]
                        par, g = fl[i] % 2, fl[i] % 4
                        h = slice(par * HD, (par + 1) * HD)
                        pool.wait_ge(s["osum_done"], G + 1)
                        pool.wait_ge(s["misc_free"], misc(t, use[f"R{i}"]) + 1)
                        pool.tensor_tensor(mix[h, 3 * (g // 2):3 * (g // 2) + REP, :].rearrange("p r n -> p (r n)"),
                                           osum[h, :], rbc[h, :], ALU.mult).then_inc(s["mix_done"], 1)
                        pool.wait_ge(s["mix_done"], G + 1)
                    if prev and i == 8:
                        pool.wait_ge(s["h2a"], t)
                        pool.tensor_tensor(h2[:, :], h2[:, :], rows[:, SH2, :], ALU.add).then_inc(s["h2b"], 1)
                    if i % REP == 0 and behind(t, i, prev, cur):
                        tb, h = behind(t, i, prev, cur)
                        g = h // REP
                        of_tile = use if i else use_numbers(not (isinstance(t, int) and t == 1), True)
                        if f"R{REP * g}" in of_tile:
                            pool.wait_ge(s["misc_mm"], misc(tb, of_tile[f"R{REP * g}"]) + 1)
                        pool.wait_ge(s["rden_done"], NKV * tb + g + 1)
                        pool.tensor_tensor(diag[g % 2][:, :, :], ident[:, :].unsqueeze(1).broadcast_to([P, REP, P]),
                                           rden[:, REP * g:REP * g + REP].unsqueeze(2).broadcast_to([P, REP, P]), ALU.mult).then_inc(s["diag_done"], 1)
                    if prev and i == 6:
                        pool.wait_ge(s["ss_done"], t)
                        pool.tensor_tensor(st2[:, 1:2], st2[:, 0:1], eps_c[:, 1:2], ALU.add).then_inc(s["mean"], 1)
                        pool.wait_ge(s["mean"], t)
                        pool.tensor_tensor(st2[:, 2:3], st2[:, 1:2], eps_c[:, 0:1], ALU.pow).then_inc(s["rstd_done"], 1)
            schedule(step, pool)

        @block.scalar
        def _(act):
            def step(t, prev, cur):
                use = use_numbers(prev, cur)
                fl = flushes(prev, cur)
                for i in range(NQ):
                    its = items(i, prev, cur)
                    ex = behind(t, i, prev, cur)
                    for c in range(NCH + 1):
                        if ex and c < NCH:
                            tb, h = ex
                            lo, hi = CH[c]
                            if c == 0:
                                act.wait_ge(s["nb_done"], NQ * tb + h + 1)
                                g = h // 3
                                if not (isinstance(tb, int) and tb == 0 and g < 2):
                                    act.wait_ge(s["t_done"], KT * (4 * tb + g - 1))
                            act.activation(pr[(h // 3 % 2) * 3 + h % 3][:, lo:hi], psum[:, (NCH * h + c) % 4, 0:hi - lo], ACT.Exp,
                                           bias=nb[:, h:h + 1], scale=SCALE, accum_out=den[:, h, c:c + 1]).then_inc(s["exp_done"], 1)
                        if c == 0 and i in fl:
                            G = 4 * t + fl[i]
                            act.wait_ge(s["pv_done"], KT * (G + 1))
                            after(act, s["osum_done"], G)
                            if fl[i] % 2 == 0:
                                act.activation(oth[0:HD, :], psum[HD:P, OB, 0:REP * P], ACT.Copy).then_inc(s["oth_done"], 1)
                            else:
                                act.activation(oth[HD:P, :], psum[0:HD, OB, 0:REP * P], ACT.Copy).then_inc(s["oth_done"], 1)
                        if c < len(its):
                            k = its[c]
                            n = NT * t + k
                            act.wait_ge(s["t_done"], n + 1)
                            if not (isinstance(t, int) and t == 0 and k < 4):
                                act.wait_ge(s["pv_done"], n - 3)
                            act.activation(pth[:, k % 4, :], psum[:, PTB + k % 2, 0:REP * P], ACT.Copy).then_inc(s["hi_done"], 1)
                        if c == 0 and i in fl:
                            act.wait_ge(s["misc_mm"], misc(t, use[f"R{i}"]) + 1)
                            after(act, s["mix_done"], G)
                            act.activation(rbc[:, :], psum[:, MB, 0:REP * P], ACT.Copy).then_inc(s["misc_free"], 1)
                    if prev and i == 8:
                        act.wait_ge(s["misc_mm"], misc(t, use["HT0"]) + 1)
                        after(act, s["neg_done"], t - 1)
                        act.activation(h2t[:, 0:4, :].rearrange("p k n -> p (k n)"), psum[:, MB, :], ACT.Copy).then_inc(s["misc_free"], 1)
                    if prev and i == 9:
                        act.wait_ge(s["misc_mm"], misc(t, use["HT1"]) + 1)
                        act.activation(h2t[:, 4:8, :].rearrange("p k n -> p (k n)"), psum[:, MB, :], ACT.Copy).then_inc(s["misc_free"], 1)
                    if prev and i == 6:
                        act.wait_ge(s["x2_done"], 2 * t)
                        after(act, s["rstd_done"], t - 1)
                        act.activation(junk2[:, :], x2[:, :], ACT.Square, accum_out=st2[:, 0:1]).then_inc(s["ss_done"], 1)
                    if prev and i == 10:
                        act.wait_ge(s["neg_done"], t)
                        act.activation(lg[:, 1, :], psum[:, MB, 0:E], ACT.Exp, bias=st2[:, 3:4], scale=1.0,
                                       accum_out=lg[:, 2, 0:1]).then_inc(s["lexp"], 1)
                    if prev and i == 11:
                        act.wait_ge(s["misc_mm"], misc(t, use["AF"]) + 1)
                        act.activation(aff[:, bass.ds((t - 1) * P, P)], psum[0:E, MB, 0:P], ACT.Copy).then_inc(s["misc_free"], 1)
            schedule(step, act)

        @block.vector
        def _(dve):
            def step(t, prev, cur):
                use = use_numbers(prev, cur)
                fl = flushes(prev, cur)
                PER0, PER = 2 * NQ, 2 * NQ + 2
                base = 0 if isinstance(t, int) and t == 0 else PER0 + (t - 1) * PER
                count = [0]

                def chain(ins):
                    count[0] += 1
                    ins.then_inc(s["dve_order"], 1)
                    dve.wait_ge(s["dve_order"], base + count[0])
                for i in range(NQ):
                    its = items(i, prev, cur)
                    for c in range(NCH + 1):
                        if cur and c < NCH:
                            lo, hi = CH[c]
                            dve.wait_ge(s["s_done"], NS * t + NCH * i + c + 1)
                            ins = dve.tensor_reduce(mx[:, i, c:c + 1], psum[:, (NCH * i + c) % 4, 0:hi - lo], AX, ALU.max)
                        if cur and c == NCH - 1:
                            chain(ins)
                            chain(dve.tensor_reduce(mx[:, i, 3:4], mx[:, i, 0:3], AX, ALU.max))
                            dve.tensor_scalar(nb[:, i:i + 1], mx[:, i, 3:4], -SCALE, None, ALU.mult).then_inc(s["nb_done"], 1)
                        if c < len(its):
                            k = its[c]
                            dve.wait_ge(s["hi_done"], NT * t + k + 1)
                            dve.tensor_tensor(ptl[:, k % 4, :], psum[:, PTB + k % 2, 0:REP * P], pth[:, k % 4, :].bitcast(F32),
                                              ALU.subtract).then_inc(s["lo_done"], 1)
                        if c == 0 and i in fl:
                            G = 4 * t + fl[i]
                            par = fl[i] % 2
                            h = slice(par * HD, (par + 1) * HD)
                            dve.wait_ge(s["oth_done"], G + 1)
                            after(dve, s["mix_done"], G)
                            dve.tensor_tensor(osum[h, :], psum[h, OB, 0:REP * P], oth[h, :], ALU.add).then_inc(s["osum_done"], 1)
                    if i % REP == 0 and behind(t, i, prev, cur):
                        tb, h = behind(t, i, prev, cur)
                        g = h // REP
                        hs = slice(REP * g, REP * g + REP)
                        dve.wait_ge(s["exp_done"], NS * tb + NCH * (h + 1))
                        ins = dve.tensor_reduce(den[:, hs, 3], den[:, hs, 0:3], AX, ALU.add)
                        if not (isinstance(tb, int) and tb == 0):
                            dve.wait_ge(s["diag_done"], NKV * (tb - 1) + g + 1)
                        ins.then_inc(s["op_sum"], 1)
                        dve.wait_ge(s["op_sum"], NKV * tb + g + 1)
                        dve.reciprocal(rden[:, hs], den[:, hs, 3]).then_inc(s["rden_done"], 1)
                    if prev and i in (4, 5):
                        j = i - 4
                        c = slice(j * 512, (j + 1) * 512)
                        dve.wait_ge(s["misc_mm"], misc(t, use[f"OP{j}"]) + 1)
                        if j == 0:
                            dve.wait_ge(s["x_in"], 16 * t)
                            after(dve, s["x2_out"], 16 * (t - 1))
                            after(dve, s["h2a"], t - 1)
                        dve.tensor_tensor(x2[:, c], psum[:, MB, :], rows[:, G1, c], ALU.mult).then_inc(s["misc_free"], 1)
                        dve.wait_ge(s["misc_free"], misc(t, use[f"OP{j}"]) + 1)
                        dve.tensor_tensor(x2[:, c], x2[:, c], xr[:, c], ALU.add).then_inc(s["x2_done"], 1)
                    if prev and i == 7:
                        dve.wait_ge(s["rstd_done"], t)
                        after(dve, s["h2_out"], 16 * (t - 1))
                        dve.scalar_tensor_tensor(out=h2[:, :], in0=x2[:, :], scalar=st2[:, 2:3], in1=rows[:, SC2, :],
                                                 op0=ALU.mult, op1=ALU.mult).then_inc(s["h2a"], 1)
                    if prev and i == 10:
                        dve.wait_ge(s["misc_mm"], misc(t, use["RT"]) + 1)
                        chain(dve.tensor_reduce(lg[:, 2, 1:2], psum[:, MB, 0:E], AX, ALU.max))
                        dve.tensor_scalar(st2[:, 3:4], lg[:, 2, 1:2], -1.0, None, ALU.mult).then_inc(s["neg_done"], 1)
                    if prev and i == 11:
                        dve.wait_ge(s["lexp"], t)
                        chain(dve.reciprocal(lg[:, 2, 2:3], lg[:, 2, 0:1]))
                        dve.tensor_scalar(lg[:, 0, :], lg[:, 1, :], lg[:, 2, 2:3], None, ALU.mult).then_inc(s["misc_free"], 1)
            schedule(step, dve)

        @block.tensor
        def _(pe):
            def step(t, prev, cur):
                use = use_numbers(prev, cur)
                fl = flushes(prev, cur)

                def times(k):
                    n = NT * t + k
                    g, kt = k // KT, k % KT
                    pe.wait_ge(s["lo_done"], n + 1)
                    if kt == 0:
                        after(pe, s["osum_done"], 4 * t + g)
                    v = vs[:, kt, g % 4, :, :].rearrange("p a d -> p (a d)")
                    pe.matmul(psum[:, OB, 0:REP * P], v, pth[:, k % 4, :], start=(kt == 0), stop=False)
                    ins = pe.matmul(psum[:, OB, 0:REP * P], v, ptl[:, k % 4, :], start=False, stop=(kt == KT - 1))
                    ins.then_inc(s["pv_done"], 1)

                def misc_free(name):
                    after(pe, s["misc_free"], misc(t, use[name]))

                for i in range(NQ):
                    its = items(i, prev, cur)
                    for c in range(NCH + 1):
                        if cur and c < NCH:
                            lo, hi = CH[c]
                            n = NCH * i + c
                            if c == 0 and i % REP == 0:
                                pe.wait_ge(q_in[i // REP], 16 * (t + 1))
                            if not (isinstance(t, int) and t == 0 and n < 4):
                                pe.wait_ge(s["exp_done"], NS * t + n - 3)
                            o = psum[:, n % 4, 0:hi - lo]
                            pe.matmul(o, qt[:, i, 0, :], ks[:, i // 3, lo:hi], start=True, stop=False)
                            pe.matmul(o, qt[:, i, 1, :], ks[:, i // 3, lo:hi], start=False, stop=True).then_inc(s["s_done"], 1)
                        if c == 0 and i in fl:
                            k0 = KT * (fl[i] + 1)
                            times(k0 - 2)
                            times(k0 - 1)
                        if c < len(its):
                            k = its[c]
                            n = NT * t + k
                            g, kt = k // KT, k % KT
                            if kt in (0, 4, 8):
                                pe.wait_ge(s["exp_done"], 9 * (4 * t + g) + 7 + kt // 4)
                            if not (isinstance(t, int) and t == 0 and k < 2):
                                pe.wait_ge(s["lo_done"], n - 1)
                            for r in range(REP):
                                ins = pe.transpose(psum[:, PTB + k % 2, r * P:(r + 1) * P],
                                                   pr[(g % 2) * 3 + r][:, kt * P:(kt + 1) * P], ident[:, :])
                            ins.then_inc(s["t_done"], 1)
                            if kt >= 2:
                                times(k - 2)
                        if c == 0 and i in fl:
                            G = 4 * t + fl[i]
                            pe.wait_ge(s["diag_done"], G + 1)
                            misc_free(f"R{i}")
                            pe.matmul(psum[:, MB, 0:REP * P], ones[:, :], diag[fl[i] % 2][:, :, :].rearrange("p r n -> p (r n)"),
                                      start=True, stop=True).then_inc(s["misc_mm"], 1)
                    if prev and i in (4, 5):
                        j = i - 4
                        if isinstance(t, int) and t == 1 and j == 0:
                            pe.wait_ge(s["w_in"], 16 * 6)
                        pe.wait_ge(s["mix_done"], 4 * t)
                        pe.wait_ge(s["ymix_done"], t)
                        misc_free(f"OP{j}")
                        for k in range(KD):
                            ins = pe.matmul(psum[:, MB, :], mix[:, k, :], wout[:, k, j * 512:(j + 1) * 512],
                                            start=(k == 0), stop=(k == KD - 1))
                        ins.then_inc(s["misc_mm"], 1)
                    if prev and i in (8, 9):
                        j = i - 8
                        pe.wait_ge(s["h2b"], t)
                        misc_free(f"HT{j}")
                        for k in range(4):
                            ins = pe.transpose(psum[:, MB, k * P:(k + 1) * P], h2[:, (4 * j + k) * P:(4 * j + k + 1) * P], ident[:, :])
                        ins.then_inc(s["misc_mm"], 1)
                    if prev and i == 10:
                        misc_free("RT")
                        for k in range(KD):
                            ins = pe.matmul(psum[:, MB, 0:E], h2t[:, k, :], wrt[:, k, :], start=(k == 0), stop=(k == KD - 1))
                        ins.then_inc(s["misc_mm"], 1)
                    if prev and i == 11:
                        misc_free("AF")
                        pe.transpose(psum[0:E, MB, 0:P], lg[:, 0, :], ident[:, :]).then_inc(s["misc_mm"], 1)
            schedule(step, pe)
    B.close()


def nc_phase_m(nc, ctx, sem, sb, a, psum, ident, rows, aff, eps_c, h2_d, acc_d, w_gate, w_up, w_down, out_d):
    G1, SH2, SC2, G2 = range(4)

    M = ExitStack()
    NU = 4
    CH = KD * UC // 2
    NJ = DE // UC
    unit = [sb(f"munit{i}", [P, KD * UC], F32, M) for i in range(NU)]
    H2 = 32
    EH = H2 + E
    NH2 = N // 2
    cand = sb("cand", [EH, NH2], F32, M)
    top = sb("top", [EH, CAP], F32, M)
    topi = sb("topi", [EH, CAP], U32, M)
    topf = sb("topf", [EH, CAP], F32, M)
    rtop, rtopf = (sb(n, [EH, CAP], F32, M) for n in ("rtop", "rtopf"))
    merge = sb("merge", [P, 5, E], F32, M)
    icol = sb("icol", [P, E], U32, M)
    gcol = sb("gcol", [P, E], F32, M)
    idx_g = sb("idx_g", [P, 1], U32, M)
    idx_s = sb("idx_s", [P, 1], U32, M)
    gate_s = sb("gate_s", [P, 1], F32, M)
    xe = sb("xe", [P, D], F32, M)
    x_hi, x_lo = (sb(f"x_{n}", [P, KD, P], F32R, M) for n in ("hi", "lo"))
    w_hi, w_lo = ([[sb(f"w_{n}{i}{c}", [P, CH], F32R, M) for c in range(2)] for i in range(2)] for n in ("hi", "lo"))
    sil = [sb(f"sil{i}", [P, UC], F32, M) for i in range(2)]
    hid = [sb(f"hid{i}", [P, UC], F32, M) for i in range(2)]
    h_hi, h_lo = ([sb(f"h_{n}{i}", [P, 2, P], F32R, M) for i in range(2)] for n in ("hi", "lo"))
    hidt = [sb(f"hidt{i}", [P, 2, P], F32, M) for i in range(2)]
    d_hi, d_lo = ([sb(f"d_{n}{i}", [P, D], F32R, M) for i in range(2)] for n in ("hi", "lo"))
    ysc = sb("ysc", [P, D], F32, M)
    carry = sb("carry", [P, 2], F32, M)
    fgain = sb("fgain", [P, D], F32, M)
    xa = [unit[1 + t // 4][:, t % 4 * D:(t % 4 + 1) * D] for t in range(TL)]
    sqj = unit[3][:, 0:D]
    fst = sb("fst", [P, TL, 3], F32, M)
    s = {n: sem("m_" + n) for n in (
        "top_order", "cand_zero", "cand_done", "merged", "carried", "top_done", "top_t", "cols_done", "idx_g", "x_in", "x_mm", "x_a", "x_b",
        "gate_mm", "up_mm", "sil_done", "hid_done", "ht_mm", "ht_done", "down_mm", "y_done", "y_out", "sel_done",
        "hi_done", "lo_done", "d_hi_done", "d_lo_done", "h_lo_done", "fg_in", "a_done", "mean", "rstd", "norm_done")}
    unit_in = [sem(f"munit_in{i}") for i in range(NU)]
    NX = TL
    xa_in = [sem(f"xa_in{i}") for i in range(NX)]
    xa_out = [sem(f"xa_out{i}") for i in range(NX)]
    Y, HB, XB = 4, 6, 7

    def arrived(e, k):
        v = 3 * NJ // NU * e + k // NU + 1
        return 16 * (v - 1 if k % NU == 2 and not (isinstance(e, int) and e == 0 and k <= 2) else v)

    with nc.Block() as block:
        @block.sync
        def _(sp):
            def load(e, k, src, cols):
                dst = unit[k % NU][:, :].rearrange("p (k n) -> p k n", n=cols)
                if k >= NU or not (isinstance(e, int) and e == 0):
                    le, lk = (e, k - NU) if k >= NU else (e - 1, k + 3 * NJ - NU)
                    if lk % 3 == 2:
                        after(sp, s["down_mm"], NJ * le + lk // 3)
                    else:
                        sp.wait_ge(s["lo_done"], 4 * (NJ * le + lk // 3) + 2 * (lk % 3) + 2)
                sp.dma_start(dst, src).then_inc(unit_in[k % NU], 16)

            def expert(e, first):
                for j in range(NJ):
                    c = slice(j * UC, (j + 1) * UC)
                    load(e, 3 * j, w_gate[e][:, :, c], UC)
                    load(e, 3 * j + 1, w_up[e][:, :, c], UC)
                    if j > 0:
                        load(e, 3 * j + 2, w_down[e][:, 4 * (j - 1):4 * j, :], D)
                    elif not first:
                        load(e, 2, w_down[e - 1][:, 4 * (NJ - 1):4 * NJ, :], D)
            sp.dma_start(fgain[:, :], a["final_norm_g"].partition_broadcast(P)).then_inc(s["fg_in"], 16)
            expert(0, True)
            with sp.Fori(1, E) as e:
                expert(e, False)
            load(E, 0, w_down[E - 1][:, 4 * (NJ - 1):4 * NJ, :], D)
            sp.wait_ge(s["y_out"], 16 * E)
            for t in range(TL):
                if t >= NX:
                    sp.wait_ge(xa_out[t % NX], 16 * (t // NX))
                sp.dma_start(xa[t % NX][:, :], acc_d.rearrange("(t p) d -> t p d", p=P)[t]).then_inc(xa_in[t % NX], 16)

        @block.gpsimd
        def _(pool):
            pool.memset(cand[:, :], 0.0).then_inc(s["cand_zero"], 1)
            pool.wait_ge(s["cols_done"], 2)

            pool.memset(carry[:, :], 0.0).then_inc(s["carried"], 1)

            def carrier(n):
                pool.wait_ge(s["carried"], n + 1)
                pool.tensor_tensor(carry[:, 1:2], carry[:, 0:1], carry[:, 0:1], ALU.add).then_inc(s["carried"], 1)

            def gather(e):
                after(pool, s["x_in"], 16 * e)
                pool.tensor_copy(idx_g[:, :], icol[:, bass.ds(e, 1)]).then_inc(s["idx_g"], 1)
                pool.wait_ge(s["idx_g"], e + 1)
                after(pool, s["x_mm"], 2 * e)
                carrier(2 * e - 1 if not (isinstance(e, int) and e == 0) else 0)
                pool.indirect_dma_start(out=xe[:, :], out_offset=None, in_=h2_d,
                                        in_offset=bass.IndirectOffsetOnAxis(ap=idx_g[:, 0:1], axis=0)).then_inc(s["x_in"], 16)

            def scatter(e):
                after(pool, s["y_out"], 16 * e)
                pool.tensor_copy(idx_s[:, :], icol[:, bass.ds(e, 1)])
                pool.tensor_copy(gate_s[:, :], gcol[:, bass.ds(e, 1)]).then_inc(s["sel_done"], 1)
                pool.wait_ge(s["sel_done"], e + 1)
                pool.wait_ge(s["y_done"], e + 1)
                carrier(2 * e + 2 if not (isinstance(e, int) and e == E - 1) else 2 * e + 1)
                pool.indirect_dma_start(out=acc_d, out_offset=bass.IndirectOffsetOnAxis(ap=idx_s[:, 0:1], axis=0),
                                        in_=ysc[:, :], in_offset=None, compute_op=ALU.add).then_inc(s["y_out"], 16)
            gather(0)
            gather(1)
            scatter(0)
            with pool.Fori(1, E - 1) as e:
                gather(e + 1)
                scatter(e)
            scatter(E - 1)
            for t in range(TL):
                pool.wait_ge(s["a_done"], t + 1)
                pool.tensor_tensor(fst[:, t, 1:2], fst[:, t, 0:1], eps_c[:, 1:2], ALU.add).then_inc(s["mean"], 1)
                pool.wait_ge(s["mean"], t + 1)
                pool.tensor_tensor(fst[:, t, 2:3], fst[:, t, 1:2], eps_c[:, 0:1], ALU.pow).then_inc(s["rstd"], 1)

        @block.scalar
        def _(act):
            act.wait_ge(s["cand_zero"], 1)
            act.activation(cand[0:E, :], aff[:, 0:NH2], ACT.Copy).then_inc(s["cand_done"], 1)
            act.activation(cand[H2:EH, :], aff[:, NH2:N], ACT.Copy).then_inc(s["cand_done"], 1)

            def x_part(e, half):
                act.wait_ge(s["x_mm"], 2 * e + half + 1)
                after(act, s["up_mm"], NJ * e)
                act.activation(x_hi[:, 4 * half:4 * half + 4, :].rearrange("p k n -> p (k n)"), psum[:, XB, :], ACT.Copy).then_inc(s["x_a"], 1)

            def split(e, j, which, c):
                k0 = 3 * j + which
                if c == 0:
                    act.wait_ge(unit_in[k0 % NU], arrived(e, k0))
                    after(act, s["up_mm" if which else "gate_mm"], NJ * e + j)
                act.activation(w_hi[which][c][:, :], unit[k0 % NU][:, c * CH:(c + 1) * CH], ACT.Copy).then_inc(s["hi_done"], 1)

            def gate(e, j):
                st = NJ * e + j
                act.wait_ge(s["gate_mm"], st + 1)
                if not (isinstance(e, int) and e == 0 and j < 2):
                    act.wait_ge(s["hid_done"], st - 1)
                act.activation(sil[j % 2][:, :], psum[:, 2 * (j % 2), :], ACT.Silu).then_inc(s["sil_done"], 1)

            def turn(e, j):
                st = NJ * e + j
                act.wait_ge(s["ht_mm"], st + 1)
                if not (isinstance(e, int) and e == 0 and j < 2):
                    act.wait_ge(s["down_mm"], st - 1)
                act.activation(h_hi[j % 2][:, :, :].rearrange("p k n -> p (k n)"), psum[:, HB, 0:2 * P], ACT.Copy)
                act.activation(hidt[j % 2][:, :, :].rearrange("p k n -> p (k n)"), psum[:, HB, 2 * P:4 * P], ACT.Copy).then_inc(s["ht_done"], 1)

            def split_down(e, j, en, kn):
                act.wait_ge(unit_in[kn % NU], arrived(en, kn))
                after(act, s["down_mm"], NJ * e + j)
                for c in range(2):
                    act.activation(d_hi[c][:, :], unit[kn % NU][:, c * D:(c + 1) * D], ACT.Copy).then_inc(s["d_hi_done"], 1)

            def expert(e, first, last):
                for j in range(NJ):
                    gate(e, j)
                    if j > 0:
                        turn(e, j - 1)
                        split_down(e, j - 1, e, 3 * j + 2)
                    elif not first:
                        turn(e - 1, NJ - 1)
                        split_down(e - 1, NJ - 1, e, 2)
                    if j < NJ - 1 or not last:
                        en, jn = (e, j + 1) if j < NJ - 1 else (e + 1, 0)
                        if j == NJ - 1:
                            x_part(en, 0)
                            x_part(en, 1)
                        for which, c in ((0, 0), (0, 1), (1, 0), (1, 1)):
                            split(en, jn, which, c)
            for which, c in ((0, 0), (0, 1), (1, 0), (1, 1)):
                split(0, 0, which, c)
            x_part(0, 0)
            x_part(0, 1)
            expert(0, True, False)
            with act.Fori(1, E - 1) as e:
                expert(e, False, False)
            expert(E - 1, False, True)
            turn(E - 1, NJ - 1)
            split_down(E - 1, NJ - 1, E, 0)

            def store(t):
                act.wait_ge(s["norm_done"], t + 1)
                act.dma_start(out_d[t], xa[t % NX][:, :]).then_inc(xa_out[t % NX], 16)
            for t in range(TL):
                act.wait_ge(xa_in[t % NX], 16 * (t // NX + 1))
                after(act, s["a_done"], t)
                act.activation(sqj[:, :], xa[t % NX][:, :], ACT.Square, accum_out=fst[:, t, 0:1]).then_inc(s["a_done"], 1)
                if t >= 1:
                    store(t - 1)
            store(TL - 1)
            for i in range(NX):
                act.wait_ge(xa_out[i], 16 * (TL // NX))

        @block.vector
        def _(dve):
            dve.wait_ge(s["fg_in"], 16)
            dve.tensor_scalar(fgain[:, :], fgain[:, :], ROOT, None, ALU.mult)
            dve.wait_ge(s["cand_done"], 2)
            for r in range(CAP // 8):
                v = slice(8 * r, 8 * r + 8)
                dve.max(top[:, v], cand[:, :]).then_inc(s["top_order"], 1)
                dve.wait_ge(s["top_order"], 2 * r + 1)
                dve.max_index(topi[:, v], top[:, v], cand[:, :])
                dve.match_replace(cand[:, :], top[:, v], cand[:, :], -1.0).then_inc(s["top_order"], 1)
                dve.wait_ge(s["top_order"], 2 * r + 2)
            dve.tensor_copy(rtop[:, CAP - 1::-1], top[:, :])
            dve.tensor_copy(rtopf[:, CAP - 1::-1], topi[:, :])
            dve.tensor_copy(topf[:, :], topi[:, :]).then_inc(s["top_done"], 1)
            dve.wait_ge(s["top_t"], 4)
            a_v, a_i, b_v, b_i = psum[:, 0, 0:E], psum[:, 1, 0:E], psum[:, 2, H2:EH], psum[:, 3, H2:EH]
            dve.tensor_copy(merge[:, 0, :], a_v)
            dve.tensor_scalar(merge[:, 2, :], b_i, float(NH2), None, ALU.add).then_inc(s["merged"], 1)
            dve.wait_ge(s["merged"], 1)
            dve.tensor_tensor(gcol[:, :], merge[:, 0, :], b_v, ALU.max).then_inc(s["cols_done"], 1)
            dve.tensor_tensor(merge[:, 1, :], merge[:, 0, :], b_v, ALU.is_ge)
            dve.tensor_tensor(merge[:, 3, :], a_i, merge[:, 2, :], ALU.subtract).then_inc(s["merged"], 1)
            dve.wait_ge(s["merged"], 2)
            dve.tensor_tensor(merge[:, 4, :], merge[:, 3, :], merge[:, 1, :], ALU.mult).then_inc(s["merged"], 1)
            dve.wait_ge(s["merged"], 3)
            dve.tensor_tensor(icol[:, :], merge[:, 4, :], merge[:, 2, :], ALU.add).then_inc(s["cols_done"], 1)

            def x_part(e, half):
                dve.wait_ge(s["x_a"], 2 * e + half + 1)
                k = slice(4 * half, 4 * half + 4)
                dve.tensor_tensor(x_lo[:, k, :].rearrange("p k n -> p (k n)"), psum[:, XB, :],
                                  x_hi[:, k, :].bitcast(F32).rearrange("p k n -> p (k n)"), ALU.subtract).then_inc(s["x_b"], 1)

            def split(e, j, which, c):
                dve.wait_ge(s["hi_done"], 4 * (NJ * e + j) + 2 * which + c + 1)
                dve.tensor_tensor(w_lo[which][c][:, :], unit[(3 * j + which) % NU][:, c * CH:(c + 1) * CH],
                                  w_hi[which][c][:, :].bitcast(F32), ALU.subtract).then_inc(s["lo_done"], 1)

            def split_down(e, j, en, kn):
                st = NJ * e + j
                dve.wait_ge(s["ht_done"], st + 1)
                dve.tensor_tensor(h_lo[j % 2][:, :, :].rearrange("p k n -> p (k n)"), psum[:, HB, 0:2 * P],
                                  h_hi[j % 2][:, :, :].bitcast(F32).rearrange("p k n -> p (k n)"), ALU.subtract).then_inc(s["h_lo_done"], 1)
                for c in range(2):
                    dve.wait_ge(s["d_hi_done"], 2 * st + c + 1)
                    dve.tensor_tensor(d_lo[c][:, :], unit[kn % NU][:, c * D:(c + 1) * D], d_hi[c][:, :].bitcast(F32),
                                      ALU.subtract).then_inc(s["d_lo_done"], 1)

            def hidden(e, j):
                st = NJ * e + j
                dve.wait_ge(s["sil_done"], st + 1)
                dve.wait_ge(s["up_mm"], st + 1)
                if not (isinstance(e, int) and e == 0 and j < 2):
                    dve.wait_ge(s["ht_mm"], st - 1)
                dve.tensor_tensor(hid[j % 2][:, :], sil[j % 2][:, :], psum[:, 2 * (j % 2) + 1, :], ALU.mult).then_inc(s["hid_done"], 1)

            def result(e):
                dve.wait_ge(s["down_mm"], NJ * (e + 1))
                dve.wait_ge(s["sel_done"], e + 1)
                after(dve, s["y_out"], 16 * e)
                dve.scalar_tensor_tensor(out=ysc[:, :], in0=psum[:, Y:Y + 2, :].rearrange("p a n -> p (a n)"), scalar=gate_s[:, 0:1],
                                         in1=rows[:, G2, :], op0=ALU.mult, op1=ALU.mult).then_inc(s["y_done"], 1)

            def expert(e, first, last):
                for j in range(NJ):
                    ahead = j < NJ - 1 or not last
                    en, jn = (e, j + 1) if j < NJ - 1 else (e + 1, 0)
                    if j > 0:
                        split_down(e, j - 1, e, 3 * j + 2)
                    elif not first:
                        split_down(e - 1, NJ - 1, e, 2)
                    if j < NJ - 1:
                        split(en, jn, 0, 0)
                        split(en, jn, 0, 1)
                    hidden(e, j)
                    if j == NJ - 1 and ahead:
                        x_part(en, 0)
                        x_part(en, 1)
                        split(en, jn, 0, 0)
                        split(en, jn, 0, 1)
                    if ahead:
                        split(en, jn, 1, 0)
                        split(en, jn, 1, 1)
                    if j == 0 and not first:
                        result(e - 1)
            for which in range(2):
                split(0, 0, which, 0)
                split(0, 0, which, 1)
                if which == 0:
                    x_part(0, 0)
                    x_part(0, 1)
            expert(0, True, False)
            with dve.Fori(1, E - 1) as e:
                expert(e, False, False)
            expert(E - 1, False, True)
            split_down(E - 1, NJ - 1, E, 0)
            result(E - 1)
            for t in range(TL):
                dve.wait_ge(s["rstd"], t + 1)
                dve.scalar_tensor_tensor(out=xa[t % NX][:, :], in0=xa[t % NX][:, :], scalar=fst[:, t, 2:3], in1=fgain[:, :],
                                         op0=ALU.mult, op1=ALU.mult).then_inc(s["norm_done"], 1)

        @block.tensor
        def _(pe):
            pe.wait_ge(s["top_done"], 1)
            for b, src in enumerate((top, topf, rtop, rtopf)):
                pe.transpose(psum[:, b, 0:EH], src[:, :], ident[0:EH, 0:EH]).then_inc(s["top_t"], 1)

            def x_turn(e, half):
                if half == 0:
                    pe.wait_ge(s["x_in"], 16 * (e + 1))
                    after(pe, s["x_b"], 2 * e)
                else:
                    pe.wait_ge(s["x_b"], 2 * e + 1)
                for k in range(4):
                    i = pe.transpose(psum[:, XB, k * P:(k + 1) * P], xe[:, (4 * half + k) * P:(4 * half + k + 1) * P], ident[:, :])
                i.then_inc(s["x_mm"], 1)

            def project(e, j, which):
                st = NJ * e + j
                if which == 0:
                    if j == 0:
                        pe.wait_ge(s["x_b"], 2 * e + 2)
                    if not (isinstance(e, int) and e == 0 and j < 2):
                        pe.wait_ge(s["sil_done"], st - 1)
                    elif j == 0:
                        pe.wait_ge(s["cols_done"], 2)
                elif not (isinstance(e, int) and e == 0 and j < 2):
                    pe.wait_ge(s["hid_done"], st - 1)
                for k in range(KD):
                    if k % 4 == 0:
                        pe.wait_ge(s["lo_done"], 4 * st + 2 * which + k // 4 + 1)
                    hi, lo = (w[which][k // 4][:, (k % 4) * UC:(k % 4 + 1) * UC] for w in (w_hi, w_lo))
                    for x_, w_ in ((x_hi, hi), (x_hi, lo), (x_lo, hi)):
                        i = pe.matmul(psum[:, 2 * (j % 2) + which, :], x_[:, k, :], w_, start=(k == 0 and w_ is hi and x_ is x_hi),
                                      stop=(k == KD - 1 and x_ is x_lo))
                i.then_inc(s["up_mm" if which else "gate_mm"], 1)

            def turn(e, j):
                st = NJ * e + j
                pe.wait_ge(s["hid_done"], st + 1)
                after(pe, s["ht_done"], st)
                after(pe, s["h_lo_done"], st)
                for k in range(4):
                    i = pe.transpose(psum[:, HB, k * P:(k + 1) * P], hid[j % 2][:, k * P:(k + 1) * P], ident[:, :])
                i.then_inc(s["ht_mm"], 1)

            def down(e, j, en, kn, parts):
                st = NJ * e + j
                if 0 in parts:
                    pe.wait_ge(s["h_lo_done"], st + 1)
                    pe.wait_ge(s["d_lo_done"], 2 * st + 2)
                    if j == 0:
                        after(pe, s["y_done"], e)
                u = unit[kn % NU][:, :].rearrange("p (k n) -> p k n", n=D)
                for h in parts:
                    c = slice(h * 512, (h + 1) * 512)
                    for k in range(2):
                        hi, lo = h_hi[j % 2][:, k, :], h_lo[j % 2][:, k, :]
                        pe.matmul(psum[:, Y + h, :], hi, d_hi[k][:, c], start=(j == 0 and k == 0), stop=False)
                        pe.matmul(psum[:, Y + h, :], hi, d_lo[k][:, c], start=False, stop=False)
                        pe.matmul(psum[:, Y + h, :], lo, d_hi[k][:, c], start=False, stop=False)
                    for k in (2, 3):
                        i = pe.matmul(psum[:, Y + h, :], hidt[j % 2][:, k - 2, :], u[:, k, c],
                                      start=False, stop=(j == NJ - 1 and k == 3))
                if 1 in parts:
                    i.then_inc(s["down_mm"], 1)

            def expert(e, first, last):
                for j in range(NJ):
                    project(e, j, 0)
                    if j > 0:
                        turn(e, j - 1)
                    elif not first:
                        turn(e - 1, NJ - 1)
                    project(e, j, 1)
                    if j == NJ - 1 and not last:
                        x_turn(e + 1, 0)
                        down(e, j - 1, e, 3 * j + 2, (0,))
                        x_turn(e + 1, 1)
                        down(e, j - 1, e, 3 * j + 2, (1,))
                    elif j > 0:
                        down(e, j - 1, e, 3 * j + 2, (0, 1))
                    elif not first:
                        down(e - 1, NJ - 1, e, 2, (0, 1))
            x_turn(0, 0)
            x_turn(0, 1)
            expert(0, True, False)
            with pe.Fori(1, E - 1) as e:
                expert(e, False, False)
            expert(E - 1, False, True)
            turn(E - 1, NJ - 1)
            down(E - 1, NJ - 1, E, 0, (0, 1))

    M.close()


def kernel(**inputs):
    import concourse.bacc as bacc
    from concourse.bass_utils import run_bass_kernel_spmd

    nc = bacc.Bacc("TRN2", target_bir_lowering=False, num_devices=1)
    arrays, args = {}, {}
    for name, v in {**{n: inputs[n] for n in INPUTS}, **constants()}.items():
        v = np.ascontiguousarray(v)
        arrays[f"in_{name}"] = v
        args[name] = nc.dram_tensor(f"in_{name}", v.shape, mybir.dt.from_np(v.dtype), kind="ExternalInput").ap()
    out = nc.dram_tensor("out", (1, N, D), F32, kind="ExternalOutput").ap()
    build(nc, args, out)
    return run_bass_kernel_spmd(nc, [arrays], core_ids=[0]).results[0]["out"]
```
